# Optimizing a Trainium2 kernel written in Bass

```python
import math
import jax
import jax.numpy as jnp
from jax import lax
import numpy as np

D_MODEL = 1024
BATCH = 1
SEQ = 512
DEPTH = 2

N_META = 16
GRID_W = 64
EPS = 1e-6
MLA_HEADS = D_MODEL // 128
MLA_NOPE = 64
MLA_ROPE = 32
MLA_V = 64
MLA_Q_RANK = D_MODEL // 4
MLA_KV_RANK = D_MODEL // 8
ROPE_THETA = 10000.0
Q_BLOCK = 128
NAT_HEADS = D_MODEL // 128
NAT_DIM = 64
WIN_ROWS = 8
WIN_COLS = 16
HY_WIDTH = D_MODEL // 2
HY_ORDER = 2
HY_SHORT = 3
HY_BANDS = 16
HY_EMB = 1 + 2 * HY_BANDS
HY_FFN = 64
HY_DIRS = 2
HY_TARGET = 1e-2
HY_MIN_RATE = math.log(1.0 / HY_TARGET) / 1.5
HY_MAX_RATE = math.log(1.0 / HY_TARGET) / 0.3
CF_WIDTH = D_MODEL // 2
CF_KERNEL = 31
MOE_GROUPS = 4
MOE_EXPERTS = 8
MOE_TOPK = 2
MOE_HIDDEN = D_MODEL // 4
A_IN_SIZES = (MLA_Q_RANK, MLA_KV_RANK, MLA_ROPE, NAT_HEADS * NAT_DIM, NAT_HEADS * NAT_DIM, NAT_HEADS * NAT_DIM)
A_OUT_WIDTH = MLA_HEADS * MLA_V + NAT_HEADS * NAT_DIM
C_IN_WIDTH = (HY_ORDER + 1) * HY_WIDTH + 2 * CF_WIDTH
C_OUT_WIDTH = HY_WIDTH + CF_WIDTH

kernel_name = 'hybrid_mla_natten_hyena_conformer_hmoe'

def split_cols(x, sizes):
    return jnp.split(x, [int(s) for s in np.cumsum(sizes)[:-1]], axis=-1)

def rmsnorm(x, g):
    x32 = x.astype(jnp.float32)
    y = x32 * lax.rsqrt(jnp.mean(x32 * x32, axis=-1, keepdims=True) + EPS)
    return (y * g.astype(jnp.float32)).astype(x.dtype)

def layernorm(x, g, b):
    x32 = x.astype(jnp.float32)
    mu = jnp.mean(x32, axis=-1, keepdims=True)
    xc = x32 - mu
    y = xc * lax.rsqrt(jnp.mean(xc * xc, axis=-1, keepdims=True) + EPS)
    return (y * g.astype(jnp.float32) + b.astype(jnp.float32)).astype(x.dtype)

def apply_rope(x, cos, sin):
    half = x.shape[-1] // 2
    x1, x2 = x[..., :half], x[..., half:]
    c = cos[None, :, None, :]
    s = sin[None, :, None, :]
    return jnp.concatenate([x1 * c - x2 * s, x1 * s + x2 * c], axis=-1).astype(x.dtype)

def depthwise_conv(x, w, b):
    k = w.shape[0]
    y = lax.conv_general_dilated(x, w[:, None, :].astype(x.dtype), window_strides=(1,), padding=[(k // 2, k // 2)],
                                 dimension_numbers=('NWC', 'WIO', 'NWC'), feature_group_count=x.shape[-1])
    return y + b.astype(x.dtype)

def dense_block_attention(q, k, v):
    B, T, H, dk = q.shape
    scale = dk ** -0.5

    def attend(qb):
        s = jnp.einsum('bqhd,bkhd->bhqk', qb, k, preferred_element_type=jnp.float32) * scale
        p = jax.nn.softmax(s, axis=-1).astype(v.dtype)
        return jnp.einsum('bhqk,bkhd->bqhd', p, v)

    out_meta = attend(q[:, :N_META])
    n_blk = (T - N_META) // Q_BLOCK
    qr = q[:, N_META:].reshape(B, n_blk, Q_BLOCK, H, dk).swapaxes(0, 1)
    out = lax.map(attend, qr)
    out = out.swapaxes(0, 1).reshape(B, n_blk * Q_BLOCK, H, v.shape[-1])
    return jnp.concatenate([out_meta, out], axis=1)

def neighbourhood_attention(q, k, v, rpb):
    B, T, H, d = q.shape
    scale = d ** -0.5
    n = T - N_META
    rows = n // GRID_W
    wr = min(WIN_ROWS, rows)
    qm, km, vm = q[:, :N_META], k[:, :N_META], v[:, :N_META]
    s_mm = jnp.einsum('bqhd,bkhd->bhqk', qm, km, preferred_element_type=jnp.float32) * scale
    out_meta = jnp.einsum('bhqk,bkhd->bqhd', jax.nn.softmax(s_mm, axis=-1).astype(v.dtype), vm)
    qg = q[:, N_META:].reshape(B, rows, GRID_W, H, d)
    kg = k[:, N_META:].reshape(B, rows, GRID_W, H, d)
    vg = v[:, N_META:].reshape(B, rows, GRID_W, H, d)
    col = np.arange(GRID_W)
    col_start = np.clip(col - WIN_COLS // 2, 0, GRID_W - WIN_COLS)
    col_idx = col_start[:, None] + np.arange(WIN_COLS)[None, :]
    col_bias_idx = (col_idx - col[:, None] + WIN_COLS - 1)[:, None, :]

    def row_block(r):
        r0 = jnp.clip(r - wr // 2, 0, rows - wr)
        kw = lax.dynamic_slice_in_dim(kg, r0, wr, axis=1)[:, :, col_idx]
        vw = lax.dynamic_slice_in_dim(vg, r0, wr, axis=1)[:, :, col_idx]
        qr = lax.dynamic_index_in_dim(qg, r, axis=1, keepdims=False)
        row_bias_idx = (r0 + jnp.arange(wr) - r + WIN_ROWS - 1)[None, :, None]
        bias = rpb[:, row_bias_idx, col_bias_idx]
        s_loc = jnp.einsum('bqhd,bwqchd->bhqwc', qr, kw, preferred_element_type=jnp.float32) * scale + bias[None]
        s_met = jnp.einsum('bqhd,bmhd->bhqm', qr, km, preferred_element_type=jnp.float32) * scale
        s = jnp.concatenate([s_met, s_loc.reshape(B, H, GRID_W, wr * WIN_COLS)], axis=-1)
        p = jax.nn.softmax(s, axis=-1).astype(v.dtype)
        p_loc = p[..., N_META:].reshape(B, H, GRID_W, wr, WIN_COLS)
        return (jnp.einsum('bhqm,bmhd->bqhd', p[..., :N_META], vm)
                + jnp.einsum('bhqwc,bwqchd->bqhd', p_loc, vw))

    out = lax.map(row_block, jnp.arange(rows))
    out = jnp.moveaxis(out, 0, 1).reshape(B, n, H, d)
    return jnp.concatenate([out_meta, out], axis=1)

def latent_neighbourhood_mixer(y, w_in, q_norm, w_uq, kv_norm, w_ukv, rpb, w_out, cos, sin):
    B, T, _ = y.shape
    c_q, c_kv, k_pe, nq, nk, nv = split_cols(y @ w_in, A_IN_SIZES)
    q = (rmsnorm(c_q, q_norm) @ w_uq).reshape(B, T, MLA_HEADS, MLA_NOPE + MLA_ROPE)
    kv = (rmsnorm(c_kv, kv_norm) @ w_ukv).reshape(B, T, MLA_HEADS, MLA_NOPE + MLA_V)
    q = jnp.concatenate([q[..., :MLA_NOPE], apply_rope(q[..., MLA_NOPE:], cos, sin)], axis=-1)
    k_pe = jnp.broadcast_to(apply_rope(k_pe[:, :, None, :], cos, sin), (B, T, MLA_HEADS, MLA_ROPE))
    k = jnp.concatenate([kv[..., :MLA_NOPE], k_pe], axis=-1)
    mla = dense_block_attention(q, k, kv[..., MLA_NOPE:])
    shp = (B, T, NAT_HEADS, NAT_DIM)
    nat = neighbourhood_attention(nq.reshape(shp), nk.reshape(shp), nv.reshape(shp), rpb)
    merged = jnp.concatenate([mla.reshape(B, T, -1), nat.reshape(B, T, -1)], axis=-1)
    return merged @ w_out

def hyena_filters(L, w1, b1, w2, b2, w3, sin_freq, log_decay):
    f32 = jnp.float32
    t = jnp.linspace(0.0, 1.0, L, dtype=f32)
    bands = jnp.linspace(1e-4, HY_BANDS - 1, HY_BANDS, dtype=f32)
    ang = 2.0 * math.pi * t[:, None] * bands[None, :]
    feats = jnp.concatenate([t[:, None], jnp.cos(ang), jnp.sin(ang)], axis=-1)
    hid = jnp.sin(sin_freq * (feats @ w1 + b1))
    hid = jnp.sin(sin_freq * (hid @ w2 + b2))
    filt = (hid @ w3).astype(f32).reshape(L, HY_DIRS, HY_ORDER, HY_WIDTH)
    filt = filt * jnp.exp(-t[:, None, None, None] * jnp.exp(log_decay.astype(f32))[None])
    fwd = filt[:, 0]
    bwd = filt[1:, 1][::-1]
    zero = jnp.zeros((1, HY_ORDER, HY_WIDTH), f32)
    return jnp.concatenate([fwd, zero, bwd], axis=0)

def fft_long_conv(z, k_freq, bias):
    L = z.shape[1]
    z32 = z.astype(jnp.float32)
    zf = jnp.fft.rfft(z32, n=2 * L, axis=1)
    y = jnp.fft.irfft(zf * k_freq[None], n=2 * L, axis=1)[:, :L]
    return (y + z32 * bias.astype(jnp.float32)).astype(z.dtype)

def hyena_conformer_mixer(y, w_in, short_w, short_b, f_w1, f_b1, f_w2, f_b2, f_w3, sin_freq, log_decay,
                          hy_bias, dw_w, dw_b, ln_g, ln_b, w_out):
    B, T, _ = y.shape
    p = y @ w_in
    hy_in, cf_in = p[..., :(HY_ORDER + 1) * HY_WIDTH], p[..., (HY_ORDER + 1) * HY_WIDTH:]
    v, *gates = jnp.split(depthwise_conv(hy_in, short_w, short_b), HY_ORDER + 1, axis=-1)
    k_freq = jnp.fft.rfft(hyena_filters(T, f_w1, f_b1, f_w2, f_b2, f_w3, sin_freq, log_decay), axis=0)
    z = v
    for o in range(HY_ORDER):
        z = gates[o] * fft_long_conv(z, k_freq[:, o], hy_bias[o])
    a, g = jnp.split(cf_in, 2, axis=-1)
    c = depthwise_conv(a * jax.nn.sigmoid(g), dw_w, dw_b)
    c = jax.nn.silu(layernorm(c, ln_g, ln_b))
    return jnp.concatenate([z, c], axis=-1) @ w_out

def hierarchical_moe(y, w_group, b_group, w_router, b_router, w1, w3, w2):
    B, T, D = y.shape
    f32 = jnp.float32
    xt = y.reshape(B * T, D)
    g_prob = jax.nn.softmax(jnp.einsum('nd,dg->ng', xt, w_group, preferred_element_type=f32) + b_group, axis=-1)
    p_group, g_idx = lax.top_k(g_prob, 1)
    g_onehot = jax.nn.one_hot(g_idx[:, 0], MOE_GROUPS, dtype=f32)
    e_logits_all = jnp.einsum('nd,gde->nge', xt, w_router, preferred_element_type=f32) + b_router
    e_logits = jnp.einsum('ng,nge->ne', g_onehot, e_logits_all)
    e_val, e_idx = lax.top_k(e_logits, MOE_TOPK)
    e_w = jax.nn.softmax(e_val, axis=-1) * p_group
    e_gate = jnp.einsum('nk,nke->ne', e_w, jax.nn.one_hot(e_idx, MOE_EXPERTS, dtype=f32))
    gate = (g_onehot[:, :, None] * e_gate[:, None, :]).astype(y.dtype)
    out = jnp.zeros((B * T, D), f32)
    for g in range(MOE_GROUPS):
        a = jnp.einsum('nd,edf->nef', xt, w1[g])
        b = jnp.einsum('nd,edf->nef', xt, w3[g])
        hid = jax.nn.silu(a) * b * gate[:, g, :, None]
        out = out + jnp.einsum('nef,efd->nd', hid, w2[g], preferred_element_type=f32)
    return out.astype(y.dtype).reshape(B, T, D)

def setup_inputs(seed: int = 0) -> dict:
    key = jax.random.key(seed)
    keys = iter(jax.random.split(key, 48))
    n_even = (DEPTH + 1) // 2
    n_odd = DEPTH // 2
    f32 = jnp.float32

    def normal(shape, scale):
        return jax.random.normal(next(keys), shape, f32) * scale

    def gain(shape):
        return 1.0 + normal(shape, 0.02)

    rates = jnp.log(jnp.linspace(HY_MIN_RATE, HY_MAX_RATE, HY_WIDTH, dtype=f32))
    hy_dec_shape = (n_odd, HY_DIRS, HY_ORDER, HY_WIDTH)
    return {
        'x': normal((BATCH, SEQ, D_MODEL), 1.0),
        'meta_tokens': normal((N_META, D_MODEL), 1.0),
        'norm_mix': gain((DEPTH, D_MODEL)),
        'norm_ffn': gain((DEPTH, D_MODEL)),
        'norm_final': gain((D_MODEL,)),
        'a_w_in': normal((n_even, D_MODEL, sum(A_IN_SIZES)), D_MODEL ** -0.5),
        'mla_q_norm': gain((n_even, MLA_Q_RANK)),
        'mla_w_uq': normal((n_even, MLA_Q_RANK, MLA_HEADS * (MLA_NOPE + MLA_ROPE)), MLA_Q_RANK ** -0.5),
        'mla_kv_norm': gain((n_even, MLA_KV_RANK)),
        'mla_w_ukv': normal((n_even, MLA_KV_RANK, MLA_HEADS * (MLA_NOPE + MLA_V)), MLA_KV_RANK ** -0.5),
        'nat_rpb': normal((n_even, NAT_HEADS, 2 * WIN_ROWS - 1, 2 * WIN_COLS - 1), 0.02),
        'a_w_out': normal((n_even, A_OUT_WIDTH, D_MODEL), A_OUT_WIDTH ** -0.5),
        'c_w_in': normal((n_odd, D_MODEL, C_IN_WIDTH), D_MODEL ** -0.5),
        'hy_short_w': normal((n_odd, HY_SHORT, (HY_ORDER + 1) * HY_WIDTH), HY_SHORT ** -0.5),
        'hy_short_b': normal((n_odd, (HY_ORDER + 1) * HY_WIDTH), 0.02),
        'hy_ffn_w1': normal((n_odd, HY_EMB, HY_FFN), HY_EMB ** -0.5),
        'hy_ffn_b1': normal((n_odd, HY_FFN), 0.02),
        'hy_ffn_w2': normal((n_odd, HY_FFN, HY_FFN), HY_FFN ** -0.5),
        'hy_ffn_b2': normal((n_odd, HY_FFN), 0.02),
        'hy_ffn_w3': normal((n_odd, HY_FFN, HY_DIRS * HY_ORDER * HY_WIDTH), 0.02 * HY_FFN ** -0.5),
        'hy_sin_freq': gain((n_odd, HY_FFN)),
        'hy_log_decay': jnp.broadcast_to(rates, hy_dec_shape) + normal(hy_dec_shape, 0.05),
        'hy_bias': normal((n_odd, HY_ORDER, HY_WIDTH), 0.5),
        'cf_dw_w': normal((n_odd, CF_KERNEL, CF_WIDTH), CF_KERNEL ** -0.5),
        'cf_dw_b': normal((n_odd, CF_WIDTH), 0.02),
        'cf_ln_g': gain((n_odd, CF_WIDTH)),
        'cf_ln_b': normal((n_odd, CF_WIDTH), 0.02),
        'c_w_out': normal((n_odd, C_OUT_WIDTH, D_MODEL), C_OUT_WIDTH ** -0.5),
        'moe_w_group': normal((DEPTH, D_MODEL, MOE_GROUPS), D_MODEL ** -0.5),
        'moe_b_group': normal((DEPTH, MOE_GROUPS), 0.01),
        'moe_w_router': normal((DEPTH, MOE_GROUPS, D_MODEL, MOE_EXPERTS), D_MODEL ** -0.5),
        'moe_b_router': normal((DEPTH, MOE_GROUPS, MOE_EXPERTS), 0.01),
        'moe_w1': normal((DEPTH, MOE_GROUPS, MOE_EXPERTS, D_MODEL, MOE_HIDDEN), D_MODEL ** -0.5),
        'moe_w3': normal((DEPTH, MOE_GROUPS, MOE_EXPERTS, D_MODEL, MOE_HIDDEN), D_MODEL ** -0.5),
        'moe_w2': normal((DEPTH, MOE_GROUPS, MOE_EXPERTS, MOE_HIDDEN, D_MODEL), MOE_HIDDEN ** -0.5),
    }

def reference(x, meta_tokens, norm_mix, norm_ffn, norm_final, a_w_in, mla_q_norm, mla_w_uq, mla_kv_norm,
              mla_w_ukv, nat_rpb, a_w_out, c_w_in, hy_short_w, hy_short_b, hy_ffn_w1, hy_ffn_b1, hy_ffn_w2,
              hy_ffn_b2, hy_ffn_w3, hy_sin_freq, hy_log_decay, hy_bias, cf_dw_w, cf_dw_b, cf_ln_g, cf_ln_b,
              c_w_out, moe_w_group, moe_b_group, moe_w_router, moe_b_router, moe_w1, moe_w3, moe_w2):
    B = x.shape[0]
    meta = jnp.broadcast_to(meta_tokens[None].astype(x.dtype), (B, N_META, D_MODEL))
    h = jnp.concatenate([meta, x], axis=1)
    T = h.shape[1]
    pos = jnp.arange(T, dtype=jnp.float32)
    inv_freq = ROPE_THETA ** (-jnp.arange(0, MLA_ROPE, 2, dtype=jnp.float32) / MLA_ROPE)
    ang = pos[:, None] * inv_freq[None, :]
    cos, sin = jnp.cos(ang), jnp.sin(ang)
    for layer in range(DEPTH):
        i = layer // 2
        y = rmsnorm(h, norm_mix[layer])
        if layer % 2 == 0:
            y = latent_neighbourhood_mixer(y, a_w_in[i], mla_q_norm[i], mla_w_uq[i], mla_kv_norm[i],
                                           mla_w_ukv[i], nat_rpb[i], a_w_out[i], cos, sin)
        else:
            y = hyena_conformer_mixer(y, c_w_in[i], hy_short_w[i], hy_short_b[i], hy_ffn_w1[i], hy_ffn_b1[i],
                                      hy_ffn_w2[i], hy_ffn_b2[i], hy_ffn_w3[i], hy_sin_freq[i],
                                      hy_log_decay[i], hy_bias[i], cf_dw_w[i], cf_dw_b[i], cf_ln_g[i],
                                      cf_ln_b[i], c_w_out[i])
        h = h + y
        h = h + hierarchical_moe(rmsnorm(h, norm_ffn[layer]), moe_w_group[layer], moe_b_group[layer],
                                 moe_w_router[layer], moe_b_router[layer], moe_w1[layer], moe_w3[layer],
                                 moe_w2[layer])
    h = rmsnorm(h, norm_final)
    return h[:, N_META:]


_drawn_inputs = setup_inputs


def setup_inputs(seed=0):
    import zlib

    import numpy as np

    out = dict(_drawn_inputs(seed))
    spreads = {}
    factors = {'norm_final': 24.22,
     'mla_q_norm': 3.681,
     'nat_rpb': 3.045,
     'hy_short_b': 15.042,
     'hy_ffn_b1': 50.571,
     'hy_ffn_b2': 33.624,
     'hy_sin_freq': 59.603,
     'cf_ln_g': 3.274,
     'cf_ln_b': 9.175,
     'hy_log_decay': 24.201,
     'moe_b_group': 3.856,
     'hy_ffn_w1': 7.86,
     'hy_ffn_w2': 6.296,
     'hy_ffn_w3': 6.25,
     'moe_b_router': 3.091}
    for name, (base, spread) in spreads.items():
        noise = np.random.default_rng([zlib.crc32(name.encode()), seed]).standard_normal(out[name].shape)
        drawn = base * np.exp(spread * noise) if base else spread * noise
        out[name] = jnp.asarray(drawn.astype(out[name].dtype))
    for name, factor in factors.items():
        out[name] = (out[name] * factor).astype(out[name].dtype)
    return out
```

```python
import math
from contextlib import ExitStack

import numpy as np

import concourse.bass as bass
from concourse import mybir

F32 = mybir.dt.float32
I32 = mybir.dt.int32
ALU = mybir.AluOpType
ACT = mybir.ActivationFunctionType
AX = mybir.AxisListType

P = 128
D = 1024
KC = D // P
META = 16
SEQ = 512
T = META + SEQ
HT = T // 2
NT = 5
EPS = 1e-6
HEADS = 8
NOPE, ROPE, VD = 64, 32, 64
QK = NOPE + ROPE
QR, KVR = 256, 128
WIN_ROWS, WIN_COLS, GRID_W = 8, 16, 64
GROUPS, EXPERTS, HID = 4, 8, 256
NE = GROUPS * EXPERTS
CAP = 96
NX = (2 * T - 1) // CAP
SLOTS = (NE + NX) * CAP
HYW = 512
HYC = HYW // P
CFK = 31
PAD31 = CFK // 2
HY_EMB, HY_FFN = 33, 64
NFFT = 2 * T
NF = T + 1
FC = 5
NEG = -1e30
MAGIC = 1.5 * 2.0 ** 23
TURN = (6.28125, 0.0019350051879882812, 2 * math.pi - 6.28125 - 0.0019350051879882812)
PI_IN = 3.1415925


def rows_of(t):
    return P if t < 4 else META


def time_cols(t):
    return slice(META + P * t, META + P * t + P) if t < 4 else slice(0, META)


def tile_cols(t):
    return slice(P * t, P * t + rows_of(t))


class Chain:

    def __init__(self, sem):
        self.sem, self.n = sem, 0

    def link(self, eng, ins):
        self.n += 1
        ins.then_inc(self.sem, 1)
        eng.wait_ge(self.sem, self.n)


def build(nc, A):
    top = ExitStack()

    def sem(name):
        return top.enter_context(nc.semaphore(name))

    reused = {}

    def sem_again(name):
        if name not in reused:
            reused[name] = sem(name)
        return reused[name]

    def clear(*sems):
        for s in sems:
            nc.gpsimd.sem_clear(s)

    def scope_alloc(scope):
        def alloc(name, shape, dt=F32):
            return scope.enter_context(nc.sbuf_tensor(name, shape, dt))
        return alloc

    with top:
        sb = scope_alloc(top)
        ps = top.enter_context(nc.psum_tensor("ps", [P, 8, 512], F32))
        flat = ps[:, :, :].rearrange("p a b -> p (a b)")

        def pair(s, rows=slice(0, P)):
            return ps[rows, 2 * s:2 * s + 2, 0:HT]

        def halves(ap):
            return ap.rearrange("p (a b) -> p a b", a=2)

        h = sb("h", [P, NT, D])
        ident = sb("ident", [P, P])
        ones = sb("ones", [P, P])
        dve_chain, act_chain = Chain(sem("dve_chain")), Chain(sem("act_chain"))

        xs = nc.dram_tensor("xs_rows", [SLOTS, D], F32).ap()
        ys = nc.dram_tensor("ys_rows", [SLOTS, D], F32).ap()

        s_in, s_one, s_zero, s_clear = sem("inputs_loaded"), sem("ones_set"), sem("zeros_set"), sem("slots_cleared")
        with ExitStack() as scope:
            zeros = scope_alloc(scope)("zeros", [CAP, D])
            with nc.Block() as block:
                @block.sync
                def _(sp):
                    sp.dma_start(h[:, 0:4, :], A["x"].rearrange("b (t p) d -> p (b t) d", p=P)).then_inc(s_in, 16)
                    sp.dma_start(h[0:META, 4, :], A["meta_tokens"]).then_inc(s_in, 16)
                    sp.dma_start(ident[:, :], A["ident"]).then_inc(s_in, 16)
                    sp.wait_ge(s_in, 48)

                @block.vector
                def _(dve):
                    dve.memset(zeros[:, :], 0.0).then_inc(s_zero, 1)
                    dve.memset(ones[:, :], 1.0).then_inc(s_one, 1)
                    dve.wait_ge(s_one, 1)

                @block.scalar
                def _(act):
                    act.wait_ge(s_zero, 1)
                    for n in range(SLOTS // CAP):
                        act.dma_start(xs[n * CAP:(n + 1) * CAP, :], zeros[:, :]).then_inc(s_clear, 16)
                    for n in range(NE, NE + NX):
                        act.dma_start(ys[n * CAP:(n + 1) * CAP, :], zeros[:, :]).then_inc(s_clear, 16)
                    act.wait_ge(s_clear, 16 * (NE + 2 * NX))

        def norm_phase(tag, gain, xn, yT):
            s_gain, s_set, s_sq, s_ms, s_rt, s_xn = (sem_again(f"norm_{n}") for n in (
                "gain_loaded", "ssq_set", "squares_summed", "mean_ready", "root_ready", "xn_ready"))
            s_tp, s_ea, s_ed = sem_again("norm_turned"), sem_again("norm_act_copied"), sem_again("norm_dve_copied")
            with ExitStack() as scope:
                al = scope_alloc(scope)
                gbc = al(f"{tag}_gbc", [P, D])
                ssq, ms, rt, rs = (al(f"{tag}_{n}", [P, NT]) for n in ("ssq", "ms", "rt", "rs"))
                with nc.Block() as block:
                    @block.sync
                    def _(sp):
                        sp.dma_start(gbc[:, :], gain).then_inc(s_gain, 16)

                    @block.scalar
                    def _(act):
                        act.wait_ge(s_set, 1)
                        for t in range(NT):
                            r = rows_of(t)
                            act.activation(xn[0:r, t, :], h[0:r, t, :], ACT.Square,
                                           accum_out=ssq[0:r, t:t + 1]).then_inc(s_sq, 1)
                        act.wait_ge(s_ms, 1)
                        act.activation(rt[:, :], ms[:, :], ACT.Sqrt).then_inc(s_rt, 1)
                        if yT is not None:
                            for t in range(NT):
                                act.wait_ge(s_tp, 2 * t + 1)
                                act.copy(yT[:, 0:4, time_cols(t)],
                                         ps[:, (2 * t) % 8, :].rearrange("p (c n) -> p c n", c=4)[:, :, 0:rows_of(t)]
                                         ).then_inc(s_ea, 1)

                    @block.vector
                    def _(dve):
                        dve.memset(ssq[:, :], 1.0).then_inc(s_set, 1)
                        dve.wait_ge(s_sq, NT)
                        dve.tensor_scalar(ms[:, :], ssq[:, :], 1.0 / D, EPS, ALU.mult, ALU.add).then_inc(s_ms, 1)
                        dve.wait_ge(s_rt, 1)
                        dve_chain.link(dve, dve.reciprocal(rs[:, :], rt[:, :]))
                        dve.wait_ge(s_gain, 16)
                        for t in range(NT):
                            r = rows_of(t)
                            dve.scalar_tensor_tensor(out=xn[0:r, t, :], in0=h[0:r, t, :], scalar=rs[0:r, t:t + 1],
                                                     in1=gbc[0:r, :], op0=ALU.mult, op1=ALU.mult).then_inc(s_xn, 1)
                        if yT is not None:
                            for t in range(NT):
                                dve.wait_ge(s_tp, 2 * t + 2)
                                dve.tensor_copy(yT[:, 4:8, time_cols(t)],
                                                ps[:, (2 * t + 1) % 8, :].rearrange("p (c n) -> p c n", c=4)[:, :, 0:rows_of(t)]
                                                ).then_inc(s_ed, 1)
                        else:
                            dve.wait_ge(s_xn, NT)

                    @block.tensor
                    def _(pe):
                        if yT is None:
                            return
                        for t in range(NT):
                            r = rows_of(t)
                            pe.wait_ge(s_xn, t + 1)
                            xc = xn[0:r, t, :].rearrange("p (q c) -> p c q", c=KC)
                            for half in range(2):
                                if t == 4:
                                    pe.wait_ge(s_ed if half else s_ea, 1)
                                bank = (2 * t + half) % 8
                                for c in range(4):
                                    last = pe.transpose(ps[:, bank, c * P:c * P + r], xc[:, 4 * half + c, :], ident[0:r, 0:r])
                                last.then_inc(s_tp, 1)
            clear(s_gain, s_set, s_sq, s_ms, s_rt, s_xn, s_tp, s_ea, s_ed)

        def load_out_weights(sp, wo, w, s_wo):
            for k in range(KC):
                sp.dma_start(wo[:, k, :], w[k * P:(k + 1) * P, :]).then_inc(s_wo, 16)

        def out_phase(tag, chunk, wo, s_wo, cols):
            s_job, s_add = sem(f"{tag}_product"), sem(f"{tag}_added")
            with nc.Block() as block:
                @block.tensor
                def _(pe):
                    pe.wait_ge(s_wo, 16 * KC)
                    for j in range(2 * NT):
                        t, n = divmod(j, 2)
                        if j >= 8:
                            pe.wait_ge(s_add, j - 7)
                        for k in range(KC):
                            last = pe.matmul(ps[0:rows_of(t), j % 8, :], chunk(k)[:, cols(t)], wo[:, k, n * 512:(n + 1) * 512],
                                             start=k == 0, stop=k == KC - 1)
                        last.then_inc(s_job, 1)

                @block.vector
                def _(dve):
                    for j in range(2 * NT):
                        t, n = divmod(j, 2)
                        r = rows_of(t)
                        hh = h[0:r, t, n * 512:(n + 1) * 512]
                        dve.wait_ge(s_job, j + 1)
                        dve.tensor_tensor(hh, hh, ps[0:r, j % 8, :], ALU.add).then_inc(s_add, 1)
                    dve.wait_ge(s_add, 2 * NT)

        def moe_phase(L):
            W = [A[n][L].rearrange("g e a b -> (g e) a b") for n in ("moe_w1", "moe_w3", "moe_w2")]
            W1, W3 = (w.rearrange("e (p c) f -> e p c f", c=KC) for w in W[0:2])
            W2 = W[2].rearrange("e (p c) n -> e p c n", c=2)
            tag = f"m{L}_"

            def sems(*names):
                return [sem_again("moe_" + n) for n in names]

            with ExitStack() as moe:
                al = scope_alloc(moe)
                xn = al(tag + "xn", [P, NT, D])
                gate = al(tag + "gate", [P, 2, NT])
                posi = al(tag + "posi", [P, 2, NT], I32)
                xe = al(tag + "extra", [1, NX + 1], I32)
                with ExitStack() as scope:
                    al = scope_alloc(scope)
                    yT = al(tag + "yT", [P, KC, T])
                    norm_phase(f"nrm{2 * L + 1}", A[f"norm_ffn{L}"], xn, yT)
                    route_phase(L, tag, sems, al, yT, gate, posi, xe)
                scatter_phase(tag, xn, posi)
                expert_phase(tag, sems, W1, W3, W2, xe)
                combine_phase(tag, sems, gate, posi)

        def route_phase(L, tag, sems, al, yT, gate, posi, xe):
            NL = GROUPS + NE
            wr, br = al(tag + "wr", [P, KC, NL]), al(tag + "br", [P, NL])
            lat, late, val = al(tag + "later", [P, P]), al(tag + "later_e", [NE, NE]), al(tag + "valid", [P, NT])
            f4, f8, erow, ecol, xrow = al(tag + "f4", [P, 4]), al(tag + "f8", [P, 8]), al(tag + "erow", [P, NE]), \
                al(tag + "ecol", [NE, 1]), al(tag + "xrow", [NE, NX])
            Lg = al(tag + "logits", [P, NT, NL])
            m4, oh4, g4 = al(tag + "m4", [P, NT, 4]), al(tag + "oh4", [P, NT, 4]), al(tag + "g4", [P, NT, 4])
            el, e2, eq = al(tag + "el", [P, NT, 8]), al(tag + "e2", [P, NT, 8]), al(tag + "eq", [P, NT, 8])
            oh = al(tag + "oh", [P, 2, NT, 8])
            OH = al(tag + "OH", [P, 2, NT, NE])
            M = al(tag + "M", [P, NT, NE])
            pr = al(tag + "pr", [P, NT, NE])
            st = al(tag + "st", [P, 16, NT])
            nt, nt1, ntb = al(tag + "nt", [NE, 1]), al(tag + "nt1", [NE, 1]), al(tag + "ntb", [NE, P])
            bcol, bend, ind, ind2 = al(tag + "bcol", [NE, 1]), al(tag + "bend", [NE, 1]), al(tag + "ind", [NE, NX]), al(tag + "ind2", [NE, NX])
            s_ld, s_lg, s_ga, s_ex, s_M, s_cum, s_nt, s_base, s_ind, s_xe = sems(
                "loaded", "logits", "differences", "exps", "choices", "ranks", "tiles", "bases", "extras", "extra_experts")
            col = lambda k: st[:, k, :]
            GM, MM, M0, M1, PG, EE, DN, RK0, RK1, EX0, EX1, B0, B1, LT, TMP, TM2 = range(16)
            wide = lambda k, n: st[:, k, :].unsqueeze(2).to_broadcast([P, NT, n])
            row = lambda ap, n: ap.unsqueeze(1).to_broadcast([P, NT, n])

            with nc.Block() as block:
                loads = ((wr[:, :, :], f"router_w{L}"), (br[:, :], f"router_b{L}"), (lat[:, :], "later"), (late[:, :], "later_e"),
                         (val[:, :], "valid"), (f4[:, :], "first4"), (f8[:, :], "first8"), (erow[:, :], "expert_row"),
                         (ecol[:, :], "expert_col"), (xrow[:, :], "extra_row"))

                @block.sync
                def _(sp):
                    for dst, name in loads:
                        sp.dma_start(dst, A[name]).then_inc(s_ld, 16)

                @block.tensor
                def _(pe):
                    pe.wait_ge(s_ld, 16 * len(loads))
                    for t in range(NT):
                        for c in range(KC):
                            last = pe.matmul(ps[0:rows_of(t), t, 0:NL], yT[:, c, time_cols(t)], wr[:, c, :],
                                             start=c == 0, stop=c == KC - 1)
                    last.then_inc(s_lg, 1)
                    pe.wait_ge(s_M, 1)
                    for t in range(NT):
                        for k in range(t):
                            pe.matmul(ps[:, 5, t * NE:(t + 1) * NE], ones[:, :], M[:, k, :], start=k == 0, stop=False)
                        pe.matmul(ps[:, 5, t * NE:(t + 1) * NE], lat[:, :], M[:, t, :], start=t == 0, stop=True)
                    for k in range(NT):
                        last = pe.matmul(ps[0:NE, 6, 0:1], M[:, k, :], ones[:, 0:1], start=k == 0, stop=k == NT - 1)
                    last.then_inc(s_cum, 1)
                    pe.wait_ge(s_nt, 1)
                    pe.matmul(ps[:, 7, 0:NE], ntb[:, :], late[:, :], start=True, stop=True)
                    pe.matmul(ps[0:NE, 7, 64:65], late[:, :], nt[:, :], start=True, stop=True).then_inc(s_base, 1)
                    pe.wait_ge(s_ind, 1)
                    pe.matmul(ps[0:1, 6, 0:1], ones[0:NE, 0:1], nt[:, :], start=True, stop=True)
                    pe.matmul(ps[0:1, 6, 1:NX + 1], ecol[:, :], ind2[:, :], start=True, stop=True).then_inc(s_xe, 1)

                @block.scalar
                def _(act):
                    act.wait_ge(s_ga, 1)
                    act.activation(g4[:, :, :], m4[:, :, :], ACT.Exp).then_inc(s_ex, 1)
                    act.wait_ge(s_ga, 2)
                    act.activation(col(EE), col(TMP), ACT.Exp).then_inc(s_ex, 1)

                @block.vector
                def _(dve):
                    def do(ins):
                        dve_chain.link(dve, ins)

                    def tt(out, a, b, op):
                        do(dve.tensor_tensor(out, a, b, op))

                    def ts(out, a, s1, s2, o1, o2=ALU.bypass):
                        do(dve.tensor_scalar(out, a, s1, s2, o1, o2) if s2 is not None else dve.tensor_scalar(out, a, s1, None, o1))

                    def reduce(out, a, op):
                        do(dve.tensor_reduce(out, a, AX.X, op))

                    do(dve.memset(Lg[:, :, :], 0.0))
                    dve.wait_ge(s_ld, 16 * len(loads))
                    dve.wait_ge(s_lg, 1)
                    for t in range(NT):
                        r = rows_of(t)
                        tt(Lg[0:r, t, :], ps[0:r, t, 0:NL], br[0:r, :], ALU.add)
                    G = Lg[:, :, 0:4]
                    reduce(col(GM), G, ALU.max)
                    dve.tensor_tensor(m4[:, :, :], G, wide(GM, 4), ALU.subtract).then_inc(s_ga, 1)
                    tt(oh4[:, :, :], G, wide(GM, 4), ALU.is_equal)
                    tt(oh4[:, :, :], oh4[:, :, :], row(f4[:, :], 4), ALU.mult)
                    reduce(col(MM), oh4[:, :, :], ALU.max)
                    tt(oh4[:, :, :], oh4[:, :, :], wide(MM, 4), ALU.is_equal)
                    for g in range(GROUPS):
                        E = Lg[:, :, GROUPS + EXPERTS * g:GROUPS + EXPERTS * (g + 1)]
                        sel = oh4[:, :, g:g + 1].to_broadcast([P, NT, 8])
                        if g == 0:
                            tt(el[:, :, :], E, sel, ALU.mult)
                        else:
                            tt(e2[:, :, :], E, sel, ALU.mult)
                            tt(el[:, :, :], el[:, :, :], e2[:, :, :], ALU.add)
                    src = el
                    for k, mk_ in ((0, M0), (1, M1)):
                        reduce(col(mk_), src[:, :, :], ALU.max)
                        tt(eq[:, :, :], src[:, :, :], wide(mk_, 8), ALU.is_equal)
                        tt(eq[:, :, :], eq[:, :, :], row(f8[:, :], 8), ALU.mult)
                        reduce(col(MM), eq[:, :, :], ALU.max)
                        tt(oh[:, k, :, :], eq[:, :, :], wide(MM, 8), ALU.is_equal)
                        if k == 0:
                            do(dve.scalar_tensor_tensor(out=e2[:, :, :], in0=oh[:, 0, :, :], scalar=NEG, in1=el[:, :, :],
                                                        op0=ALU.mult, op1=ALU.add))
                            src = e2
                    dve.tensor_tensor(col(TMP), col(M1), col(M0), ALU.subtract).then_inc(s_ga, 1)
                    for k in range(2):
                        for g in range(GROUPS):
                            tt(OH[:, k, :, EXPERTS * g:EXPERTS * (g + 1)], oh[:, k, :, :],
                               oh4[:, :, g:g + 1].to_broadcast([P, NT, 8]), ALU.mult)
                        tt(OH[:, k, :, :], OH[:, k, :, :], val[:, :].unsqueeze(2).to_broadcast([P, NT, NE]), ALU.mult)
                    dve.tensor_tensor(M[:, :, :], OH[:, 0, :, :], OH[:, 1, :, :], ALU.add).then_inc(s_M, 1)
                    dve.wait_ge(s_ex, 2)
                    reduce(col(PG), g4[:, :, :], ALU.add)
                    ts(col(DN), col(EE), 1.0, None, ALU.add)
                    tt(col(DN), col(DN), col(PG), ALU.mult)
                    do(dve.reciprocal(gate[:, 0, :], col(DN)))
                    tt(gate[:, 1, :], gate[:, 0, :], col(EE), ALU.mult)
                    dve.wait_ge(s_cum, 1)
                    for j in range(1, (T - 1) // CAP + 1):
                        dst = nt if j == 1 else nt1
                        ts(dst[:, :], ps[0:NE, 6, 0:1], float(j * CAP), None, ALU.is_gt)
                        if j > 1:
                            tt(nt[:, :], nt[:, :], nt1[:, :], ALU.add)
                    dve.tensor_scalar(ntb[:, :], ones[0:NE, :], nt[:, 0:1], None, ALU.mult).then_inc(s_nt, 1)
                    for k, (rk, ex) in enumerate(((RK0, EX0), (RK1, EX1))):
                        tt(pr[:, :, :], OH[:, k, :, :], ps[:, 5, 0:NT * NE].rearrange("p (a b) -> p a b", a=NT), ALU.mult)
                        reduce(col(rk), pr[:, :, :], ALU.add)
                        tt(pr[:, :, :], OH[:, k, :, :], row(erow[:, :], NE), ALU.mult)
                        reduce(col(ex), pr[:, :, :], ALU.add)
                    dve.wait_ge(s_base, 1)
                    ts(bcol[:, :], ps[0:NE, 7, 64:65], 0.0, None, ALU.add)
                    tt(bend[:, :], bcol[:, :], nt[:, :], ALU.add)
                    ts(ind[:, :], xrow[:, :], bcol[:, 0:1], None, ALU.is_ge)
                    ts(ind2[:, :], xrow[:, :], bend[:, 0:1], None, ALU.is_lt)
                    dve.tensor_tensor(ind2[:, :], ind2[:, :], ind[:, :], ALU.mult).then_inc(s_ind, 1)
                    for k, (rk, ex, b) in enumerate(((RK0, EX0, B0), (RK1, EX1, B1))):
                        tt(pr[:, :, :], OH[:, k, :, :], ps[:, 7, 0:NE].unsqueeze(1).to_broadcast([P, NT, NE]), ALU.mult)
                        reduce(col(b), pr[:, :, :], ALU.add)
                        ts(col(b), col(b), float(CAP), float((NE - 1) * CAP), ALU.mult, ALU.add)
                        ts(col(ex), col(ex), float(CAP), None, ALU.mult)
                        ts(col(LT), col(rk), float(CAP), None, ALU.is_lt)
                        tt(col(TMP), col(ex), col(b), ALU.subtract)
                        tt(col(TMP), col(TMP), col(LT), ALU.mult)
                        tt(col(TMP), col(TMP), col(b), ALU.add)
                        tt(col(TM2), col(TMP), col(rk), ALU.add)
                        do(dve.tensor_copy(posi[:, k, :], col(TM2)))
                    dve.wait_ge(s_xe, 1)
                    do(dve.tensor_copy(xe[:, :], ps[0:1, 6, 0:NX + 1]))
            clear(s_ld, s_lg, s_ga, s_ex, s_M, s_cum, s_nt, s_base, s_ind, s_xe)

        def scatter_phase(tag, xn, posi):
            s_sc = sem(tag + "rows_scattered")
            with nc.Block() as block:
                @block.gpsimd
                def _(pool):
                    for t in range(NT):
                        for k in range(2):
                            r = rows_of(t)
                            pool.indirect_dma_start(xs[:, :], bass.IndirectOffsetOnAxis(posi[0:r, k, t:t + 1], 0),
                                                    xn[0:r, t, :], None).then_inc(s_sc, 16)
                    pool.wait_ge(s_sc, 2 * NT * 16)

        def expert_phase(tag, sems, W1, W3, W2, xe):
            with ExitStack() as scope:
                al = scope_alloc(scope)
                w1, w3 = al(tag + "w1", [P, 2, KC, HID]), al(tag + "w3", [P, 2, KC, HID])
                w2 = al(tag + "w2", [P, 2, 2, D])
                xg = al(tag + "xg", [CAP, 2, D])
                xgT = al(tag + "xgT", [P, KC, CAP])
                sg, hd = al(tag + "sg", [CAP, HID]), al(tag + "hd", [CAP, HID])
                hT = al(tag + "hT", [P, 2, CAP])
                yb = al(tag + "yb", [CAP, 2, D])
                s_w13 = list(sems("w13_0", "w13_1"))
                s_w2 = list(sems("w2_0", "w2_1"))
                s_x = list(sems("x_0", "x_1"))
                s_yo = list(sems("y_out_0", "y_out_1"))
                s_tx, s_txc, s_ab, s_sg, s_hd, s_th, s_thc, s_y, s_ya, s_yd = sems(
                    "x_turned", "xT_copied", "hidden_products", "silu_done", "hidden_ready", "hidden_turned", "hT_copied",
                    "y_product", "y_act_copied", "y_dve_copied")
                s_ew, s_ex, s_eo = sems("extra_weights", "extra_x", "extra_y_out")
                C = slice(0, CAP)

                def turn_x(pe, u):
                    xc = xg[:, u, :].rearrange("p (q c) -> p c q", c=KC)
                    for c in range(KC):
                        last = pe.transpose(ps[:, c // 4, (c % 4) * CAP:(c % 4 + 1) * CAP], xc[:, c, :], ident[C, C])
                    last.then_inc(s_tx, 1)

                def hidden(pe, w, bank, u):
                    for c in range(KC):
                        last = pe.matmul(ps[C, bank, 0:HID], xgT[:, c, :], w[:, u, c, :], start=c == 0, stop=c == KC - 1)
                    return last

                def turn_hidden(pe):
                    hc = hd[:, :].rearrange("p (q c) -> p c q", c=2)
                    for c in range(2):
                        last = pe.transpose(ps[:, 4, c * CAP:(c + 1) * CAP], hc[:, c, :], ident[C, C])
                    last.then_inc(s_th, 1)

                def output(pe, u):
                    for n in range(2):
                        for c in range(2):
                            last = pe.matmul(ps[C, 5 + n, :], hT[:, c, :], w2[:, u, c, n * 512:(n + 1) * 512], start=c == 0, stop=c == 1)
                    last.then_inc(s_y, 1)

                def pe_step(pe, e, q, u, first=False, last=False):
                    pe.wait_ge(s_txc, e + 1)
                    pe.wait_ge(s_w13[u], 32 * (q + 1))
                    if not first:
                        pe.wait_ge(s_hd, e)
                    hidden(pe, w1, 2, u)
                    if not first:
                        turn_hidden(pe)
                    hidden(pe, w3, 3, u).then_inc(s_ab, 1)
                    if not last:
                        pe.wait_ge(s_x[1 - u], 16 * (q + 1 + u))
                        turn_x(pe, 1 - u)
                    if not first:
                        pe_output(pe, e, q - 1 + u, 1 - u)

                def pe_output(pe, e, q, u):
                    pe.wait_ge(s_thc, e)
                    pe.wait_ge(s_w2[u], 16 * (q + 1))
                    pe.wait_ge(s_ya, e)
                    pe.wait_ge(s_yd, e)
                    output(pe, u)

                def copy_xT(act, e):
                    act.wait_ge(s_tx, e + 1)
                    act.copy(xgT[:, :, :].rearrange("p (a c) n -> p a (c n)", a=2), ps[:, 0:2, 0:4 * CAP]).then_inc(s_txc, 1)

                def silu(act, e):
                    act.wait_ge(s_ab, e + 1)
                    act.activation(sg[:, :], ps[C, 2, 0:HID], ACT.Silu).then_inc(s_sg, 1)

                def hide(dve, e):
                    dve.wait_ge(s_sg, e + 1)
                    dve.tensor_tensor(hd[:, :], sg[:, :], ps[C, 3, 0:HID], ALU.mult).then_inc(s_hd, 1)

                def copy_hT(dve, e):
                    dve.wait_ge(s_th, e + 1)
                    dve.tensor_copy(hT[:, :, :].rearrange("p a b -> p (a b)"), ps[:, 4, 0:2 * CAP]).then_inc(s_thc, 1)

                def load_w13(sp, e, u, sm):
                    sp.dma_start(w1[:, u, :, :], W1[e]).then_inc(sm, 16)
                    sp.dma_start(w3[:, u, :, :], W3[e]).then_inc(sm, 16)

                def load_w2(sp, e, u, sm):
                    sp.dma_start(w2[:, u, :, :], W2[e]).then_inc(sm, 16)

                def slot_rows(buf, e):
                    return buf[bass.ds(e * CAP, CAP), :]

                with nc.Block() as block:
                    @block.sync
                    def _(sp):
                        def load_x(e, u, sm):
                            sp.dma_start(xg[:, u, :], slot_rows(xs, e)).then_inc(sm, 16)

                        for e in range(2):
                            load_x(e, e, s_x[e])
                            load_w13(sp, e, e, s_w13[e])
                            load_w2(sp, e, e, s_w2[e])
                        with sp.Fori(0, NE // 2 - 1) as i:
                            for u in range(2):
                                sp.wait_ge(s_tx, 2 * i + u + 1)
                                load_x(2 * i + 2 + u, u, s_x[u])
                                sp.wait_ge(s_ab, 2 * i + u + 1)
                                load_w13(sp, 2 * i + 2 + u, u, s_w13[u])
                                sp.wait_ge(s_y, 2 * i + u + 1)
                                load_w2(sp, 2 * i + 2 + u, u, s_w2[u])
                        n_extra = sp.value_load(xe[0:1, 0:1], min_val=0, max_val=NX)
                        with sp.If(n_extra > 0):
                            with sp.Fori(0, n_extra) as j:
                                sp.wait_ge(s_y, NE + j)
                                load_x(NE + j, 0, s_ex)
                                e = sp.value_load(xe[0:1, bass.ds(j + 1, 1)], min_val=0, max_val=NE - 1)
                                load_w13(sp, e, 0, s_ew)
                                load_w2(sp, e, 0, s_ew)

                    @block.tensor
                    def _(pe):
                        pe.wait_ge(s_x[0], 16)
                        turn_x(pe, 0)
                        pe_step(pe, 0, 0, 0, first=True)
                        with pe.Fori(0, NE // 2 - 1) as i:
                            pe_step(pe, 2 * i + 1, i, 1)
                            pe_step(pe, 2 * i + 2, i + 1, 0)
                        pe_step(pe, NE - 1, NE // 2 - 1, 1, last=True)
                        pe.wait_ge(s_hd, NE)
                        turn_hidden(pe)
                        pe_output(pe, NE, NE // 2 - 1, 1)
                        n_extra = pe.value_load(xe[0:1, 0:1], min_val=0, max_val=NX)
                        with pe.If(n_extra > 0):
                            with pe.Fori(0, n_extra) as j:
                                pe.wait_ge(s_ew, 48 * (j + 1))
                                pe.wait_ge(s_ex, 16 * (j + 1))
                                turn_x(pe, 0)
                                pe.wait_ge(s_txc, NE + j + 1)
                                hidden(pe, w1, 2, 0)
                                hidden(pe, w3, 3, 0).then_inc(s_ab, 1)
                                pe.wait_ge(s_hd, NE + j + 1)
                                turn_hidden(pe)
                                pe.wait_ge(s_thc, NE + j + 1)
                                pe.wait_ge(s_ya, NE + j + 1)
                                pe.wait_ge(s_yd, NE + j + 1)
                                output(pe, 0)

                    def copy_y(eng, copy, e, u, half, done):
                        eng.wait_ge(s_y, e + 1)
                        copy(yb[:, u, half * 512:(half + 1) * 512], ps[C, 5 + half, :]).then_inc(done, 1)

                    @block.scalar
                    def _(act):
                        act.sem_inc(s_ya, 1)
                        copy_xT(act, 0)

                        def act_step(e, q, u, first=False, last=False):
                            silu(act, e)
                            if not last:
                                copy_xT(act, e + 1)
                            if not first:
                                copy_prev(e, q - 1 + u, 1 - u)

                        def store_y(e, u, sm):
                            act.wait_ge(s_ya, e + 2)
                            act.wait_ge(s_yd, e + 2)
                            act.dma_start(slot_rows(ys, e), yb[:, u, :]).then_inc(sm, 16)

                        def copy_prev(e, q, u, waits=True):
                            if waits:
                                act.wait_ge(s_yo[u], 16 * q)
                            copy_y(act, act.copy, e - 1, u, 0, s_ya)
                            store_y(e - 1, u, s_yo[u])

                        act_step(0, 0, 0, first=True)
                        silu(act, 1); copy_xT(act, 2); copy_prev(1, 0, 0, False)
                        silu(act, 2); copy_xT(act, 3); copy_prev(2, 0, 1, False)
                        with act.Fori(1, NE // 2 - 1) as i:
                            act_step(2 * i + 1, i, 1)
                            act_step(2 * i + 2, i + 1, 0)
                        act_step(NE - 1, NE // 2 - 1, 1, last=True)
                        copy_prev(NE, NE // 2 - 1, 1)
                        for u in range(2):
                            act.wait_ge(s_yo[u], 16 * (NE // 2))
                        n_extra = act.value_load(xe[0:1, 0:1], min_val=0, max_val=NX)
                        with act.If(n_extra > 0):
                            with act.Fori(0, n_extra) as j:
                                copy_xT(act, NE + j)
                                silu(act, NE + j)
                                copy_y(act, act.copy, NE + j, 0, 0, s_ya)
                                store_y(NE + j, 0, s_eo)
                                act.wait_ge(s_eo, 16 * (j + 1))

                    @block.vector
                    def _(dve):
                        dve.sem_inc(s_yd, 1)

                        def dve_step(e, q, u, waits=True):
                            copy_hT(dve, e - 1)
                            hide(dve, e)
                            if waits:
                                dve.wait_ge(s_yo[1 - u], 16 * (q - 1 + u))
                            copy_y(dve, dve.tensor_copy, e - 1, 1 - u, 1, s_yd)

                        hide(dve, 0)
                        dve_step(1, 0, 1, False)
                        dve_step(2, 1, 0, False)
                        with dve.Fori(1, NE // 2 - 1) as i:
                            dve_step(2 * i + 1, i, 1)
                            dve_step(2 * i + 2, i + 1, 0)
                        dve_step(NE - 1, NE // 2 - 1, 1)
                        copy_hT(dve, NE - 1)
                        dve.wait_ge(s_yo[1], 16 * (NE // 2 - 1))
                        copy_y(dve, dve.tensor_copy, NE - 1, 1, 1, s_yd)
                        n_extra = dve.value_load(xe[0:1, 0:1], min_val=0, max_val=NX)
                        with dve.If(n_extra > 0):
                            with dve.Fori(0, n_extra) as j:
                                hide(dve, NE + j)
                                copy_hT(dve, NE + j)
                                copy_y(dve, dve.tensor_copy, NE + j, 0, 1, s_yd)
            clear(*s_w13, *s_w2, *s_x, *s_yo, s_tx, s_txc, s_ab, s_sg, s_hd, s_th, s_thc, s_y, s_ya, s_yd, s_ew, s_ex, s_eo)

        def combine_phase(tag, sems, gate, posi):
            with ExitStack() as scope:
                yg = scope_alloc(scope)(tag + "yg", [P, 2 * NT, D])
                s_add, = sems("rows_added")
                s_g = [sem(f"{tag}gather{n}") for n in range(2 * NT)]
                with nc.Block() as block:
                    @block.gpsimd
                    def _(pool):
                        for n in range(2 * NT):
                            t, k = divmod(n, 2)
                            r = rows_of(t)
                            pool.indirect_dma_start(yg[0:r, n, :], None, ys[:, :],
                                                    bass.IndirectOffsetOnAxis(posi[0:r, k, t:t + 1], 0)).then_inc(s_g[n], 16)

                    @block.vector
                    def _(dve):
                        for n in range(2 * NT):
                            t, k = divmod(n, 2)
                            r = rows_of(t)
                            dve.wait_ge(s_g[n], 16)
                            dve.scalar_tensor_tensor(out=h[0:r, t, :], in0=yg[0:r, n, :], scalar=gate[0:r, k, t:t + 1],
                                                     in1=h[0:r, t, :], op0=ALU.mult, op1=ALU.add).then_inc(s_add, 1)
                            dve.wait_ge(s_add, n + 1)
            clear(s_add)

        with ExitStack() as attn:
            al = scope_alloc(attn)
            qkT = al("qkT", [P, 2 * HEADS, T])
            qT, kT = qkT[:, 0:HEADS, :], qkT[:, HEADS:2 * HEADS, :]
            Vm = al("Vm", [P, NT, HEADS * VD])
            nqT = al("nqT", [P, 4, T])
            nkT = al("nkT", [P, 4, T])
            Vn = al("Vn", [P, NT, HEADS * VD])

            with ExitStack() as scope:
                al = scope_alloc(scope)
                yT = al("yT_a", [P, KC, T])
                with ExitStack() as s2:
                    xn = scope_alloc(s2)("xn_a", [P, NT, D])
                    norm_phase("nrm0", A["norm_mix0"], xn, yT)

                cT = al("cT", [P, 3, T])
                kpe = al("kpe", [P, 2, T])
                NJ, R = 13, 6
                dests = [cT[:, j, :] for j in range(3)] + [kpe[:, j, :] for j in range(2)] \
                    + [nqT[:, j, :] for j in range(4)] + [nkT[:, j, :] for j in range(4)]
                s_w = [sem(f"a1_w{j}_loaded") for j in range(R)]
                s_wnv, s_job, s_ea, s_ed = sem("a1_wnv_loaded"), sem("a1_product"), sem("a1_act_copied"), sem("a1_dve_copied")
                with ExitStack() as s2:
                    al2 = scope_alloc(s2)
                    wr = al2("a1_w", [P, R, KC, P])
                    wnv = al2("a1_wnv", [P, KC, 512])
                    with nc.Block() as block:
                        @block.sync
                        def _(sp):
                            for j in range(NJ):
                                if j >= R:
                                    sp.wait_ge(s_job, j - R + 1)
                                sp.dma_start(wr[:, j % R, :, :], A["wa"][j]).then_inc(s_w[j % R], 16)
                                if j == R - 1:
                                    sp.dma_start(wnv[:, :, :], A["wnv"]).then_inc(s_wnv, 16)

                        @block.tensor
                        def _(pe):
                            for j in range(NJ + NT):
                                s = j % 4
                                if j >= 4:
                                    pe.wait_ge(s_ed if j % 2 else s_ea, (j - 4) // 2 + 1)
                                if j < NJ:
                                    pe.wait_ge(s_w[j % R], 16 * (j // R + 1))
                                    for n in range(2):
                                        for c in range(KC):
                                            last = pe.matmul(ps[:, 2 * s + n, 0:HT], wr[:, j % R, c, :],
                                                             yT[:, c, n * HT:(n + 1) * HT], start=c == 0, stop=c == KC - 1)
                                else:
                                    t = j - NJ
                                    pe.wait_ge(s_wnv, 16)
                                    for c in range(KC):
                                        last = pe.matmul(ps[0:rows_of(t), 2 * s, :], yT[:, c, time_cols(t)],
                                                         wnv[:, c, :], start=c == 0, stop=c == KC - 1)
                                last.then_inc(s_job, 1)

                        def copy_out(j, eng, copy, done):
                            eng.wait_ge(s_job, j + 1)
                            if j < NJ:
                                copy(halves(dests[j]), pair(j % 4)).then_inc(done, 1)
                            else:
                                r = rows_of(j - NJ)
                                copy(Vn[0:r, j - NJ, :], ps[0:r, 2 * (j % 4), :]).then_inc(done, 1)

                        @block.scalar
                        def _(act):
                            for j in range(0, NJ + NT, 2):
                                copy_out(j, act, act.copy, s_ea)

                        @block.vector
                        def _(dve):
                            for j in range(1, NJ + NT, 2):
                                copy_out(j, dve, dve.tensor_copy, s_ed)

                with ExitStack() as s2:
                    al2 = scope_alloc(s2)
                    wuq = al2("wuq", [P, 2, HEADS * QK])
                    wsw = al2("wsw", [P, 2, HEADS * ROPE])
                    wkn = al2("wkn", [P, HEADS * NOPE])
                    wv = al2("wv", [P, HEADS * VD])
                    gl = al2("gl", [P, 3])
                    rc = al2("rope_cos", [P, T])
                    rsn = al2("rope_sin", [P, T])
                    sq = al2("lat_sq", [P, 3, T])
                    mr = al2("lat_ms", [P, 2, T])
                    ra = al2("rope_a", [P, T])
                    rb = al2("rope_b", [P, T])
                    kr = al2("kr", [P, T])
                    s_ld, s_sq, s_sum, s_ms, s_rt, s_cn = (sem(f"a2_{n}") for n in (
                        "weights_loaded", "squares", "sums", "means", "roots", "latents_normed"))
                    s_kr, s_kc, s_q, s_qa, s_qd, s_k, s_ka = (sem(f"a2_{n}") for n in (
                        "key_rotated", "key_copied", "q_product", "q_act_copied", "q_rotated", "kv_product", "kv_copied"))
                    with nc.Block() as block:
                        @block.sync
                        def _(sp):
                            for dst, name in ((wuq[:, :, :], "wuq"), (wsw[:, :, :], "wsw"), (wkn[:, :], "wkn"), (wv[:, :], "wv"),
                                              (gl[:, :], "gl"), (rc[:, :], "rope_cos"), (rsn[:, :], "rope_sin")):
                                sp.dma_start(dst, A[name]).then_inc(s_ld, 16)

                        @block.vector
                        def _(dve):
                            dve.tensor_tensor(sq[:, :, :], cT[:, :, :], cT[:, :, :], ALU.mult).then_inc(s_sq, 1)
                            dve.wait_ge(s_ld, 7 * 16)
                            dve_chain.link(dve, dve.tensor_tensor(ra[:, :], kpe[:, 0, :], rc[:, :], ALU.mult))
                            dve_chain.link(dve, dve.tensor_tensor(rb[:, :], kpe[:, 1, :], rsn[:, :], ALU.mult))
                            dve.tensor_tensor(kr[:, :], ra[:, :], rb[:, :], ALU.add).then_inc(s_kr, 1)
                            dve.wait_ge(s_sum, 2)
                            dve.tensor_scalar(halves(mr[:, 0, :]), pair(0), 1.0 / QR, EPS, ALU.mult, ALU.add).then_inc(s_ms, 1)
                            dve.tensor_scalar(halves(mr[:, 1, :]), pair(1), 1.0 / KVR, EPS, ALU.mult, ALU.add).then_inc(s_ms, 1)
                            dve.wait_ge(s_rt, 1)
                            dve_chain.link(dve, dve.reciprocal(mr[:, :, :], sq[:, 0:2, :]))
                            for j in range(3):
                                dve.scalar_tensor_tensor(out=cT[:, j, :], in0=cT[:, j, :], scalar=gl[:, j:j + 1],
                                                         in1=mr[:, j // 2, :], op0=ALU.mult, op1=ALU.mult).then_inc(s_cn, 1)
                            R6 = slice(NOPE, QK)
                            for g in range(HEADS):
                                s = 2 * (g % 2)
                                dve.wait_ge(s_q, g + 1)
                                dve_chain.link(dve, dve.tensor_tensor(halves(ra[R6, :]), pair(s, R6), halves(rc[R6, :]), ALU.mult))
                                dve_chain.link(dve, dve.tensor_tensor(halves(rb[R6, :]), pair(s + 1, R6), halves(rsn[R6, :]), ALU.mult))
                                dve.tensor_tensor(qT[R6, g, :], ra[R6, :], rb[R6, :], ALU.add).then_inc(s_qd, 1)
                                dve.wait_ge(s_qd, g + 1)

                        @block.gpsimd
                        def _(pool):
                            pool.wait_ge(s_kr, 1)
                            for g in range(HEADS):
                                pool.tensor_copy(kT[NOPE:QK, g, :], kr[NOPE:QK, :]).then_inc(s_kc, 1)
                            pool.wait_ge(s_kc, HEADS)

                        @block.tensor
                        def _(pe):
                            pe.wait_ge(s_sq, 1)
                            for a, chunks in enumerate(((0, 1), (2,))):
                                for n in range(2):
                                    for j in chunks:
                                        last = pe.matmul(ps[:, 2 * a + n, 0:HT], ones[:, :], sq[:, j, n * HT:(n + 1) * HT],
                                                         start=j == chunks[0], stop=j == chunks[-1])
                                last.then_inc(s_sum, 1)
                            pe.wait_ge(s_ld, 7 * 16)
                            pe.wait_ge(s_cn, 3)
                            for g in range(HEADS):
                                s = 2 * (g % 2)
                                if g >= 2:
                                    pe.wait_ge(s_qa, g - 1)
                                    pe.wait_ge(s_qd, g - 1)
                                for n in range(2):
                                    for j in range(2):
                                        pe.matmul(ps[0:QK, 2 * s + n, 0:HT], wuq[:, j, g * QK:(g + 1) * QK],
                                                  cT[:, j, n * HT:(n + 1) * HT], start=j == 0, stop=j == 1)
                                    for j in range(2):
                                        last = pe.matmul(ps[NOPE:QK, 2 * s + 2 + n, 0:HT], wsw[:, j, g * ROPE:(g + 1) * ROPE],
                                                         cT[:, j, n * HT:(n + 1) * HT], start=j == 0, stop=j == 1)
                                last.then_inc(s_q, 1)
                            pe.wait_ge(s_qa, HEADS)
                            pe.wait_ge(s_qd, HEADS)
                            for g in range(HEADS + NT):
                                s = g % 4
                                if g >= 4:
                                    pe.wait_ge(s_ka, g - 3)
                                if g < HEADS:
                                    for n in range(2):
                                        last = pe.matmul(ps[0:NOPE, 2 * s + n, 0:HT], wkn[:, g * NOPE:(g + 1) * NOPE],
                                                         cT[:, 2, n * HT:(n + 1) * HT], start=True, stop=True)
                                else:
                                    t = g - HEADS
                                    last = pe.matmul(ps[0:rows_of(t), 2 * s, :], cT[:, 2, time_cols(t)], wv[:, :],
                                                     start=True, stop=True)
                                last.then_inc(s_k, 1)

                        @block.scalar
                        def _(act):
                            act.wait_ge(s_ms, 2)
                            act.activation(sq[:, 0:2, :], mr[:, :, :], ACT.Sqrt).then_inc(s_rt, 1)
                            for g in range(HEADS):
                                act.wait_ge(s_q, g + 1)
                                act.copy(halves(qT[0:NOPE, g, :]), pair(2 * (g % 2), slice(0, NOPE))).then_inc(s_qa, 1)
                            for g in range(HEADS + NT):
                                act.wait_ge(s_k, g + 1)
                                if g < HEADS:
                                    act.copy(halves(kT[0:NOPE, g, :]), pair(g % 4, slice(0, NOPE))).then_inc(s_ka, 1)
                                else:
                                    t = g - HEADS
                                    act.copy(Vm[0:rows_of(t), t, :], ps[0:rows_of(t), 2 * (g % 4), :]).then_inc(s_ka, 1)

            al = scope_alloc(attn)
            mT = al("mT", [P, KC, T])
            wo = qkT[:, :, :].rearrange("p a b -> p (a b)")[:, 0:KC * D].rearrange("p (k n) -> p k n", k=KC)
            s_wo = sem("a4_w_loaded")
            with ExitStack() as scope:
                al = scope_alloc(scope)
                Pb = al("Pb", [P, 2, NT, T])
                PT = al("PT", [P, 2, NT, T])
                tb = al("tb", [P, HEADS, 14, GRID_W])
                mk = al("mk", [P, GRID_W])
                mx, ng, sm, rc = (al(f"at_{n}", [P, 10]) for n in ("mx", "ng", "sm", "rc"))
                s_tb, s_bias, s_sc, s_ng, s_ex, s_rc, s_pn, s_tr, s_te, s_pv, s_me = (sem(f"at_{n}") for n in (
                    "table_loaded", "bias_ready", "scores", "max_ready", "exps", "reciprocal", "normed",
                    "turned", "turned_copied", "pv", "merged"))
                s_cl = sem("at_meta_cleared")
                NH = 2 * HEADS
                STEPS = NT * NH
                LAG, PVLAG = 6, 7
                MLA_SCALE, NAT_SCALE = QK ** -0.5, NOPE ** -0.5

                def prob(n):
                    g, t = divmod(n, NT)
                    return Pb[0:rows_of(t), g % 2, t, :]

                with nc.Block() as block:
                    @block.sync
                    def _(sp):
                        sp.dma_start(tb[:, :, :, :], A["nat_table"]).then_inc(s_tb, 16)
                        sp.dma_start(mk[:, :], A["nat_mask"]).then_inc(s_tb, 16)
                        sp.wait_ge(s_sc, HEADS * NT)
                        load_out_weights(sp, wo, A["a_w_out"], s_wo)

                    @block.tensor
                    def _(pe):
                        for n in range(STEPS + PVLAG + NT):
                            if n < STEPS:
                                g, t = divmod(n, NT)
                                s, r = n % 2, rows_of(t)
                                if n >= 2:
                                    pe.wait_ge(s_ex, n - 1)
                                if g < HEADS:
                                    for k in range(2):
                                        last = pe.matmul(ps[0:r, 2 * s + k, 0:HT], qT[0:QK, g, time_cols(t)],
                                                         kT[0:QK, g, k * HT:(k + 1) * HT], start=True, stop=True)
                                else:
                                    rr = slice(64 * (g % 2), 64 * (g % 2) + 64)
                                    c = (g - HEADS) // 2
                                    if t < 4:
                                        pe.matmul(ps[0:r, 2 * s, :], nqT[rr, c, time_cols(t)], nkT[rr, c, META:T],
                                                  start=True, stop=True)
                                    last = pe.matmul(ps[0:r, 2 * s + 1, 0:META], nqT[rr, c, time_cols(t)],
                                                     nkT[rr, c, 0:META], start=True, stop=True)
                                last.then_inc(s_sc, 1)
                            m = n - LAG - NT
                            if m >= 0 and m % NT == 0 and m // NT < NH:
                                g = m // NT
                                pe.wait_ge(s_te, NT * (g + 1))
                                if g >= 1:
                                    pe.wait_ge(s_me, g)
                                V = Vm if g < HEADS else Vn
                                o = 64 * (g % 2)
                                for k in range(2):
                                    for kc in range(NT):
                                        r = rows_of(kc)
                                        last = pe.matmul(ps[o:o + 64, 6 + k, 0:HT], V[0:r, kc, (g % HEADS) * VD:(g % HEADS + 1) * VD],
                                                         PT[0:r, g % 2, kc, k * HT:(k + 1) * HT], start=kc == 0, stop=kc == NT - 1)
                                last.then_inc(s_pv, 1)
                            m = n - LAG
                            if 0 <= m < STEPS:
                                g, kc = divmod(m, NT)
                                pe.wait_ge(s_pn, NT * (g + 1))
                                if m >= 1:
                                    pe.wait_ge(s_te, m)
                                for t in range(NT):
                                    r, k = rows_of(t), rows_of(kc)
                                    last = pe.transpose(flat[0:k, 4 * 512 + P * t:4 * 512 + P * t + r],
                                                        Pb[0:r, g % 2, t, time_cols(kc)], ident[0:r, 0:r])
                                last.then_inc(s_tr, 1)

                    @block.vector
                    def _(dve):
                        dve.wait_ge(s_tb, 32)
                        for g in range(HEADS):
                            dve.tensor_tensor(tb[:, g, :, :], tb[:, g, :, :], mk[:, :].unsqueeze(1).to_broadcast([P, 14, GRID_W]),
                                              ALU.add).then_inc(s_bias, 1)
                        dve.wait_ge(s_bias, HEADS)
                        for n in range(STEPS + LAG):
                            if n < STEPS:
                                g, t = divmod(n, NT)
                                s, r, b = n % 2, rows_of(t), n % 10
                                if g >= HEADS and t == 0:
                                    dve.wait_ge(s_tr, NT * (g - 1))
                                    if g < HEADS + 2:
                                        dve.memset(Pb[0:META, g % 2, 4, META:T], 0.0).then_inc(s_cl, 1)
                                dve.wait_ge(s_sc, n + 1)
                                if n >= 10:
                                    dve.wait_ge(s_ex, n - 9)
                                if g < HEADS:
                                    dve_chain.link(dve, dve.tensor_reduce(mx[0:r, b:b + 1], pair(s, slice(0, r)), AX.XY, ALU.max))
                                else:
                                    row = prob(n)
                                    if t < 4:
                                        bias = tb[:, g - HEADS, :, :].rearrange("p a b -> p (a b)")
                                        at = (6 - 2 * t) * GRID_W
                                        dve_chain.link(dve, dve.scalar_tensor_tensor(
                                            out=row[:, META:T], in0=ps[0:r, 2 * s, :], scalar=NAT_SCALE,
                                            in1=bias[:, at:at + SEQ], op0=ALU.mult, op1=ALU.add))
                                    dve_chain.link(dve, dve.tensor_scalar(row[:, 0:META], ps[0:r, 2 * s + 1, 0:META],
                                                                          NAT_SCALE, None, ALU.mult))
                                    cols = T if t < 4 else META
                                    dve_chain.link(dve, dve.tensor_reduce(mx[0:r, b:b + 1], row[:, 0:cols], AX.X, ALU.max))
                                dve.tensor_scalar(ng[0:r, b:b + 1], mx[0:r, b:b + 1],
                                                  -MLA_SCALE if g < HEADS else -1.0, None, ALU.mult).then_inc(s_ng, 1)
                            m = n - 1
                            if 0 <= m < STEPS:
                                r, b = rows_of(m % NT), m % 10
                                dve.wait_ge(s_ex, m + 1)
                                if m >= 10:
                                    dve.wait_ge(s_pn, m - 9)
                                dve.reciprocal(rc[0:r, b:b + 1], sm[0:r, b:b + 1]).then_inc(s_rc, 1)
                            m = n - LAG
                            if 0 <= m < STEPS:
                                g, kc = divmod(m, NT)
                                if kc == 0 and g >= 2:
                                    dve.wait_ge(s_pv, g - 1)
                                dve.wait_ge(s_tr, m + 1)
                                k = rows_of(kc)
                                dve.tensor_copy(PT[0:k, g % 2, kc, :], flat[0:k, 4 * 512:4 * 512 + T]).then_inc(s_te, 1)

                    @block.scalar
                    def _(act):
                        for n in range(STEPS + PVLAG + NT):
                            if n < STEPS:
                                g, t = divmod(n, NT)
                                r, b = rows_of(t), n % 10
                                act.wait_ge(s_ng, n + 1)
                                if n >= 10:
                                    act.wait_ge(s_rc, n - 9)
                                if g < HEADS:
                                    if t == 0 and g >= 2:
                                        act.wait_ge(s_tr, NT * (g - 1))
                                    act.activation(halves(prob(n)), pair(n % 2, slice(0, r)), ACT.Exp, bias=ng[0:r, b:b + 1],
                                                   scale=MLA_SCALE, accum_out=sm[0:r, b:b + 1]).then_inc(s_ex, 1)
                                else:
                                    row = prob(n)[:, 0:T if t < 4 else META]
                                    act.activation(row, row, ACT.Exp, bias=ng[0:r, b:b + 1],
                                                   accum_out=sm[0:r, b:b + 1]).then_inc(s_ex, 1)
                            m = n - LAG - NT
                            if m >= 0 and m % NT == 0 and m // NT < NH:
                                g = m // NT
                                o = 64 * (g % 2)
                                act.wait_ge(s_pv, g + 1)
                                act.copy(halves(mT[o:o + 64, g // 2, :]), pair(3, slice(o, o + 64))).then_inc(s_me, 1)

                    @block.gpsimd
                    def _(pool):
                        for n in range(STEPS):
                            g, t = divmod(n, NT)
                            b = n % 10
                            row = prob(n)[:, 0:T if g < HEADS or t < 4 else META]
                            pool.wait_ge(s_rc, n + 1)
                            pool.tensor_scalar(row, row, rc[0:rows_of(t), b:b + 1], None, ALU.mult).then_inc(s_pn, 1)

            out_phase("a4", lambda k: mT[:, k, :], wo, s_wo, tile_cols)

        moe_phase(0)

        with ExitStack() as conv:
            al = scope_alloc(conv)
            hy = al("hy", [P, 3 * HYC, T])
            glu = al("glu", [P, HYC, T + 2 * PAD31])
            cc = al("cc", [P, HYC, T])

            with ExitStack() as scope:
                al = scope_alloc(scope)
                yT = al("yT_c", [P, KC, T])
                with ExitStack() as s2:
                    xn = scope_alloc(s2)("xn_c", [P, NT, D])
                    norm_phase("nrm2", A["norm_mix1"], xn, yT)
                NJ, NHY, R = 20, 12, 8
                wr = al("c1_w", [P, R, KC, P])
                xp = al("c1_padded", [P, 2, T + 2])
                tap = al("c1_tap", [P, T])
                sg = al("c1_sigmoid", [P, 2, T])
                sw = al("short_w", [P, NHY, 3])
                sbias = al("short_b", [P, NHY])
                s_w = [sem(f"c1_w{j}_loaded") for j in range(R)]
                s_ld, s_pad, s_job, s_ea, s_ed, s_cv = (sem(f"c1_{n}") for n in (
                    "short_loaded", "pads_set", "product", "act_copied", "gated", "short_done"))
                with nc.Block() as block:
                    @block.sync
                    def _(sp):
                        sp.dma_start(sw[:, :, :], A["short_w"]).then_inc(s_ld, 16)
                        sp.dma_start(sbias[:, :], A["short_b"]).then_inc(s_ld, 16)
                        for j in range(NJ):
                            if j >= R:
                                sp.wait_ge(s_job, j - R + 1)
                            sp.dma_start(wr[:, j % R, :, :], A["wc"][j]).then_inc(s_w[j % R], 16)

                    @block.tensor
                    def _(pe):
                        for j in range(NJ):
                            s = j % 4
                            if 4 <= j < 4 + NHY:
                                pe.wait_ge(s_ea, j - 3)
                            elif j >= 4 + NHY and j % 2 == 0:
                                pe.wait_ge(s_ea, NHY + (j - 4 - NHY) // 2 + 1)
                            elif j >= 4 + NHY:
                                pe.wait_ge(s_ed, (j - 4 - NHY) // 2 + 1)
                            pe.wait_ge(s_w[j % R], 16 * (j // R + 1))
                            for n in range(2):
                                for c in range(KC):
                                    last = pe.matmul(ps[:, 2 * s + n, 0:HT], wr[:, j % R, c, :],
                                                     yT[:, c, n * HT:(n + 1) * HT], start=c == 0, stop=c == KC - 1)
                            last.then_inc(s_job, 1)

                    @block.scalar
                    def _(act):
                        act.wait_ge(s_pad, 1)
                        for j in range(NJ):
                            if j >= NHY and (j - NHY) % 2:
                                continue
                            act.wait_ge(s_job, j + 1)
                            if j < NHY:
                                if j >= 2:
                                    act.wait_ge(s_cv, j - 1)
                                act.copy(halves(xp[:, j % 2, 1:T + 1]), pair(j % 4)).then_inc(s_ea, 1)
                            else:
                                i = (j - NHY) // 2
                                if i >= 2:
                                    act.wait_ge(s_ed, i - 1)
                                act.activation(halves(sg[:, i % 2, :]), pair(j % 4), ACT.Sigmoid).then_inc(s_ea, 1)

                    @block.vector
                    def _(dve):
                        dve.memset(glu[:, :, :], 0.0).then_inc(dve_chain.sem, 1)
                        dve_chain.n += 1
                        dve.memset(xp[:, :, :], 0.0).then_inc(s_pad, 1)
                        dve.wait_ge(dve_chain.sem, dve_chain.n)
                        dve.wait_ge(s_ld, 32)
                        for j in range(NHY):
                            x = xp[:, j % 2, :]
                            dve.wait_ge(s_ea, j + 1)
                            if j:
                                dve.wait_ge(s_cv, j)
                            dve_chain.link(dve, dve.tensor_scalar(tap[:, :], x[:, 0:T], sw[:, j, 0:1], sbias[:, j:j + 1], ALU.mult, ALU.add))
                            dve_chain.link(dve, dve.scalar_tensor_tensor(out=tap[:, :], in0=x[:, 1:T + 1], scalar=sw[:, j, 1:2],
                                                                         in1=tap[:, :], op0=ALU.mult, op1=ALU.add))
                            dve.scalar_tensor_tensor(out=hy[:, j, :], in0=x[:, 2:T + 2], scalar=sw[:, j, 2:3],
                                                     in1=tap[:, :], op0=ALU.mult, op1=ALU.add).then_inc(s_cv, 1)
                        for i in range(HYC):
                            j = NHY + 2 * i + 1
                            dve.wait_ge(s_ea, NHY + i + 1)
                            dve.wait_ge(s_job, j + 1)
                            dve.tensor_tensor(halves(glu[:, i, PAD31:PAD31 + T]), pair(j % 4), halves(sg[:, i % 2, :]),
                                              ALU.mult).then_inc(s_ed, 1)
                        dve.wait_ge(s_ed, HYC)

            with ExitStack() as scope:
                al = scope_alloc(scope)
                dft = al("dft", [P, NT, 2 * FC * P])
                idft = al("idft", [P, 2 * FC, T])
                CD = al("CD", [P, 2 * FC, HYW])
                FS = al("FS", [P, 2 * FC, HYW])
                zt = al("zt", [P, NT, HYW])
                eld = al("eld", [P, 4, HYW])
                dec = al("dec", [P, 2, HYW])
                fil = al("fil", [P, 2, HYW])
                tm = al("tm", [P, 4, HYW])
                w3 = al("w3f", [HY_FFN, 4, HYW])
                feat = al("feat", [HY_EMB, T])
                w1 = al("w1f", [HY_EMB, HY_FFN])
                w2 = al("w2f", [HY_FFN, HY_FFN])
                vec = al("hy_vec", [HY_FFN, 3])
                ntc = al("neg_time", [P, NT])
                ck = al("ck", [P, FC])
                hb = al("hy_bias", [P, 2, HYC])
                cw = al("cf_w", [P, HYC, CFK])
                cb = al("cf_b", [P, HYC])
                hid = al("hidf", [HY_FFN, T])
                arg, kk = al("sin_arg", [HY_FFN, T]), al("sin_turns", [HY_FFN, T])
                s_ld, s_u, s_arg, s_sin, s_eld, s_f, s_dec, s_fe, s_fs = (sem(f"c2_{n}") for n in (
                    "constants_loaded", "affine", "argument", "sine", "rates", "filter_product", "decay", "filter_decayed", "filter_ready"))
                s_tp, s_zt, s_sp, s_se, s_ab, s_cx, s_iv, s_z, s_dw = (sem(f"c2_{n}") for n in (
                    "z_turned", "z_copied", "spectrum", "spectrum_copied", "z_spectrum", "product_ready", "inverse", "z_ready", "depthwise"))
                s_ld2, s_a1 = sem("c2_tables_loaded"), sem("c2_affine_read")
                HF = slice(0, HY_FFN)

                with nc.Block() as block:
                    small = [(feat[:, :], "feat"), (w1[:, :], "hy_ffn_w1"), (w2[:, :], "hy_ffn_w2"), (vec[:, :], "hy_vec"),
                             (w3[:, :, :], "hy_ffn_w3"), (eld[:, :, :], "log_decay"), (ntc[:, :], "neg_time"), (ck[:, :], "ck"),
                             (hb[:, :, :], "hy_bias"), (cw[:, :, :], "cf_w"), (cb[:, :], "cf_b")]
                    LD = 16 * len(small)

                    @block.sync
                    def _(sp):
                        for dst, name in small:
                            sp.dma_start(dst, A[name]).then_inc(s_ld, 16)
                        sp.dma_start(dft[:, :, :], A["dft"]).then_inc(s_ld2, 16)
                        sp.dma_start(idft[:, :, :], A["idft"]).then_inc(s_ld2, 16)

                    @block.tensor
                    def _(pe):
                        pe.wait_ge(s_ld, LD)
                        for n in range(2):
                            last = pe.matmul(ps[HF, n, 0:HT], w1[:, :], feat[:, n * HT:(n + 1) * HT], start=True, stop=True)
                        last.then_inc(s_u, 1)
                        pe.wait_ge(s_sin, 1)
                        for n in range(2):
                            last = pe.matmul(ps[HF, 2 + n, 0:HT], w2[:, :], hid[:, n * HT:(n + 1) * HT], start=True, stop=True)
                        last.then_inc(s_u, 1)
                        pe.wait_ge(s_sin, 2)
                        for o in range(2):
                            if o:
                                pe.wait_ge(s_z, HYC)
                            for t in range(NT):
                                r = rows_of(t)
                                if t >= 2:
                                    pe.wait_ge(s_zt, NT * o + t - 1)
                                for c in range(HYC):
                                    last = pe.transpose(ps[0:r, 4 + t % 2, c * P:(c + 1) * P], hy[:, c, time_cols(t)], ident[:, :])
                                last.then_inc(s_tp, 1)
                            for t in range(NT):
                                r = rows_of(t)
                                if NT * o + t >= 2:
                                    pe.wait_ge(s_fe, NT * o + t - 1)
                                for d in range(2):
                                    last = pe.matmul(ps[0:r, 2 * (t % 2) + d, :], hid[:, time_cols(t)], w3[:, 2 * d + o, :],
                                                     start=True, stop=True)
                                last.then_inc(s_f, 1)
                            pe.wait_ge(s_fs, NT * (o + 1))
                            pe.wait_ge(s_ld2, 32)
                            for m in range(2 * FC):
                                if m >= 2:
                                    pe.wait_ge(s_se, 2 * FC * o + m - 1)
                                for t in range(NT):
                                    r = rows_of(t)
                                    last = pe.matmul(ps[:, 6 + m % 2, :], dft[0:r, t, m * P:(m + 1) * P],
                                                     FS[0:r, (m // FC) * FC + t, :], start=t == 0, stop=t == NT - 1)
                                last.then_inc(s_sp, 1)
                            pe.wait_ge(s_zt, NT * (o + 1))
                            for m in range(FC):
                                if m >= 2:
                                    pe.wait_ge(s_cx, FC * o + m - 1)
                                for part in range(2):
                                    for t in range(NT):
                                        r = rows_of(t)
                                        at = (part * FC + m) * P
                                        last = pe.matmul(ps[:, 2 * (m % 2) + part, :], dft[0:r, t, at:at + P], zt[0:r, t, :],
                                                         start=t == 0, stop=t == NT - 1)
                                last.then_inc(s_ab, 1)
                            pe.wait_ge(s_cx, FC * (o + 1))
                            pe.wait_ge(s_se, 2 * FC * (o + 1))
                            for c in range(HYC):
                                if c >= 2:
                                    pe.wait_ge(s_z, HYC * o + c - 1)
                                for n in range(2):
                                    for m in range(2 * FC):
                                        last = pe.matmul(ps[:, 4 + 2 * (c % 2) + n, 0:HT], FS[:, m, c * P:(c + 1) * P],
                                                         idft[:, m, n * HT:(n + 1) * HT], start=m == 0, stop=m == 2 * FC - 1)
                                last.then_inc(s_iv, 1)

                    @block.scalar
                    def _(act):
                        for k in range(2):
                            act.wait_ge(s_arg, k + 1)
                            act.activation(hid[:, :], arg[:, :], ACT.Sin).then_inc(s_sin, 1)
                        act.wait_ge(s_ld, LD)
                        act.activation(eld[:, :, :], eld[:, :, :], ACT.Exp).then_inc(s_eld, 1)
                        act.wait_ge(s_eld, 1)
                        for o in range(2):
                            for t in range(NT):
                                n = NT * o + t
                                r = rows_of(t)
                                act.wait_ge(s_tp, n + 1)
                                act.copy(zt[0:r, t, :], ps[0:r, 4 + t % 2, :]).then_inc(s_zt, 1)
                            for t in range(NT):
                                n = NT * o + t
                                r = rows_of(t)
                                if n >= 1:
                                    act.wait_ge(s_fe, n)
                                act.activation(dec[0:r, :, :], eld[0:r, o::2, :], ACT.Exp,
                                               scale=ntc[0:r, t:t + 1]).then_inc(s_dec, 1)
                            for m in range(2 * FC):
                                act.wait_ge(s_sp, 2 * FC * o + m + 1)
                                if o:
                                    act.wait_ge(s_cx, FC)
                                act.mul(CD[:, m, :], ps[:, 6 + m % 2, :], ck[:, m % FC:m % FC + 1]).then_inc(s_se, 1)

                    @block.vector
                    def _(dve):
                        taps = 0

                        def depthwise(count):
                            nonlocal taps
                            for n in range(taps, min(taps + count, CFK * HYC)):
                                k, c = divmod(n, HYC)
                                x = glu[:, c, k:k + T]
                                if k == 0:
                                    ins = dve.tensor_scalar(cc[:, c, :], x, cw[:, c, 0:1], cb[:, c:c + 1], ALU.mult, ALU.add)
                                else:
                                    dve.wait_ge(s_dw, n - HYC + 1)
                                    ins = dve.scalar_tensor_tensor(out=cc[:, c, :], in0=x, scalar=cw[:, c, k:k + 1],
                                                                   in1=cc[:, c, :], op0=ALU.mult, op1=ALU.add)
                                ins.then_inc(s_dw, 1)
                                taps = n + 1

                        dve.wait_ge(s_ld, LD)
                        for k in range(2):
                            dve.wait_ge(s_u, k + 1)
                            if k:
                                dve.wait_ge(s_sin, 1)
                            dve_chain.link(dve, dve.tensor_scalar(halves(arg[:, :]), pair(k, HF), vec[:, k:k + 1], vec[:, 2:3], ALU.add, ALU.mult))
                            dve_chain.link(dve, dve.tensor_scalar(kk[:, :], arg[:, :], 1.0 / (2 * math.pi), MAGIC, ALU.mult, ALU.add))
                            dve_chain.link(dve, dve.tensor_scalar(kk[:, :], kk[:, :], MAGIC, None, ALU.subtract))
                            for part in TURN:
                                dve_chain.link(dve, dve.scalar_tensor_tensor(out=arg[:, :], in0=kk[:, :], scalar=-part, in1=arg[:, :],
                                                                             op0=ALU.mult, op1=ALU.add))
                            dve.tensor_scalar(arg[:, :], arg[:, :], PI_IN, -PI_IN, ALU.min, ALU.max).then_inc(s_arg, 1)
                        for o in range(2):
                            if o:
                                dve.wait_ge(s_iv, HYC)
                            for t in range(NT):
                                n = NT * o + t
                                r = rows_of(t)
                                dve.wait_ge(s_f, n + 1)
                                dve.wait_ge(s_dec, n + 1)
                                if n:
                                    dve.wait_ge(s_fs, n)
                                dve.tensor_tensor(fil[0:r, :, :], ps[0:r, 2 * (t % 2):2 * (t % 2) + 2, :], dec[0:r, :, :],
                                                  ALU.mult).then_inc(s_fe, 1)
                                dve.wait_ge(s_fe, n + 1)
                                if t == 4:
                                    dve_chain.link(dve, dve.memset(fil[0:1, 1, :], 0.0))
                                dve_chain.link(dve, dve.tensor_tensor(FS[0:r, t, :], fil[0:r, 0, :], fil[0:r, 1, :], ALU.add))
                                dve.tensor_tensor(FS[0:r, FC + t, :], fil[0:r, 0, :], fil[0:r, 1, :], ALU.subtract).then_inc(s_fs, 1)
                            depthwise(42)
                            for m in range(FC):
                                bank = 2 * (m % 2)
                                if m:
                                    depthwise(5)
                                dve.wait_ge(s_ab, FC * o + m + 1)
                                dve.wait_ge(s_se, 2 * FC * (o + 1))
                                if FC * o + m:
                                    dve.wait_ge(s_cx, FC * o + m)
                                C, Dm = CD[:, m, :], CD[:, FC + m, :]
                                for k, (x, y) in enumerate(((0, C), (1, Dm), (0, Dm), (1, C))):
                                    op = dve.tensor_tensor(tm[:, k, :], ps[:, bank + x, :], y, ALU.mult)
                                    if k == 3:
                                        dve_chain.link(dve, op)
                                dve_chain.link(dve, dve.tensor_tensor(FS[:, m, :], tm[:, 0, :], tm[:, 1, :], ALU.subtract))
                                dve.tensor_tensor(FS[:, FC + m, :], tm[:, 2, :], tm[:, 3, :], ALU.add).then_inc(s_cx, 1)
                            for c in range(HYC):
                                dve.wait_ge(s_iv, HYC * o + c + 1)
                                dve.wait_ge(s_cx, FC * (o + 1))
                                if HYC * o + c:
                                    dve.wait_ge(s_z, HYC * o + c)
                                t1 = tm[:, 2 * (c % 2):2 * (c % 2) + 2, :].rearrange("p a b -> p (a b)")[:, 0:T]
                                dve_chain.link(dve, dve.scalar_tensor_tensor(
                                    out=halves(t1), in0=halves(hy[:, c, :]), scalar=hb[:, o, c:c + 1],
                                    in1=ps[:, 4 + 2 * (c % 2):6 + 2 * (c % 2), 0:HT], op0=ALU.mult, op1=ALU.add))
                                dve.tensor_tensor(hy[:, c, :], t1, hy[:, HYC * (o + 1) + c, :], ALU.mult).then_inc(s_z, 1)


            with ExitStack() as scope:
                al = scope_alloc(scope)
                wo = al("wo_c", [P, KC, D])
                s_wo = sem("c5_w_loaded")
                with ExitStack() as s2:
                    al2 = scope_alloc(s2)
                    lg = al2("ln_gb", [P, 2, HYC])
                    mu, sq, rt = al2("ln_mu", [P, T]), al2("ln_sq", [P, HYC, T]), al2("ln_rt", [P, T])
                    s_ld, s_s1, s_sq, s_s2, s_ms, s_rt, s_xc, s_out = (sem(f"c4_{n}") for n in (
                        "loaded", "sums", "squares", "square_sums", "variance", "root", "scaled", "silu"))
                    with nc.Block() as block:
                        @block.sync
                        def _(sp):
                            sp.dma_start(lg[:, :, :], A["ln_gb"]).then_inc(s_ld, 16)
                            load_out_weights(sp, wo, A["c_w_out"], s_wo)

                        @block.tensor
                        def _(pe):
                            for n in range(2):
                                for c in range(HYC):
                                    last = pe.matmul(ps[:, n, 0:HT], ones[:, :], cc[:, c, n * HT:(n + 1) * HT], start=c == 0, stop=c == HYC - 1)
                            last.then_inc(s_s1, 1)
                            pe.wait_ge(s_sq, 1)
                            for n in range(2):
                                for c in range(HYC):
                                    last = pe.matmul(ps[:, 2 + n, 0:HT], ones[:, :], sq[:, c, n * HT:(n + 1) * HT], start=c == 0, stop=c == HYC - 1)
                            last.then_inc(s_s2, 1)

                        @block.vector
                        def _(dve):
                            dve.wait_ge(s_s1, 1)
                            dve_chain.link(dve, dve.tensor_scalar(halves(mu[:, :]), pair(0), 1.0 / HYW, None, ALU.mult))
                            bc = mu[:, :].unsqueeze(1).to_broadcast([P, HYC, T])
                            dve_chain.link(dve, dve.tensor_tensor(cc[:, :, :], cc[:, :, :], bc, ALU.subtract))
                            dve.tensor_tensor(sq[:, :, :], cc[:, :, :], cc[:, :, :], ALU.mult).then_inc(s_sq, 1)
                            dve.wait_ge(s_s2, 1)
                            dve.tensor_scalar(halves(mu[:, :]), pair(1), 1.0 / HYW, EPS, ALU.mult, ALU.add).then_inc(s_ms, 1)
                            dve.wait_ge(s_rt, 1)
                            dve_chain.link(dve, dve.reciprocal(mu[:, :], rt[:, :]))
                            dve.tensor_tensor(cc[:, :, :], cc[:, :, :], bc, ALU.mult).then_inc(s_xc, 1)

                        @block.scalar
                        def _(act):
                            act.wait_ge(s_ms, 1)
                            act.activation(rt[:, :], mu[:, :], ACT.Sqrt).then_inc(s_rt, 1)
                            act.wait_ge(s_ld, 16)
                            act.wait_ge(s_xc, 1)
                            for c in range(HYC):
                                act.activation(cc[:, c, :], cc[:, c, :], ACT.Silu, bias=lg[:, 1, c:c + 1],
                                               scale=lg[:, 0, c:c + 1]).then_inc(s_out, 1)
                            act.wait_ge(s_out, HYC)

                out_phase("c5", lambda k: hy[:, k, :] if k < HYC else cc[:, k - HYC, :], wo, s_wo, time_cols)

        moe_phase(1)
        with ExitStack() as scope:
            xn = scope_alloc(scope)("xn_out", [P, NT, D])
            norm_phase("nrm4", A["norm_final"], xn, None)
            s_out = sem("output_stored")
            with nc.Block() as block:
                @block.sync
                def _(sp):
                    for t in range(4):
                        sp.dma_start(A["out"][0, P * t:P * t + P, :], xn[:, t, :]).then_inc(s_out, 16)
                    sp.wait_ge(s_out, 64)



def tables():
    t = {}
    t["ident"] = np.eye(P, dtype=np.float32)
    pos = np.arange(T, dtype=np.float32)
    inv = (np.float32(10000.0) ** (-np.arange(0, ROPE, 2, dtype=np.float32) / ROPE)).astype(np.float32)
    ang = (inv[:, None] * pos[None, :]).astype(np.float32)
    c, s = np.cos(ang), np.sin(ang)
    t["rope_cos"] = np.tile(np.concatenate([c, c]), (4, 1))
    t["rope_sin"] = np.tile(np.concatenate([-s, s]), (4, 1))
    qc, kc = np.arange(GRID_W)[:, None], np.arange(GRID_W)[None, :]
    start = np.clip(qc - WIN_COLS // 2, 0, GRID_W - WIN_COLS)
    inside = (kc >= start) & (kc < start + WIN_COLS)
    t["nat_mask"] = np.tile(np.where(inside, 0.0, NEG), (2, 1))
    n, k = np.arange(T)[:, None], np.arange(FC * P)[None, :]
    w = 2 * np.pi * ((n * k) % NFFT) / NFFT
    real = k < NF
    both = np.concatenate([np.cos(w) * real, np.sin(w) * real], axis=1)
    dft = np.zeros((P, NT, 2 * FC * P))
    neg_time = np.zeros((P, NT))
    tt = np.linspace(0.0, 1.0, T, dtype=np.float32)
    for i in range(NT):
        r = rows_of(i)
        dft[:r, i] = both[time_cols(i)]
        neg_time[:r, i] = -tt[time_cols(i)]
    t["dft"], t["neg_time"] = dft, neg_time
    t["idft"] = both.T.reshape(2 * FC, P, T).transpose(1, 0, 2)
    weight = np.where((np.arange(FC * P) % T) == 0, 1.0, 2.0) / NFFT
    t["ck"] = weight.reshape(FC, P).T
    bands = np.linspace(1e-4, 15, 16, dtype=np.float32)
    a = (np.float32(2.0 * math.pi) * tt[:, None] * bands[None, :]).astype(np.float32)
    t["feat"] = np.concatenate([tt[:, None], np.cos(a), np.sin(a)], axis=1).T
    e = np.arange(NE)
    t["later"] = (np.arange(P)[:, None] < np.arange(P)[None, :])
    t["later_e"] = (e[:, None] < e[None, :])
    valid = np.zeros((P, NT))
    for i in range(NT):
        valid[:rows_of(i), i] = 1.0
    t["valid"] = valid
    t["first4"] = np.tile(np.arange(GROUPS, 0, -1), (P, 1))
    t["first8"] = np.tile(np.arange(EXPERTS, 0, -1), (P, 1))
    t["expert_row"] = np.tile(e, (P, 1))
    t["expert_col"] = e[:, None]
    t["extra_row"] = np.tile(np.arange(NX), (NE, 1))
    return {k: np.ascontiguousarray(v, dtype=np.float32) for k, v in t.items()}


def lay_out(x):
    a = dict(tables())
    by_chunk = lambda w: w.reshape(P, KC, -1, P).transpose(2, 0, 1, 3)
    cols = lambda v: v.reshape(-1, P).T
    rep = lambda v: np.broadcast_to(v.reshape(1, -1), (P, v.size))
    a["x"], a["meta_tokens"] = x["x"], x["meta_tokens"]
    for i in range(2):
        a[f"norm_mix{i}"], a[f"norm_ffn{i}"] = rep(x["norm_mix"][i]), rep(x["norm_ffn"][i])
        a[f"router_w{i}"] = np.concatenate([x["moe_w_group"][i], x["moe_w_router"][i].transpose(1, 0, 2).reshape(D, NE)],
                                           axis=1).reshape(P, KC, GROUPS + NE)
        a[f"router_b{i}"] = rep(np.concatenate([x["moe_b_group"][i], x["moe_b_router"][i].reshape(-1)]))
    a["norm_final"] = rep(x["norm_final"])
    w = x["a_w_in"][0]
    kpe = w[:, 384:416]
    swap = np.concatenate([kpe[:, 16:], kpe[:, :16]], axis=1)
    a["wa"] = by_chunk(np.concatenate([w[:, 0:384], np.tile(kpe, (1, 4)), np.tile(swap, (1, 4)), w[:, 416:1440]], axis=1))
    a["wnv"] = w[:, 1440:1952].reshape(P, KC, 512)
    uq = x["mla_w_uq"][0].reshape(2, P, HEADS, QK).transpose(1, 0, 2, 3)
    a["wuq"] = uq.reshape(P, 2, HEADS * QK)
    a["wsw"] = np.concatenate([uq[..., NOPE + 16:], uq[..., NOPE:NOPE + 16]], axis=-1).reshape(P, 2, HEADS * ROPE)
    ukv = x["mla_w_ukv"][0].reshape(P, HEADS, NOPE + VD)
    a["wkn"], a["wv"] = ukv[:, :, :NOPE].reshape(P, -1), ukv[:, :, NOPE:].reshape(P, -1)
    a["gl"] = np.concatenate([cols(x["mla_q_norm"][0]), cols(x["mla_kv_norm"][0])], axis=1)
    rpb = x["nat_rpb"][0]
    half, qc = np.divmod(np.arange(P), GRID_W)
    row = np.arange(14)[None, :] + 1 - half[:, None]
    col = np.clip(np.arange(GRID_W)[None, :] - qc[:, None] + WIN_COLS - 1, 0, 2 * WIN_COLS - 2)
    a["nat_table"] = rpb[:, row[:, :, None], col[:, None, :]].transpose(1, 0, 2, 3)
    a["a_w_out"] = x["a_w_out"][0]
    w = x["c_w_in"][0]
    parts = [w[:, 0:1536]]
    for i in range(HYC):
        parts += [w[:, 2048 + P * i:2048 + P * (i + 1)], w[:, 1536 + P * i:1536 + P * (i + 1)]]
    a["wc"] = by_chunk(np.concatenate(parts, axis=1))
    a["short_w"] = x["hy_short_w"][0].reshape(3, 12, P).transpose(2, 1, 0)
    a["short_b"] = cols(x["hy_short_b"][0])
    a["hy_ffn_w1"], a["hy_ffn_w2"] = x["hy_ffn_w1"][0], x["hy_ffn_w2"][0]
    a["hy_ffn_w3"] = x["hy_ffn_w3"][0].reshape(HY_FFN, 4, HYW)
    a["hy_vec"] = np.stack([x["hy_ffn_b1"][0], x["hy_ffn_b2"][0], x["hy_sin_freq"][0]], axis=1)
    a["log_decay"] = np.broadcast_to(x["hy_log_decay"][0].reshape(1, 4, HYW), (P, 4, HYW))
    a["hy_bias"] = x["hy_bias"][0].reshape(2, HYC, P).transpose(2, 0, 1)
    a["cf_w"] = x["cf_dw_w"][0].reshape(CFK, HYC, P).transpose(2, 1, 0)
    a["cf_b"] = cols(x["cf_dw_b"][0])
    a["ln_gb"] = np.stack([cols(x["cf_ln_g"][0]), cols(x["cf_ln_b"][0])], axis=1)
    a["c_w_out"] = x["c_w_out"][0]
    for name in ("moe_w1", "moe_w3", "moe_w2"):
        a[name] = x[name]
    return {k: np.ascontiguousarray(v) for k, v in a.items()}


def kernel(**inputs):
    import concourse.bacc as bacc
    from concourse.bass_utils import run_bass_kernel_spmd

    laid = lay_out({k: np.asarray(v) for k, v in inputs.items()})
    nc = bacc.Bacc("TRN2", target_bir_lowering=False, num_devices=1)
    arrays, aps = {}, {}
    for name, a in laid.items():
        arrays[f"in_{name}"] = a
        aps[name] = nc.dram_tensor(f"in_{name}", a.shape, mybir.dt.from_np(a.dtype), kind="ExternalInput").ap()
    aps["out"] = nc.dram_tensor("out_0_dram", (1, SEQ, D), F32, kind="ExternalOutput").ap()
    build(nc, aps)
    r = run_bass_kernel_spmd(nc, [arrays], core_ids=[0])
    return r.results[0]["out_0_dram"]
```

```python
import math
from contextlib import ExitStack

import numpy as np

import concourse.bass as bass
from concourse import mybir

F32 = mybir.dt.float32
I32 = mybir.dt.int32
ALU = mybir.AluOpType
ACT = mybir.ActivationFunctionType
AX = mybir.AxisListType

P = 128
D = 1024
KC = D // P
META = 16
SEQ = 512
T = META + SEQ
HT = T // 2
NT = 5
EPS = 1e-6
HEADS = 8
NOPE, ROPE, VD = 64, 32, 64
QK = NOPE + ROPE
QR, KVR = 256, 128
WIN_ROWS, WIN_COLS, GRID_W = 8, 16, 64
GROUPS, EXPERTS, HID = 4, 8, 256
NE = GROUPS * EXPERTS
CAP = 64
RING = 4
NX = (2 * T - 1) // CAP
SLOTS = (NE + NX) * CAP
HYW = 512
HYC = HYW // P
CFK = 31
PAD31 = CFK // 2
HY_EMB, HY_FFN = 33, 64
NFFT = 2 * T
NF = T + 1
FC = 5
NEG = -1e30
MAGIC = 1.5 * 2.0 ** 23
TURN = (6.28125, 0.0019350051879882812, 2 * math.pi - 6.28125 - 0.0019350051879882812)
PI_IN = 3.1415925


def rows_of(t):
    return P if t < 4 else META


def time_cols(t):
    return slice(META + P * t, META + P * t + P) if t < 4 else slice(0, META)


def tile_cols(t):
    return slice(P * t, P * t + rows_of(t))


class Chain:

    def __init__(self, sem):
        self.sem, self.n = sem, 0

    def link(self, eng, ins):
        self.n += 1
        ins.then_inc(self.sem, 1)
        eng.wait_ge(self.sem, self.n)


def build(nc, A):
    top = ExitStack()

    def sem(name):
        return top.enter_context(nc.semaphore(name))

    reused = {}

    def sem_again(name):
        if name not in reused:
            reused[name] = sem(name)
        return reused[name]

    def clear(*sems):
        for s in sems:
            nc.gpsimd.sem_clear(s)

    def scope_alloc(scope):
        def alloc(name, shape, dt=F32):
            return scope.enter_context(nc.sbuf_tensor(name, shape, dt))
        return alloc

    with top:
        sb = scope_alloc(top)
        ps = top.enter_context(nc.psum_tensor("ps", [P, 8, 512], F32))
        flat = ps[:, :, :].rearrange("p a b -> p (a b)")

        def pair(s, rows=slice(0, P)):
            return ps[rows, 2 * s:2 * s + 2, 0:HT]

        def halves(ap):
            return ap.rearrange("p (a b) -> p a b", a=2)

        h = sb("h", [P, NT, D])
        ident = sb("ident", [P, P])
        ones = sb("ones", [P, P])
        dve_chain, act_chain = Chain(sem("dve_chain")), Chain(sem("act_chain"))

        xs = nc.dram_tensor("xs_rows", [SLOTS, D], F32).ap()
        ys = nc.dram_tensor("ys_rows", [SLOTS, D], F32).ap()

        s_in, s_one, s_clear = sem("inputs_loaded"), sem("ones_set"), sem("slots_cleared")
        with nc.Block() as block:
            @block.sync
            def _(sp):
                sp.dma_start(h[:, 0:4, :], A["x"].rearrange("b (t p) d -> p (b t) d", p=P)).then_inc(s_in, 16)
                sp.dma_start(h[0:META, 4, :], A["meta_tokens"]).then_inc(s_in, 16)
                sp.dma_start(ident[:, :], A["ident"]).then_inc(s_in, 16)
                sp.wait_ge(s_in, 48)

            @block.vector
            def _(dve):
                dve.memset(ones[:, :], 1.0).then_inc(s_one, 1)
                dve.wait_ge(s_one, 1)

        def clear_slots(eng):
            rows = [xs[n:n + P, :] for n in range(0, SLOTS, P)] + [ys[n:n + P, :] for n in range(NE * CAP, SLOTS, P)]
            for r in rows:
                eng.dma_start(r, A["zeros"]).then_inc(s_clear, 16)
            eng.wait_ge(s_clear, 16 * len(rows))

        def norm_phase(tag, gain, xn, yT):
            s_gain, s_set, s_sq, s_ms, s_rt, s_xn = (sem_again(f"norm_{n}") for n in (
                "gain_loaded", "ssq_set", "squares_summed", "mean_ready", "root_ready", "xn_ready"))
            s_tp, s_ea, s_ed = sem_again("norm_turned"), sem_again("norm_act_copied"), sem_again("norm_dve_copied")
            with ExitStack() as scope:
                al = scope_alloc(scope)
                gbc = al(f"{tag}_gbc", [P, D])
                ssq, ms, rt, rs = (al(f"{tag}_{n}", [P, NT]) for n in ("ssq", "ms", "rt", "rs"))
                with nc.Block() as block:
                    @block.sync
                    def _(sp):
                        sp.dma_start(gbc[:, :], gain).then_inc(s_gain, 16)

                    @block.scalar
                    def _(act):
                        act.wait_ge(s_set, 1)
                        for t in range(NT):
                            r = rows_of(t)
                            act.activation(xn[0:r, t, :], h[0:r, t, :], ACT.Square,
                                           accum_out=ssq[0:r, t:t + 1]).then_inc(s_sq, 1)
                        act.wait_ge(s_ms, 1)
                        act.activation(rt[:, :], ms[:, :], ACT.Sqrt).then_inc(s_rt, 1)
                        if yT is not None:
                            for t in range(NT):
                                act.wait_ge(s_tp, 2 * t + 1)
                                act.copy(yT[:, 0:4, time_cols(t)],
                                         ps[:, (2 * t) % 8, :].rearrange("p (c n) -> p c n", c=4)[:, :, 0:rows_of(t)]
                                         ).then_inc(s_ea, 1)

                    @block.vector
                    def _(dve):
                        dve.memset(ssq[:, :], 1.0).then_inc(s_set, 1)
                        dve.wait_ge(s_sq, NT)
                        dve.tensor_scalar(ms[:, :], ssq[:, :], 1.0 / D, EPS, ALU.mult, ALU.add).then_inc(s_ms, 1)
                        dve.wait_ge(s_rt, 1)
                        dve_chain.link(dve, dve.reciprocal(rs[:, :], rt[:, :]))
                        dve.wait_ge(s_gain, 16)
                        for t in range(NT):
                            r = rows_of(t)
                            dve.scalar_tensor_tensor(out=xn[0:r, t, :], in0=h[0:r, t, :], scalar=rs[0:r, t:t + 1],
                                                     in1=gbc[0:r, :], op0=ALU.mult, op1=ALU.mult).then_inc(s_xn, 1)
                        if yT is not None:
                            for t in range(NT):
                                dve.wait_ge(s_tp, 2 * t + 2)
                                dve.tensor_copy(yT[:, 4:8, time_cols(t)],
                                                ps[:, (2 * t + 1) % 8, :].rearrange("p (c n) -> p c n", c=4)[:, :, 0:rows_of(t)]
                                                ).then_inc(s_ed, 1)
                        else:
                            dve.wait_ge(s_xn, NT)

                    @block.tensor
                    def _(pe):
                        if yT is None:
                            return
                        for t in range(NT):
                            r = rows_of(t)
                            pe.wait_ge(s_xn, t + 1)
                            xc = xn[0:r, t, :].rearrange("p (q c) -> p c q", c=KC)
                            for half in range(2):
                                if t == 4:
                                    pe.wait_ge(s_ed if half else s_ea, 1)
                                bank = (2 * t + half) % 8
                                for c in range(4):
                                    last = pe.transpose(ps[:, bank, c * P:c * P + r], xc[:, 4 * half + c, :], ident[0:r, 0:r])
                                last.then_inc(s_tp, 1)
            clear(s_gain, s_set, s_sq, s_ms, s_rt, s_xn, s_tp, s_ea, s_ed)

        def load_out_weights(sp, wo, w, s_wo):
            for k in range(KC):
                sp.dma_start(wo[:, k, :], w[k * P:(k + 1) * P, :]).then_inc(s_wo, 16)

        def out_phase(tag, chunk, wo, s_wo, cols, tiles, prefetch):
            s_job, s_add = sem(f"{tag}_product"), sem(f"{tag}_added")
            with nc.Block() as block:
                @block.sync
                def _(sp):
                    prefetch(sp)

                @block.tensor
                def _(pe):
                    pe.wait_ge(s_wo, 16 * KC)
                    for j in range(2 * tiles):
                        t, n = divmod(j, 2)
                        if j >= 8:
                            pe.wait_ge(s_add, j - 7)
                        for k in range(KC):
                            last = pe.matmul(ps[0:rows_of(t), j % 8, :], chunk(k)[:, cols(t)], wo[:, k, n * 512:(n + 1) * 512],
                                             start=k == 0, stop=k == KC - 1)
                        last.then_inc(s_job, 1)

                @block.vector
                def _(dve):
                    for j in range(2 * tiles):
                        t, n = divmod(j, 2)
                        r = rows_of(t)
                        hh = h[0:r, t, n * 512:(n + 1) * 512]
                        dve.wait_ge(s_job, j + 1)
                        dve.tensor_tensor(hh, hh, ps[0:r, j % 8, :], ALU.add).then_inc(s_add, 1)
                    dve.wait_ge(s_add, 2 * tiles)

        def expert_weights(L, ring_scope):
            W = [A[n][L].rearrange("g e a b -> (g e) a b") for n in ("moe_w1", "moe_w3", "moe_w2")]
            W1, W3 = (w.rearrange("e (p c) f -> e p c f", c=KC) for w in W[0:2])
            W2 = W[2].rearrange("e (p c) n -> e p c n", c=2)

            def ral(name, shape):
                return ring_scope.enter_context(nc.sbuf_tensor(f"m{L}_{name}", shape, F32, side="right"))

            w1, w3, w2 = ral("w1", [P, RING, KC, HID]), ral("w3", [P, RING, KC, HID]), ral("w2", [P, RING, 2, D])
            s_w13 = [sem_again(f"moe_w13_{r}") for r in range(RING)]
            s_w2 = [sem_again(f"moe_w2_{r}") for r in range(RING)]

            def load_w13(sp, e, r, sm=None):
                sp.dma_start(w1[:, r, :, :], W1[e]).then_inc(sm or s_w13[r], 16)
                sp.dma_start(w3[:, r, :, :], W3[e]).then_inc(sm or s_w13[r], 16)

            def load_w2(sp, e, r, sm=None):
                sp.dma_start(w2[:, r, :, :], W2[e]).then_inc(sm or s_w2[r], 16)

            def prefetch(sp):
                for r in range(RING):
                    load_w13(sp, r, r)
                    load_w2(sp, r, r)

            return w1, w3, w2, s_w13, s_w2, load_w13, load_w2, prefetch

        def moe_phase(L, weights, ring_scope, tiles):
            tag = f"m{L}_"

            def sems(*names):
                return [sem_again("moe_" + n) for n in names]

            with ExitStack() as moe:
                al = scope_alloc(moe)
                gate = al(tag + "gate", [P, 2, NT])
                posi = al(tag + "posi", [P, 2, NT], I32)
                xe = al(tag + "extra", [1, NX + 1], I32)
                with ExitStack() as scope:
                    al = scope_alloc(scope)
                    xn = al(tag + "xn", [P, NT, D])
                    yT = al(tag + "yT", [P, KC, T])
                    norm_phase(f"nrm{2 * L + 1}", A[f"norm_ffn{L}"], xn, yT)
                    route_phase(L, tag, sems, al, yT, gate, posi, xe)
                    scatter_phase(tag, xn, posi, tiles)
                expert_phase(tag, sems, weights, xe)
                ring_scope.close()
                combine_phase(tag, sems, gate, posi, tiles)

        def route_phase(L, tag, sems, al, yT, gate, posi, xe):
            NL = GROUPS + NE
            wr, br = al(tag + "wr", [P, KC, NL]), al(tag + "br", [P, NL])
            lat, late, val = al(tag + "later", [P, P]), al(tag + "later_e", [NE, NE]), al(tag + "valid", [P, NT])
            f4, f8, erow, ecol, xrow = al(tag + "f4", [P, 4]), al(tag + "f8", [P, 8]), al(tag + "erow", [P, NE]), \
                al(tag + "ecol", [NE, 1]), al(tag + "xrow", [NE, NX])
            Lg = al(tag + "logits", [P, NT, NL])
            m4, oh4, g4 = al(tag + "m4", [P, NT, 4]), al(tag + "oh4", [P, NT, 4]), al(tag + "g4", [P, NT, 4])
            el, e2, eq = al(tag + "el", [P, NT, 8]), al(tag + "e2", [P, NT, 8]), al(tag + "eq", [P, NT, 8])
            oh = al(tag + "oh", [P, 2, NT, 8])
            OH = al(tag + "OH", [P, 2, NT, NE])
            M = al(tag + "M", [P, NT, NE])
            pr = al(tag + "pr", [P, NT, NE])
            st = al(tag + "st", [P, 16, NT])
            nt, nt1, ntb = al(tag + "nt", [NE, 1]), al(tag + "nt1", [NE, 1]), al(tag + "ntb", [NE, P])
            bcol, bend, ind, ind2 = al(tag + "bcol", [NE, 1]), al(tag + "bend", [NE, 1]), al(tag + "ind", [NE, NX]), al(tag + "ind2", [NE, NX])
            s_ld, s_lg, s_ga, s_ex, s_M, s_cum, s_nt, s_base, s_ind, s_xe = sems(
                "loaded", "logits", "differences", "exps", "choices", "ranks", "tiles", "bases", "extras", "extra_experts")
            col = lambda k: st[:, k, :]
            GM, MM, M0, M1, PG, EE, DN, RK0, RK1, EX0, EX1, B0, B1, LT, TMP, TM2 = range(16)
            wide = lambda k, n: st[:, k, :].unsqueeze(2).to_broadcast([P, NT, n])
            row = lambda ap, n: ap.unsqueeze(1).to_broadcast([P, NT, n])

            with nc.Block() as block:
                loads = ((wr[:, :, :], f"router_w{L}"), (br[:, :], f"router_b{L}"), (lat[:, :], "later"), (late[:, :], "later_e"),
                         (val[:, :], "valid"), (f4[:, :], "first4"), (f8[:, :], "first8"), (erow[:, :], "expert_row"),
                         (ecol[:, :], "expert_col"), (xrow[:, :], "extra_row"))

                @block.sync
                def _(sp):
                    for dst, name in loads:
                        sp.dma_start(dst, A[name]).then_inc(s_ld, 16)

                @block.tensor
                def _(pe):
                    pe.wait_ge(s_ld, 16 * len(loads))
                    for t in range(NT):
                        for c in range(KC):
                            last = pe.matmul(ps[0:rows_of(t), t, 0:NL], yT[:, c, time_cols(t)], wr[:, c, :],
                                             start=c == 0, stop=c == KC - 1)
                    last.then_inc(s_lg, 1)
                    pe.wait_ge(s_M, 1)
                    for t in range(NT):
                        for k in range(t):
                            pe.matmul(ps[:, 5, t * NE:(t + 1) * NE], ones[:, :], M[:, k, :], start=k == 0, stop=False)
                        pe.matmul(ps[:, 5, t * NE:(t + 1) * NE], lat[:, :], M[:, t, :], start=t == 0, stop=True)
                    for k in range(NT):
                        last = pe.matmul(ps[0:NE, 6, 0:1], M[:, k, :], ones[:, 0:1], start=k == 0, stop=k == NT - 1)
                    last.then_inc(s_cum, 1)
                    pe.wait_ge(s_nt, 1)
                    pe.matmul(ps[:, 7, 0:NE], ntb[:, :], late[:, :], start=True, stop=True)
                    pe.matmul(ps[0:NE, 7, 64:65], late[:, :], nt[:, :], start=True, stop=True).then_inc(s_base, 1)
                    pe.wait_ge(s_ind, 1)
                    pe.matmul(ps[0:1, 6, 0:1], ones[0:NE, 0:1], nt[:, :], start=True, stop=True)
                    pe.matmul(ps[0:1, 6, 1:NX + 1], ecol[:, :], ind2[:, :], start=True, stop=True).then_inc(s_xe, 1)

                @block.scalar
                def _(act):
                    act.wait_ge(s_ga, 1)
                    act.activation(g4[:, :, :], m4[:, :, :], ACT.Exp).then_inc(s_ex, 1)
                    act.wait_ge(s_ga, 2)
                    act.activation(col(EE), col(TMP), ACT.Exp).then_inc(s_ex, 1)

                @block.vector
                def _(dve):
                    def do(ins):
                        dve_chain.link(dve, ins)

                    def tt(out, a, b, op):
                        do(dve.tensor_tensor(out, a, b, op))

                    def ts(out, a, s1, s2, o1, o2=ALU.bypass):
                        do(dve.tensor_scalar(out, a, s1, s2, o1, o2) if s2 is not None else dve.tensor_scalar(out, a, s1, None, o1))

                    def reduce(out, a, op):
                        do(dve.tensor_reduce(out, a, AX.X, op))

                    do(dve.memset(Lg[:, :, :], 0.0))
                    dve.wait_ge(s_ld, 16 * len(loads))
                    dve.wait_ge(s_lg, 1)
                    for t in range(NT):
                        r = rows_of(t)
                        tt(Lg[0:r, t, :], ps[0:r, t, 0:NL], br[0:r, :], ALU.add)
                    G = Lg[:, :, 0:4]
                    reduce(col(GM), G, ALU.max)
                    dve.tensor_tensor(m4[:, :, :], G, wide(GM, 4), ALU.subtract).then_inc(s_ga, 1)
                    tt(oh4[:, :, :], G, wide(GM, 4), ALU.is_equal)
                    tt(oh4[:, :, :], oh4[:, :, :], row(f4[:, :], 4), ALU.mult)
                    reduce(col(MM), oh4[:, :, :], ALU.max)
                    tt(oh4[:, :, :], oh4[:, :, :], wide(MM, 4), ALU.is_equal)
                    for g in range(GROUPS):
                        E = Lg[:, :, GROUPS + EXPERTS * g:GROUPS + EXPERTS * (g + 1)]
                        sel = oh4[:, :, g:g + 1].to_broadcast([P, NT, 8])
                        if g == 0:
                            tt(el[:, :, :], E, sel, ALU.mult)
                        else:
                            tt(e2[:, :, :], E, sel, ALU.mult)
                            tt(el[:, :, :], el[:, :, :], e2[:, :, :], ALU.add)
                    src = el
                    for k, mk_ in ((0, M0), (1, M1)):
                        reduce(col(mk_), src[:, :, :], ALU.max)
                        tt(eq[:, :, :], src[:, :, :], wide(mk_, 8), ALU.is_equal)
                        tt(eq[:, :, :], eq[:, :, :], row(f8[:, :], 8), ALU.mult)
                        reduce(col(MM), eq[:, :, :], ALU.max)
                        tt(oh[:, k, :, :], eq[:, :, :], wide(MM, 8), ALU.is_equal)
                        if k == 0:
                            do(dve.scalar_tensor_tensor(out=e2[:, :, :], in0=oh[:, 0, :, :], scalar=NEG, in1=el[:, :, :],
                                                        op0=ALU.mult, op1=ALU.add))
                            src = e2
                    dve.tensor_tensor(col(TMP), col(M1), col(M0), ALU.subtract).then_inc(s_ga, 1)
                    for k in range(2):
                        for g in range(GROUPS):
                            tt(OH[:, k, :, EXPERTS * g:EXPERTS * (g + 1)], oh[:, k, :, :],
                               oh4[:, :, g:g + 1].to_broadcast([P, NT, 8]), ALU.mult)
                        tt(OH[:, k, :, :], OH[:, k, :, :], val[:, :].unsqueeze(2).to_broadcast([P, NT, NE]), ALU.mult)
                    dve.tensor_tensor(M[:, :, :], OH[:, 0, :, :], OH[:, 1, :, :], ALU.add).then_inc(s_M, 1)
                    dve.wait_ge(s_ex, 2)
                    reduce(col(PG), g4[:, :, :], ALU.add)
                    ts(col(DN), col(EE), 1.0, None, ALU.add)
                    tt(col(DN), col(DN), col(PG), ALU.mult)
                    do(dve.reciprocal(gate[:, 0, :], col(DN)))
                    tt(gate[:, 1, :], gate[:, 0, :], col(EE), ALU.mult)
                    dve.wait_ge(s_cum, 1)
                    for j in range(1, (T - 1) // CAP + 1):
                        dst = nt if j == 1 else nt1
                        ts(dst[:, :], ps[0:NE, 6, 0:1], float(j * CAP), None, ALU.is_gt)
                        if j > 1:
                            tt(nt[:, :], nt[:, :], nt1[:, :], ALU.add)
                    dve.tensor_scalar(ntb[:, :], ones[0:NE, :], nt[:, 0:1], None, ALU.mult).then_inc(s_nt, 1)
                    for k, (rk, ex) in enumerate(((RK0, EX0), (RK1, EX1))):
                        tt(pr[:, :, :], OH[:, k, :, :], ps[:, 5, 0:NT * NE].rearrange("p (a b) -> p a b", a=NT), ALU.mult)
                        reduce(col(rk), pr[:, :, :], ALU.add)
                        tt(pr[:, :, :], OH[:, k, :, :], row(erow[:, :], NE), ALU.mult)
                        reduce(col(ex), pr[:, :, :], ALU.add)
                    dve.wait_ge(s_base, 1)
                    ts(bcol[:, :], ps[0:NE, 7, 64:65], 0.0, None, ALU.add)
                    tt(bend[:, :], bcol[:, :], nt[:, :], ALU.add)
                    ts(ind[:, :], xrow[:, :], bcol[:, 0:1], None, ALU.is_ge)
                    ts(ind2[:, :], xrow[:, :], bend[:, 0:1], None, ALU.is_lt)
                    dve.tensor_tensor(ind2[:, :], ind2[:, :], ind[:, :], ALU.mult).then_inc(s_ind, 1)
                    for k, (rk, ex, b) in enumerate(((RK0, EX0, B0), (RK1, EX1, B1))):
                        tt(pr[:, :, :], OH[:, k, :, :], ps[:, 7, 0:NE].unsqueeze(1).to_broadcast([P, NT, NE]), ALU.mult)
                        reduce(col(b), pr[:, :, :], ALU.add)
                        ts(col(b), col(b), float(CAP), float((NE - 1) * CAP), ALU.mult, ALU.add)
                        ts(col(ex), col(ex), float(CAP), None, ALU.mult)
                        ts(col(LT), col(rk), float(CAP), None, ALU.is_lt)
                        tt(col(TMP), col(ex), col(b), ALU.subtract)
                        tt(col(TMP), col(TMP), col(LT), ALU.mult)
                        tt(col(TMP), col(TMP), col(b), ALU.add)
                        tt(col(TM2), col(TMP), col(rk), ALU.add)
                        do(dve.tensor_copy(posi[:, k, :], col(TM2)))
                    dve.wait_ge(s_xe, 1)
                    do(dve.tensor_copy(xe[:, :], ps[0:1, 6, 0:NX + 1]))
            clear(s_ld, s_lg, s_ga, s_ex, s_M, s_cum, s_nt, s_base, s_ind, s_xe)

        def scatter_phase(tag, xn, posi, tiles):
            s_sc = sem(tag + "rows_scattered")
            with nc.Block() as block:
                @block.gpsimd
                def _(pool):
                    for t in range(tiles):
                        for k in range(2):
                            r = rows_of(t)
                            pool.indirect_dma_start(xs[:, :], bass.IndirectOffsetOnAxis(posi[0:r, k, t:t + 1], 0),
                                                    xn[0:r, t, :], None).then_inc(s_sc, 16)
                    pool.wait_ge(s_sc, 2 * tiles * 16)

        def expert_phase(tag, sems, weights, xe):
            w1, w3, w2, s_w13, s_w2, load_w13, load_w2, _ = weights
            with ExitStack() as scope:
                al = scope_alloc(scope)
                xg = al(tag + "xg", [CAP, RING, D])
                xgT = al(tag + "xgT", [P, KC, CAP])
                sg, hd = al(tag + "sg", [P, HID]), al(tag + "hd", [CAP, HID])
                hT = al(tag + "hT", [P, 2, CAP])
                yb = al(tag + "yb", [P, 2, D // 2])
                s_x = sems(*(f"x_{r}" for r in range(RING)))
                s_yo = sems("y_out_0", "y_out_1")
                s_tx, s_txc, s_ab, s_sg, s_hd, s_th, s_thc, s_y, s_yd = sems(
                    "x_turned", "xT_copied", "hidden_products", "silu_done", "hidden_ready", "hidden_turned", "hT_copied",
                    "y_product", "y_copied")
                s_ew, s_ex, s_eo = sems("extra_weights", "extra_x", "extra_y_out")
                s_turning, = sems("turning")
                C, UP = slice(0, CAP), slice(CAP, 2 * CAP)
                Q = NE // RING

                def turn_x(pe, r, value, sm=None):
                    pe.wait_ge(sm or s_x[r], value)
                    pe.sem_inc(s_turning, 1)
                    xc = xg[:, r, :].rearrange("p (q c) -> p c q", c=KC)
                    for c in range(KC):
                        last = pe.transpose(ps[:, 0, c * CAP:(c + 1) * CAP], xc[:, c, :], ident[C, C])
                    last.then_inc(s_tx, 1)

                def hidden(pe, r, bank):
                    for c in range(KC):
                        pe.matmul(ps[C, bank, 0:HID], xgT[:, c, :], w1[:, r, c, :], start=c == 0, stop=c == KC - 1)
                        last = pe.matmul(ps[UP, bank, 0:HID], xgT[:, c, :], w3[:, r, c, :], start=c == 0, stop=c == KC - 1)
                    last.then_inc(s_ab, 1)

                def turn_hidden(pe, value):
                    pe.wait_ge(s_hd, value)
                    pe.sem_inc(s_turning, 1)
                    hc = hd[:, :].rearrange("p (q c) -> p c q", c=2)
                    for c in range(2):
                        last = pe.transpose(ps[:, 1, c * CAP:(c + 1) * CAP], hc[:, c, :], ident[C, C])
                    last.then_inc(s_th, 1)

                def output(pe, r):
                    for c in range(2):
                        pe.matmul(ps[C, 5, :], hT[:, c, :], w2[:, r, c, 0:512], start=c == 0, stop=c == 1)
                        last = pe.matmul(ps[UP, 5, :], hT[:, c, :], w2[:, r, c, 512:D], start=c == 0, stop=c == 1)
                    last.then_inc(s_y, 1)

                def pe_step(pe, e, q, r, last=False):
                    pe.wait_ge(s_txc, e + 1)
                    pe.wait_ge(s_w13[r], 32 * (q + 1))
                    hidden(pe, r, 2 + r % 2)
                    turn_hidden(pe, e)
                    if not last:
                        n = (r + 1) % RING
                        turn_x(pe, n, 16 * (q + (2 if n == 0 else 1)))
                    pe_output(pe, e, q if r else q - 1, (r - 1) % RING)

                def pe_output(pe, e, q, r):
                    pe.wait_ge(s_thc, e)
                    pe.wait_ge(s_w2[r], 16 * (q + 1))
                    pe.wait_ge(s_yd, e)
                    output(pe, r)

                def copy_xT(act, e):
                    act.wait_ge(s_tx, e + 1)
                    act.copy(xgT[:, :, :].rearrange("p c n -> p (c n)"), ps[:, 0, :]).then_inc(s_txc, 1)

                def silu(act, e, bank):
                    act.wait_ge(s_ab, e + 1)
                    act.activation(sg[UP, :], ps[C, bank, 0:HID], ACT.Silu).then_inc(s_sg, 1)

                def store_y(act, e, u, sm):
                    act.wait_ge(s_yd, e + 2)
                    for n, part in enumerate((C, UP)):
                        act.dma_start(slot_rows(ys, e)[:, n * 512:(n + 1) * 512], yb[part, u, :]).then_inc(sm, 16)

                def hide(dve, e, bank):
                    dve.wait_ge(s_sg, e + 1)
                    dve.tensor_tensor(hd[:, :], sg[UP, :], ps[UP, bank, 0:HID], ALU.mult).then_inc(s_hd, 1)

                def copy_hT(dve, e):
                    dve.wait_ge(s_th, e + 1)
                    dve.tensor_copy(hT[:, :, :].rearrange("p a b -> p (a b)"), ps[:, 1, 0:2 * CAP]).then_inc(s_thc, 1)

                def copy_y(dve, e, u):
                    dve.wait_ge(s_y, e + 1)
                    dve.tensor_copy(yb[:, u, :], ps[:, 5, :]).then_inc(s_yd, 1)

                def slot_rows(buf, e):
                    return buf[bass.ds(e * CAP, CAP), :]

                with nc.Block() as block:
                    @block.sync
                    def _(sp):
                        def load_x(e, r, sm):
                            sp.dma_start(xg[:, r, :], slot_rows(xs, e)).then_inc(sm, 16)

                        for r in range(RING):
                            load_x(r, r, s_x[r])
                        with sp.Fori(0, Q - 1) as i:
                            for r in range(RING):
                                e = RING * i + RING + r
                                sp.wait_ge(s_tx, RING * i + r + 1)
                                load_x(e, r, s_x[r])
                                sp.wait_ge(s_ab, RING * i + r + 1)
                                load_w13(sp, e, r)
                                sp.wait_ge(s_y, RING * i + r + 1)
                                load_w2(sp, e, r)
                        n_extra = sp.value_load(xe[0:1, 0:1], min_val=0, max_val=NX)
                        with sp.If(n_extra > 0):
                            sp.wait_ge(s_y, NE - RING + 1)
                            e = sp.value_load(xe[0:1, 1:2], min_val=0, max_val=NE - 1)
                            load_x(NE, 0, s_ex)
                            load_w13(sp, e, 0, s_ew)
                            load_w2(sp, e, 0, s_ew)
                            with sp.If(n_extra > 1):
                                with sp.Fori(1, n_extra) as j:
                                    sp.wait_ge(s_y, NE + j)
                                    e = sp.value_load(xe[0:1, bass.ds(j + 1, 1)], min_val=0, max_val=NE - 1)
                                    load_x(NE + j, 0, s_ex)
                                    load_w13(sp, e, 0, s_ew)
                                    load_w2(sp, e, 0, s_ew)
                            with sp.Else():
                                sp.nop()

                    @block.tensor
                    def _(pe):
                        turn_x(pe, 0, 16)
                        pe.wait_ge(s_txc, 1)
                        pe.wait_ge(s_w13[0], 32)
                        hidden(pe, 0, 2)
                        turn_x(pe, 1, 16)
                        with pe.Fori(0, Q - 1) as i:
                            for k in range(RING):
                                r = (k + 1) % RING
                                pe_step(pe, RING * i + k + 1, i + (k + 1) // RING, r)
                        for e in range(NE - RING + 1, NE):
                            pe_step(pe, e, Q - 1, e % RING, last=e == NE - 1)
                        turn_hidden(pe, NE)
                        pe_output(pe, NE, Q - 1, RING - 1)
                        n_extra = pe.value_load(xe[0:1, 0:1], min_val=0, max_val=NX)
                        with pe.If(n_extra > 0):
                            with pe.Fori(0, n_extra) as j:
                                turn_x(pe, 0, 16 * (j + 1), s_ex)
                                pe.wait_ge(s_txc, NE + j + 1)
                                pe.wait_ge(s_ew, 48 * (j + 1))
                                hidden(pe, 0, 2)
                                turn_hidden(pe, NE + j + 1)
                                pe.wait_ge(s_thc, NE + j + 1)
                                pe.wait_ge(s_yd, NE + j + 1)
                                output(pe, 0)

                    @block.scalar
                    def _(act):
                        def act_step(e, r, last=False):
                            act.wait_ge(s_hd, e)
                            silu(act, e, 2 + r % 2)
                            if not last:
                                copy_xT(act, e + 1)
                            store_y(act, e - 1, (r - 1) % 2, s_yo[(r - 1) % 2])

                        copy_xT(act, 0)
                        silu(act, 0, 2)
                        copy_xT(act, 1)
                        with act.Fori(0, Q - 1) as i:
                            for k in range(RING):
                                act_step(RING * i + k + 1, (k + 1) % RING)
                        for e in range(NE - RING + 1, NE):
                            act_step(e, e % RING, last=e == NE - 1)
                        store_y(act, NE - 1, 1, s_yo[1])
                        for u in range(2):
                            act.wait_ge(s_yo[u], 16 + 32 * (NE // 2))
                        n_extra = act.value_load(xe[0:1, 0:1], min_val=0, max_val=NX)
                        with act.If(n_extra > 0):
                            with act.Fori(0, n_extra) as j:
                                copy_xT(act, NE + j)
                                act.wait_ge(s_hd, NE + j)
                                silu(act, NE + j, 2)
                                store_y(act, NE + j, 0, s_eo)
                                act.wait_ge(s_eo, 32 * (j + 1))

                    @block.vector
                    def _(dve):
                        dve.sem_inc(s_yd, 1)
                        for u in range(2):
                            dve.sem_inc(s_yo[u], 16)

                        hide(dve, 0, 2)
                        with dve.Fori(0, Q - 1) as i:
                            for k in range(RING):
                                e = RING * i + k + 1
                                copy_hT(dve, e - 1)
                                hide(dve, e, 2 + (k + 1) % 2)
                                dve.wait_ge(s_yo[k % 2], 16 + 32 * (RING // 2 * i + k // 2))
                                copy_y(dve, e - 1, k % 2)
                        for e in range(NE - RING + 1, NE + 1):
                            copy_hT(dve, e - 1)
                            if e < NE:
                                hide(dve, e, 2 + e % 2)
                            dve.wait_ge(s_yo[(e - 1) % 2], 16 + 32 * ((e - 1) // 2))
                            copy_y(dve, e - 1, (e - 1) % 2)
                        n_extra = dve.value_load(xe[0:1, 0:1], min_val=0, max_val=NX)
                        with dve.If(n_extra > 0):
                            with dve.Fori(0, n_extra) as j:
                                hide(dve, NE + j, 2)
                                copy_hT(dve, NE + j)
                                copy_y(dve, NE + j, 0)
            clear(*s_w13, *s_w2, *s_x, *s_yo, s_tx, s_txc, s_ab, s_sg, s_hd, s_th, s_thc, s_y, s_yd, s_ew, s_ex, s_eo,
                  s_turning)

        def combine_phase(tag, sems, gate, posi, tiles):
            with ExitStack() as scope:
                yg = scope_alloc(scope)(tag + "yg", [P, 2 * tiles, D])
                s_add, = sems("rows_added")
                s_g = [sem(f"{tag}gather{n}") for n in range(2 * tiles)]
                with nc.Block() as block:
                    @block.gpsimd
                    def _(pool):
                        for n in range(2 * tiles):
                            t, k = divmod(n, 2)
                            r = rows_of(t)
                            pool.indirect_dma_start(yg[0:r, n, :], None, ys[:, :],
                                                    bass.IndirectOffsetOnAxis(posi[0:r, k, t:t + 1], 0)).then_inc(s_g[n], 16)

                    @block.vector
                    def _(dve):
                        for n in range(2 * tiles):
                            t, k = divmod(n, 2)
                            r = rows_of(t)
                            dve.wait_ge(s_g[n], 16)
                            dve.scalar_tensor_tensor(out=h[0:r, t, :], in0=yg[0:r, n, :], scalar=gate[0:r, k, t:t + 1],
                                                     in1=h[0:r, t, :], op0=ALU.mult, op1=ALU.add).then_inc(s_add, 1)
                            dve.wait_ge(s_add, n + 1)
            clear(s_add)

        with ExitStack() as last:
          al = scope_alloc(last)
          mT = al("mT", [P, KC, T])
          with ExitStack() as attn:
            qkT = al("qkT", [P, 2 * HEADS, T])
            qT, kT = qkT[:, 0:HEADS, :], qkT[:, HEADS:2 * HEADS, :]
            al = scope_alloc(attn)
            Vm = al("Vm", [P, NT, HEADS * VD])
            nqT = al("nqT", [P, 4, T])
            nkT = al("nkT", [P, 4, T])
            Vn = al("Vn", [P, NT, HEADS * VD])

            with ExitStack() as scope:
                al = scope_alloc(scope)
                yT = al("yT_a", [P, KC, T])
                with ExitStack() as s2:
                    xn = scope_alloc(s2)("xn_a", [P, NT, D])
                    norm_phase("nrm0", A["norm_mix0"], xn, yT)

                cT = al("cT", [P, 3, T])
                kpe = al("kpe", [P, 2, T])
                NJ, R = 13, 6
                dests = [cT[:, j, :] for j in range(3)] + [kpe[:, j, :] for j in range(2)] \
                    + [nqT[:, j, :] for j in range(4)] + [nkT[:, j, :] for j in range(4)]
                s_w = [sem(f"a1_w{j}_loaded") for j in range(R)]
                s_wnv, s_job, s_ea, s_ed = sem("a1_wnv_loaded"), sem("a1_product"), sem("a1_act_copied"), sem("a1_dve_copied")
                with ExitStack() as s2:
                    al2 = scope_alloc(s2)
                    wr = al2("a1_w", [P, R, KC, P])
                    wnv = al2("a1_wnv", [P, KC, 512])
                    with nc.Block() as block:
                        @block.sync
                        def _(sp):
                            for j in range(NJ):
                                if j >= R:
                                    sp.wait_ge(s_job, j - R + 1)
                                sp.dma_start(wr[:, j % R, :, :], A["wa"][j]).then_inc(s_w[j % R], 16)
                                if j == R - 1:
                                    sp.dma_start(wnv[:, :, :], A["wnv"]).then_inc(s_wnv, 16)

                        @block.tensor
                        def _(pe):
                            for j in range(NJ + NT):
                                s = j % 4
                                if j >= 4:
                                    pe.wait_ge(s_ed if j % 2 else s_ea, (j - 4) // 2 + 1)
                                if j < NJ:
                                    pe.wait_ge(s_w[j % R], 16 * (j // R + 1))
                                    for n in range(2):
                                        for c in range(KC):
                                            last = pe.matmul(ps[:, 2 * s + n, 0:HT], wr[:, j % R, c, :],
                                                             yT[:, c, n * HT:(n + 1) * HT], start=c == 0, stop=c == KC - 1)
                                else:
                                    t = j - NJ
                                    pe.wait_ge(s_wnv, 16)
                                    for c in range(KC):
                                        last = pe.matmul(ps[0:rows_of(t), 2 * s, :], yT[:, c, time_cols(t)],
                                                         wnv[:, c, :], start=c == 0, stop=c == KC - 1)
                                last.then_inc(s_job, 1)

                        def copy_out(j, eng, copy, done):
                            eng.wait_ge(s_job, j + 1)
                            if j < NJ:
                                copy(halves(dests[j]), pair(j % 4)).then_inc(done, 1)
                            else:
                                r = rows_of(j - NJ)
                                copy(Vn[0:r, j - NJ, :], ps[0:r, 2 * (j % 4), :]).then_inc(done, 1)

                        @block.scalar
                        def _(act):
                            for j in range(0, NJ + NT, 2):
                                copy_out(j, act, act.copy, s_ea)

                        @block.vector
                        def _(dve):
                            for j in range(1, NJ + NT, 2):
                                copy_out(j, dve, dve.tensor_copy, s_ed)

                with ExitStack() as s2:
                    al2 = scope_alloc(s2)
                    wuq = al2("wuq", [P, 2, HEADS * QK])
                    wsw = al2("wsw", [P, 2, HEADS * ROPE])
                    wkn = al2("wkn", [P, HEADS * NOPE])
                    wv = al2("wv", [P, HEADS * VD])
                    gl = al2("gl", [P, 3])
                    rc = al2("rope_cos", [P, T])
                    rsn = al2("rope_sin", [P, T])
                    sq = al2("lat_sq", [P, 3, T])
                    mr = al2("lat_ms", [P, 2, T])
                    ra = al2("rope_a", [P, T])
                    rb = al2("rope_b", [P, T])
                    kr = al2("kr", [P, T])
                    s_ld, s_sq, s_sum, s_ms, s_rt, s_cn = (sem(f"a2_{n}") for n in (
                        "weights_loaded", "squares", "sums", "means", "roots", "latents_normed"))
                    s_kr, s_kc, s_q, s_qa, s_qd, s_k, s_ka = (sem(f"a2_{n}") for n in (
                        "key_rotated", "key_copied", "q_product", "q_act_copied", "q_rotated", "kv_product", "kv_copied"))
                    with nc.Block() as block:
                        @block.sync
                        def _(sp):
                            for dst, name in ((wuq[:, :, :], "wuq"), (wsw[:, :, :], "wsw"), (wkn[:, :], "wkn"), (wv[:, :], "wv"),
                                              (gl[:, :], "gl"), (rc[:, :], "rope_cos"), (rsn[:, :], "rope_sin")):
                                sp.dma_start(dst, A[name]).then_inc(s_ld, 16)

                        @block.vector
                        def _(dve):
                            dve.tensor_tensor(sq[:, :, :], cT[:, :, :], cT[:, :, :], ALU.mult).then_inc(s_sq, 1)
                            dve.wait_ge(s_ld, 7 * 16)
                            dve_chain.link(dve, dve.tensor_tensor(ra[:, :], kpe[:, 0, :], rc[:, :], ALU.mult))
                            dve_chain.link(dve, dve.tensor_tensor(rb[:, :], kpe[:, 1, :], rsn[:, :], ALU.mult))
                            dve.tensor_tensor(kr[:, :], ra[:, :], rb[:, :], ALU.add).then_inc(s_kr, 1)
                            dve.wait_ge(s_sum, 2)
                            dve.tensor_scalar(halves(mr[:, 0, :]), pair(0), 1.0 / QR, EPS, ALU.mult, ALU.add).then_inc(s_ms, 1)
                            dve.tensor_scalar(halves(mr[:, 1, :]), pair(1), 1.0 / KVR, EPS, ALU.mult, ALU.add).then_inc(s_ms, 1)
                            dve.wait_ge(s_rt, 1)
                            dve_chain.link(dve, dve.reciprocal(mr[:, :, :], sq[:, 0:2, :]))
                            for j in range(3):
                                dve.scalar_tensor_tensor(out=cT[:, j, :], in0=cT[:, j, :], scalar=gl[:, j:j + 1],
                                                         in1=mr[:, j // 2, :], op0=ALU.mult, op1=ALU.mult).then_inc(s_cn, 1)
                            R6 = slice(NOPE, QK)
                            for g in range(HEADS):
                                s = 2 * (g % 2)
                                dve.wait_ge(s_q, g + 1)
                                dve_chain.link(dve, dve.tensor_tensor(halves(ra[R6, :]), pair(s, R6), halves(rc[R6, :]), ALU.mult))
                                dve_chain.link(dve, dve.tensor_tensor(halves(rb[R6, :]), pair(s + 1, R6), halves(rsn[R6, :]), ALU.mult))
                                dve.tensor_tensor(qT[R6, g, :], ra[R6, :], rb[R6, :], ALU.add).then_inc(s_qd, 1)
                                dve.wait_ge(s_qd, g + 1)

                        @block.gpsimd
                        def _(pool):
                            pool.wait_ge(s_kr, 1)
                            for g in range(HEADS):
                                pool.tensor_copy(kT[NOPE:QK, g, :], kr[NOPE:QK, :]).then_inc(s_kc, 1)
                            pool.wait_ge(s_kc, HEADS)

                        @block.tensor
                        def _(pe):
                            pe.wait_ge(s_sq, 1)
                            for a, chunks in enumerate(((0, 1), (2,))):
                                for n in range(2):
                                    for j in chunks:
                                        last = pe.matmul(ps[:, 2 * a + n, 0:HT], ones[:, :], sq[:, j, n * HT:(n + 1) * HT],
                                                         start=j == chunks[0], stop=j == chunks[-1])
                                last.then_inc(s_sum, 1)
                            pe.wait_ge(s_ld, 7 * 16)
                            pe.wait_ge(s_cn, 3)
                            for g in range(HEADS):
                                s = 2 * (g % 2)
                                if g >= 2:
                                    pe.wait_ge(s_qa, g - 1)
                                    pe.wait_ge(s_qd, g - 1)
                                for n in range(2):
                                    for j in range(2):
                                        pe.matmul(ps[0:QK, 2 * s + n, 0:HT], wuq[:, j, g * QK:(g + 1) * QK],
                                                  cT[:, j, n * HT:(n + 1) * HT], start=j == 0, stop=j == 1)
                                    for j in range(2):
                                        last = pe.matmul(ps[NOPE:QK, 2 * s + 2 + n, 0:HT], wsw[:, j, g * ROPE:(g + 1) * ROPE],
                                                         cT[:, j, n * HT:(n + 1) * HT], start=j == 0, stop=j == 1)
                                last.then_inc(s_q, 1)
                            pe.wait_ge(s_qa, HEADS)
                            pe.wait_ge(s_qd, HEADS)
                            for g in range(HEADS + NT):
                                s = g % 4
                                if g >= 4:
                                    pe.wait_ge(s_ka, g - 3)
                                if g < HEADS:
                                    for n in range(2):
                                        last = pe.matmul(ps[0:NOPE, 2 * s + n, 0:HT], wkn[:, g * NOPE:(g + 1) * NOPE],
                                                         cT[:, 2, n * HT:(n + 1) * HT], start=True, stop=True)
                                else:
                                    t = g - HEADS
                                    last = pe.matmul(ps[0:rows_of(t), 2 * s, :], cT[:, 2, time_cols(t)], wv[:, :],
                                                     start=True, stop=True)
                                last.then_inc(s_k, 1)

                        @block.scalar
                        def _(act):
                            act.wait_ge(s_ms, 2)
                            act.activation(sq[:, 0:2, :], mr[:, :, :], ACT.Sqrt).then_inc(s_rt, 1)
                            for g in range(HEADS):
                                act.wait_ge(s_q, g + 1)
                                act.copy(halves(qT[0:NOPE, g, :]), pair(2 * (g % 2), slice(0, NOPE))).then_inc(s_qa, 1)
                            for g in range(HEADS + NT):
                                act.wait_ge(s_k, g + 1)
                                if g < HEADS:
                                    act.copy(halves(kT[0:NOPE, g, :]), pair(g % 4, slice(0, NOPE))).then_inc(s_ka, 1)
                                else:
                                    t = g - HEADS
                                    act.copy(Vm[0:rows_of(t), t, :], ps[0:rows_of(t), 2 * (g % 4), :]).then_inc(s_ka, 1)

            wo = qkT[:, :, :].rearrange("p a b -> p (a b)")[:, 0:KC * D].rearrange("p (k n) -> p k n", k=KC)
            s_wo = sem("a4_w_loaded")
            with ExitStack() as scope:
                al = scope_alloc(scope)
                Pb = al("Pb", [P, 2, NT, T])
                PT = al("PT", [P, 2, NT, T])
                tb = al("tb", [P, HEADS, 14, GRID_W])
                mk = al("mk", [P, GRID_W])
                mx, ng, sm, rc = (al(f"at_{n}", [P, 10]) for n in ("mx", "ng", "sm", "rc"))
                s_tb, s_bias, s_sc, s_ng, s_ex, s_rc, s_pn, s_tr, s_te, s_pv, s_me = (sem(f"at_{n}") for n in (
                    "table_loaded", "bias_ready", "scores", "max_ready", "exps", "reciprocal", "normed",
                    "turned", "turned_copied", "pv", "merged"))
                s_cl = sem("at_meta_cleared")
                NH = 2 * HEADS
                STEPS = NT * NH
                LAG, PVLAG = 6, 7
                MLA_SCALE, NAT_SCALE = QK ** -0.5, NOPE ** -0.5

                def prob(n):
                    g, t = divmod(n, NT)
                    return Pb[0:rows_of(t), g % 2, t, :]

                with nc.Block() as block:
                    @block.sync
                    def _(sp):
                        sp.dma_start(tb[:, :, :, :], A["nat_table"]).then_inc(s_tb, 16)
                        sp.dma_start(mk[:, :], A["nat_mask"]).then_inc(s_tb, 16)
                        sp.wait_ge(s_sc, HEADS * NT)
                        load_out_weights(sp, wo, A["a_w_out"], s_wo)
                        clear_slots(sp)

                    @block.tensor
                    def _(pe):
                        for n in range(STEPS + PVLAG + NT):
                            if n < STEPS:
                                g, t = divmod(n, NT)
                                s, r = n % 2, rows_of(t)
                                if n >= 2:
                                    pe.wait_ge(s_ex, n - 1)
                                if g < HEADS:
                                    for k in range(2):
                                        last = pe.matmul(ps[0:r, 2 * s + k, 0:HT], qT[0:QK, g, time_cols(t)],
                                                         kT[0:QK, g, k * HT:(k + 1) * HT], start=True, stop=True)
                                else:
                                    rr = slice(64 * (g % 2), 64 * (g % 2) + 64)
                                    c = (g - HEADS) // 2
                                    if t < 4:
                                        pe.matmul(ps[0:r, 2 * s, :], nqT[rr, c, time_cols(t)], nkT[rr, c, META:T],
                                                  start=True, stop=True)
                                    last = pe.matmul(ps[0:r, 2 * s + 1, 0:META], nqT[rr, c, time_cols(t)],
                                                     nkT[rr, c, 0:META], start=True, stop=True)
                                last.then_inc(s_sc, 1)
                            m = n - LAG - NT
                            if m >= 0 and m % NT == 0 and m // NT < NH:
                                g = m // NT
                                pe.wait_ge(s_te, NT * (g + 1))
                                if g >= 1:
                                    pe.wait_ge(s_me, g)
                                V = Vm if g < HEADS else Vn
                                o = 64 * (g % 2)
                                for k in range(2):
                                    for kc in range(NT):
                                        r = rows_of(kc)
                                        last = pe.matmul(ps[o:o + 64, 6 + k, 0:HT], V[0:r, kc, (g % HEADS) * VD:(g % HEADS + 1) * VD],
                                                         PT[0:r, g % 2, kc, k * HT:(k + 1) * HT], start=kc == 0, stop=kc == NT - 1)
                                last.then_inc(s_pv, 1)
                            m = n - LAG
                            if 0 <= m < STEPS:
                                g, kc = divmod(m, NT)
                                pe.wait_ge(s_pn, NT * (g + 1))
                                if m >= 1:
                                    pe.wait_ge(s_te, m)
                                for t in range(NT):
                                    r, k = rows_of(t), rows_of(kc)
                                    last = pe.transpose(flat[0:k, 4 * 512 + P * t:4 * 512 + P * t + r],
                                                        Pb[0:r, g % 2, t, time_cols(kc)], ident[0:r, 0:r])
                                last.then_inc(s_tr, 1)

                    @block.vector
                    def _(dve):
                        dve.wait_ge(s_tb, 32)
                        for g in range(HEADS):
                            dve.tensor_tensor(tb[:, g, :, :], tb[:, g, :, :], mk[:, :].unsqueeze(1).to_broadcast([P, 14, GRID_W]),
                                              ALU.add).then_inc(s_bias, 1)
                        dve.wait_ge(s_bias, HEADS)
                        for n in range(STEPS + LAG):
                            if n < STEPS:
                                g, t = divmod(n, NT)
                                s, r, b = n % 2, rows_of(t), n % 10
                                if g >= HEADS and t == 0:
                                    dve.wait_ge(s_tr, NT * (g - 1))
                                    if g < HEADS + 2:
                                        dve.memset(Pb[0:META, g % 2, 4, META:T], 0.0).then_inc(s_cl, 1)
                                dve.wait_ge(s_sc, n + 1)
                                if n >= 10:
                                    dve.wait_ge(s_ex, n - 9)
                                if g < HEADS:
                                    dve_chain.link(dve, dve.tensor_reduce(mx[0:r, b:b + 1], pair(s, slice(0, r)), AX.XY, ALU.max))
                                else:
                                    row = prob(n)
                                    if t < 4:
                                        bias = tb[:, g - HEADS, :, :].rearrange("p a b -> p (a b)")
                                        at = (6 - 2 * t) * GRID_W
                                        dve_chain.link(dve, dve.scalar_tensor_tensor(
                                            out=row[:, META:T], in0=ps[0:r, 2 * s, :], scalar=NAT_SCALE,
                                            in1=bias[:, at:at + SEQ], op0=ALU.mult, op1=ALU.add))
                                    dve_chain.link(dve, dve.tensor_scalar(row[:, 0:META], ps[0:r, 2 * s + 1, 0:META],
                                                                          NAT_SCALE, None, ALU.mult))
                                    cols = T if t < 4 else META
                                    dve_chain.link(dve, dve.tensor_reduce(mx[0:r, b:b + 1], row[:, 0:cols], AX.X, ALU.max))
                                dve.tensor_scalar(ng[0:r, b:b + 1], mx[0:r, b:b + 1],
                                                  -MLA_SCALE if g < HEADS else -1.0, None, ALU.mult).then_inc(s_ng, 1)
                            m = n - 1
                            if 0 <= m < STEPS:
                                r, b = rows_of(m % NT), m % 10
                                dve.wait_ge(s_ex, m + 1)
                                if m >= 10:
                                    dve.wait_ge(s_pn, m - 9)
                                dve.reciprocal(rc[0:r, b:b + 1], sm[0:r, b:b + 1]).then_inc(s_rc, 1)
                            m = n - LAG
                            if 0 <= m < STEPS:
                                g, kc = divmod(m, NT)
                                if kc == 0 and g >= 2:
                                    dve.wait_ge(s_pv, g - 1)
                                dve.wait_ge(s_tr, m + 1)
                                k = rows_of(kc)
                                dve.tensor_copy(PT[0:k, g % 2, kc, :], flat[0:k, 4 * 512:4 * 512 + T]).then_inc(s_te, 1)

                    @block.scalar
                    def _(act):
                        for n in range(STEPS + PVLAG + NT):
                            if n < STEPS:
                                g, t = divmod(n, NT)
                                r, b = rows_of(t), n % 10
                                act.wait_ge(s_ng, n + 1)
                                if n >= 10:
                                    act.wait_ge(s_rc, n - 9)
                                if g < HEADS:
                                    if t == 0 and g >= 2:
                                        act.wait_ge(s_tr, NT * (g - 1))
                                    act.activation(halves(prob(n)), pair(n % 2, slice(0, r)), ACT.Exp, bias=ng[0:r, b:b + 1],
                                                   scale=MLA_SCALE, accum_out=sm[0:r, b:b + 1]).then_inc(s_ex, 1)
                                else:
                                    row = prob(n)[:, 0:T if t < 4 else META]
                                    act.activation(row, row, ACT.Exp, bias=ng[0:r, b:b + 1],
                                                   accum_out=sm[0:r, b:b + 1]).then_inc(s_ex, 1)
                            m = n - LAG - NT
                            if m >= 0 and m % NT == 0 and m // NT < NH:
                                g = m // NT
                                o = 64 * (g % 2)
                                act.wait_ge(s_pv, g + 1)
                                act.copy(halves(mT[o:o + 64, g // 2, :]), pair(3, slice(o, o + 64))).then_inc(s_me, 1)

                    @block.gpsimd
                    def _(pool):
                        for n in range(STEPS):
                            g, t = divmod(n, NT)
                            b = n % 10
                            row = prob(n)[:, 0:T if g < HEADS or t < 4 else META]
                            pool.wait_ge(s_rc, n + 1)
                            pool.tensor_scalar(row, row, rc[0:rows_of(t), b:b + 1], None, ALU.mult).then_inc(s_pn, 1)

          ring = ExitStack()
          weights = expert_weights(0, ring)
          out_phase("a4", lambda k: mT[:, k, :], wo, s_wo, tile_cols, NT, weights[-1])

        moe_phase(0, weights, ring, NT)

        with ExitStack() as conv:
            al = scope_alloc(conv)
            hy = al("hy", [P, 3 * HYC, T])
            glu = al("glu", [P, HYC, T + 2 * PAD31])
            cc = al("cc", [P, HYC, T])

            with ExitStack() as scope:
                al = scope_alloc(scope)
                yT = al("yT_c", [P, KC, T])
                with ExitStack() as s2:
                    xn = scope_alloc(s2)("xn_c", [P, NT, D])
                    norm_phase("nrm2", A["norm_mix1"], xn, yT)
                NJ, NHY, R = 20, 12, 8
                wr = al("c1_w", [P, R, KC, P])
                xp = al("c1_padded", [P, 2, T + 2])
                tap = al("c1_tap", [P, T])
                sg = al("c1_sigmoid", [P, 2, T])
                sw = al("short_w", [P, NHY, 3])
                sbias = al("short_b", [P, NHY])
                s_w = [sem(f"c1_w{j}_loaded") for j in range(R)]
                s_ld, s_pad, s_job, s_ea, s_ed, s_cv = (sem(f"c1_{n}") for n in (
                    "short_loaded", "pads_set", "product", "act_copied", "gated", "short_done"))
                with nc.Block() as block:
                    @block.sync
                    def _(sp):
                        sp.dma_start(sw[:, :, :], A["short_w"]).then_inc(s_ld, 16)
                        sp.dma_start(sbias[:, :], A["short_b"]).then_inc(s_ld, 16)
                        for j in range(NJ):
                            if j >= R:
                                sp.wait_ge(s_job, j - R + 1)
                            sp.dma_start(wr[:, j % R, :, :], A["wc"][j]).then_inc(s_w[j % R], 16)

                    @block.tensor
                    def _(pe):
                        for j in range(NJ):
                            s = j % 4
                            if 4 <= j < 4 + NHY:
                                pe.wait_ge(s_ea, j - 3)
                            elif j >= 4 + NHY and j % 2 == 0:
                                pe.wait_ge(s_ea, NHY + (j - 4 - NHY) // 2 + 1)
                            elif j >= 4 + NHY:
                                pe.wait_ge(s_ed, (j - 4 - NHY) // 2 + 1)
                            pe.wait_ge(s_w[j % R], 16 * (j // R + 1))
                            for n in range(2):
                                for c in range(KC):
                                    last = pe.matmul(ps[:, 2 * s + n, 0:HT], wr[:, j % R, c, :],
                                                     yT[:, c, n * HT:(n + 1) * HT], start=c == 0, stop=c == KC - 1)
                            last.then_inc(s_job, 1)

                    @block.scalar
                    def _(act):
                        act.wait_ge(s_pad, 1)
                        for j in range(NJ):
                            if j >= NHY and (j - NHY) % 2:
                                continue
                            act.wait_ge(s_job, j + 1)
                            if j < NHY:
                                if j >= 2:
                                    act.wait_ge(s_cv, j - 1)
                                act.copy(halves(xp[:, j % 2, 1:T + 1]), pair(j % 4)).then_inc(s_ea, 1)
                            else:
                                i = (j - NHY) // 2
                                if i >= 2:
                                    act.wait_ge(s_ed, i - 1)
                                act.activation(halves(sg[:, i % 2, :]), pair(j % 4), ACT.Sigmoid).then_inc(s_ea, 1)

                    @block.vector
                    def _(dve):
                        dve.memset(glu[:, :, :], 0.0).then_inc(dve_chain.sem, 1)
                        dve_chain.n += 1
                        dve.memset(xp[:, :, :], 0.0).then_inc(s_pad, 1)
                        dve.wait_ge(dve_chain.sem, dve_chain.n)
                        dve.wait_ge(s_ld, 32)
                        for j in range(NHY):
                            x = xp[:, j % 2, :]
                            dve.wait_ge(s_ea, j + 1)
                            if j:
                                dve.wait_ge(s_cv, j)
                            dve_chain.link(dve, dve.tensor_scalar(tap[:, :], x[:, 0:T], sw[:, j, 0:1], sbias[:, j:j + 1], ALU.mult, ALU.add))
                            dve_chain.link(dve, dve.scalar_tensor_tensor(out=tap[:, :], in0=x[:, 1:T + 1], scalar=sw[:, j, 1:2],
                                                                         in1=tap[:, :], op0=ALU.mult, op1=ALU.add))
                            dve.scalar_tensor_tensor(out=hy[:, j, :], in0=x[:, 2:T + 2], scalar=sw[:, j, 2:3],
                                                     in1=tap[:, :], op0=ALU.mult, op1=ALU.add).then_inc(s_cv, 1)
                        for i in range(HYC):
                            j = NHY + 2 * i + 1
                            dve.wait_ge(s_ea, NHY + i + 1)
                            dve.wait_ge(s_job, j + 1)
                            dve.tensor_tensor(halves(glu[:, i, PAD31:PAD31 + T]), pair(j % 4), halves(sg[:, i % 2, :]),
                                              ALU.mult).then_inc(s_ed, 1)
                        dve.wait_ge(s_ed, HYC)

            with ExitStack() as scope:
                al = scope_alloc(scope)
                dft = al("dft", [P, NT, 2 * FC * P])
                idft = al("idft", [P, 2 * FC, T])
                CD = al("CD", [P, 2 * FC, HYW])
                FS = al("FS", [P, 2 * FC, HYW])
                zt = al("zt", [P, NT, HYW])
                eld = al("eld", [P, 4, HYW])
                dec = al("dec", [P, 2, HYW])
                fil = al("fil", [P, 2, HYW])
                tm = al("tm", [P, 4, HYW])
                w3 = al("w3f", [HY_FFN, 4, HYW])
                feat = al("feat", [HY_EMB, T])
                w1 = al("w1f", [HY_EMB, HY_FFN])
                w2 = al("w2f", [HY_FFN, HY_FFN])
                vec = al("hy_vec", [HY_FFN, 3])
                ntc = al("neg_time", [P, NT])
                ck = al("ck", [P, FC])
                hb = al("hy_bias", [P, 2, HYC])
                cw = al("cf_w", [P, HYC, CFK])
                cb = al("cf_b", [P, HYC])
                hid = al("hidf", [HY_FFN, T])
                arg, kk = al("sin_arg", [HY_FFN, T]), al("sin_turns", [HY_FFN, T])
                s_ld, s_u, s_arg, s_sin, s_eld, s_f, s_dec, s_fe, s_fs = (sem(f"c2_{n}") for n in (
                    "constants_loaded", "affine", "argument", "sine", "rates", "filter_product", "decay", "filter_decayed", "filter_ready"))
                s_tp, s_zt, s_sp, s_se, s_ab, s_cx, s_iv, s_z, s_dw = (sem(f"c2_{n}") for n in (
                    "z_turned", "z_copied", "spectrum", "spectrum_copied", "z_spectrum", "product_ready", "inverse", "z_ready", "depthwise"))
                s_ld2, s_a1 = sem("c2_tables_loaded"), sem("c2_affine_read")
                HF = slice(0, HY_FFN)

                with nc.Block() as block:
                    small = [(feat[:, :], "feat"), (w1[:, :], "hy_ffn_w1"), (w2[:, :], "hy_ffn_w2"), (vec[:, :], "hy_vec"),
                             (w3[:, :, :], "hy_ffn_w3"), (eld[:, :, :], "log_decay"), (ntc[:, :], "neg_time"), (ck[:, :], "ck"),
                             (hb[:, :, :], "hy_bias"), (cw[:, :, :], "cf_w"), (cb[:, :], "cf_b")]
                    LD = 16 * len(small)

                    @block.sync
                    def _(sp):
                        for dst, name in small:
                            sp.dma_start(dst, A[name]).then_inc(s_ld, 16)
                        sp.dma_start(dft[:, :, :], A["dft"]).then_inc(s_ld2, 16)
                        sp.dma_start(idft[:, :, :], A["idft"]).then_inc(s_ld2, 16)

                    @block.tensor
                    def _(pe):
                        pe.wait_ge(s_ld, LD)
                        for n in range(2):
                            last = pe.matmul(ps[HF, n, 0:HT], w1[:, :], feat[:, n * HT:(n + 1) * HT], start=True, stop=True)
                        last.then_inc(s_u, 1)
                        pe.wait_ge(s_sin, 1)
                        for n in range(2):
                            last = pe.matmul(ps[HF, 2 + n, 0:HT], w2[:, :], hid[:, n * HT:(n + 1) * HT], start=True, stop=True)
                        last.then_inc(s_u, 1)
                        pe.wait_ge(s_sin, 2)
                        for o in range(2):
                            if o:
                                pe.wait_ge(s_z, HYC)
                            for t in range(NT):
                                r = rows_of(t)
                                if t >= 2:
                                    pe.wait_ge(s_zt, NT * o + t - 1)
                                for c in range(HYC):
                                    last = pe.transpose(ps[0:r, 4 + t % 2, c * P:(c + 1) * P], hy[:, c, time_cols(t)], ident[:, :])
                                last.then_inc(s_tp, 1)
                            for t in range(NT):
                                r = rows_of(t)
                                if NT * o + t >= 2:
                                    pe.wait_ge(s_fe, NT * o + t - 1)
                                for d in range(2):
                                    last = pe.matmul(ps[0:r, 2 * (t % 2) + d, :], hid[:, time_cols(t)], w3[:, 2 * d + o, :],
                                                     start=True, stop=True)
                                last.then_inc(s_f, 1)
                            pe.wait_ge(s_fs, NT * (o + 1))
                            pe.wait_ge(s_ld2, 32)
                            for m in range(2 * FC):
                                if m >= 2:
                                    pe.wait_ge(s_se, 2 * FC * o + m - 1)
                                for t in range(NT):
                                    r = rows_of(t)
                                    last = pe.matmul(ps[:, 6 + m % 2, :], dft[0:r, t, m * P:(m + 1) * P],
                                                     FS[0:r, (m // FC) * FC + t, :], start=t == 0, stop=t == NT - 1)
                                last.then_inc(s_sp, 1)
                            pe.wait_ge(s_zt, NT * (o + 1))
                            for m in range(FC):
                                if m >= 2:
                                    pe.wait_ge(s_cx, FC * o + m - 1)
                                for part in range(2):
                                    for t in range(NT):
                                        r = rows_of(t)
                                        at = (part * FC + m) * P
                                        last = pe.matmul(ps[:, 2 * (m % 2) + part, :], dft[0:r, t, at:at + P], zt[0:r, t, :],
                                                         start=t == 0, stop=t == NT - 1)
                                last.then_inc(s_ab, 1)
                            pe.wait_ge(s_cx, FC * (o + 1))
                            pe.wait_ge(s_se, 2 * FC * (o + 1))
                            for c in range(HYC):
                                if c >= 2:
                                    pe.wait_ge(s_z, HYC * o + c - 1)
                                for n in range(2):
                                    for m in range(2 * FC):
                                        last = pe.matmul(ps[:, 4 + 2 * (c % 2) + n, 0:HT], FS[:, m, c * P:(c + 1) * P],
                                                         idft[:, m, n * HT:(n + 1) * HT], start=m == 0, stop=m == 2 * FC - 1)
                                last.then_inc(s_iv, 1)

                    @block.scalar
                    def _(act):
                        for k in range(2):
                            act.wait_ge(s_arg, k + 1)
                            act.activation(hid[:, :], arg[:, :], ACT.Sin).then_inc(s_sin, 1)
                        act.wait_ge(s_ld, LD)
                        act.activation(eld[:, :, :], eld[:, :, :], ACT.Exp).then_inc(s_eld, 1)
                        act.wait_ge(s_eld, 1)
                        for o in range(2):
                            for t in range(NT):
                                n = NT * o + t
                                r = rows_of(t)
                                act.wait_ge(s_tp, n + 1)
                                act.copy(zt[0:r, t, :], ps[0:r, 4 + t % 2, :]).then_inc(s_zt, 1)
                            for t in range(NT):
                                n = NT * o + t
                                r = rows_of(t)
                                if n >= 1:
                                    act.wait_ge(s_fe, n)
                                act.activation(dec[0:r, :, :], eld[0:r, o::2, :], ACT.Exp,
                                               scale=ntc[0:r, t:t + 1]).then_inc(s_dec, 1)
                            for m in range(2 * FC):
                                act.wait_ge(s_sp, 2 * FC * o + m + 1)
                                if o:
                                    act.wait_ge(s_cx, FC)
                                act.mul(CD[:, m, :], ps[:, 6 + m % 2, :], ck[:, m % FC:m % FC + 1]).then_inc(s_se, 1)

                    @block.vector
                    def _(dve):
                        taps = 0

                        def depthwise(count):
                            nonlocal taps
                            for n in range(taps, min(taps + count, CFK * HYC)):
                                k, c = divmod(n, HYC)
                                x = glu[:, c, k:k + T]
                                if k == 0:
                                    ins = dve.tensor_scalar(cc[:, c, :], x, cw[:, c, 0:1], cb[:, c:c + 1], ALU.mult, ALU.add)
                                else:
                                    dve.wait_ge(s_dw, n - HYC + 1)
                                    ins = dve.scalar_tensor_tensor(out=cc[:, c, :], in0=x, scalar=cw[:, c, k:k + 1],
                                                                   in1=cc[:, c, :], op0=ALU.mult, op1=ALU.add)
                                ins.then_inc(s_dw, 1)
                                taps = n + 1

                        dve.wait_ge(s_ld, LD)
                        for k in range(2):
                            dve.wait_ge(s_u, k + 1)
                            if k:
                                dve.wait_ge(s_sin, 1)
                            dve_chain.link(dve, dve.tensor_scalar(halves(arg[:, :]), pair(k, HF), vec[:, k:k + 1], vec[:, 2:3], ALU.add, ALU.mult))
                            dve_chain.link(dve, dve.tensor_scalar(kk[:, :], arg[:, :], 1.0 / (2 * math.pi), MAGIC, ALU.mult, ALU.add))
                            dve_chain.link(dve, dve.tensor_scalar(kk[:, :], kk[:, :], MAGIC, None, ALU.subtract))
                            for part in TURN:
                                dve_chain.link(dve, dve.scalar_tensor_tensor(out=arg[:, :], in0=kk[:, :], scalar=-part, in1=arg[:, :],
                                                                             op0=ALU.mult, op1=ALU.add))
                            dve.tensor_scalar(arg[:, :], arg[:, :], PI_IN, -PI_IN, ALU.min, ALU.max).then_inc(s_arg, 1)
                        for o in range(2):
                            if o:
                                dve.wait_ge(s_iv, HYC)
                            for t in range(NT):
                                n = NT * o + t
                                r = rows_of(t)
                                dve.wait_ge(s_f, n + 1)
                                dve.wait_ge(s_dec, n + 1)
                                if n:
                                    dve.wait_ge(s_fs, n)
                                dve.tensor_tensor(fil[0:r, :, :], ps[0:r, 2 * (t % 2):2 * (t % 2) + 2, :], dec[0:r, :, :],
                                                  ALU.mult).then_inc(s_fe, 1)
                                dve.wait_ge(s_fe, n + 1)
                                if t == 4:
                                    dve_chain.link(dve, dve.memset(fil[0:1, 1, :], 0.0))
                                dve_chain.link(dve, dve.tensor_tensor(FS[0:r, t, :], fil[0:r, 0, :], fil[0:r, 1, :], ALU.add))
                                dve.tensor_tensor(FS[0:r, FC + t, :], fil[0:r, 0, :], fil[0:r, 1, :], ALU.subtract).then_inc(s_fs, 1)
                            depthwise(42)
                            for m in range(FC):
                                bank = 2 * (m % 2)
                                if m:
                                    depthwise(5)
                                dve.wait_ge(s_ab, FC * o + m + 1)
                                dve.wait_ge(s_se, 2 * FC * (o + 1))
                                if FC * o + m:
                                    dve.wait_ge(s_cx, FC * o + m)
                                C, Dm = CD[:, m, :], CD[:, FC + m, :]
                                for k, (x, y) in enumerate(((0, C), (1, Dm), (0, Dm), (1, C))):
                                    op = dve.tensor_tensor(tm[:, k, :], ps[:, bank + x, :], y, ALU.mult)
                                    if k == 3:
                                        dve_chain.link(dve, op)
                                dve_chain.link(dve, dve.tensor_tensor(FS[:, m, :], tm[:, 0, :], tm[:, 1, :], ALU.subtract))
                                dve.tensor_tensor(FS[:, FC + m, :], tm[:, 2, :], tm[:, 3, :], ALU.add).then_inc(s_cx, 1)
                            for c in range(HYC):
                                dve.wait_ge(s_iv, HYC * o + c + 1)
                                dve.wait_ge(s_cx, FC * (o + 1))
                                if HYC * o + c:
                                    dve.wait_ge(s_z, HYC * o + c)
                                t1 = tm[:, 2 * (c % 2):2 * (c % 2) + 2, :].rearrange("p a b -> p (a b)")[:, 0:T]
                                dve_chain.link(dve, dve.scalar_tensor_tensor(
                                    out=halves(t1), in0=halves(hy[:, c, :]), scalar=hb[:, o, c:c + 1],
                                    in1=ps[:, 4 + 2 * (c % 2):6 + 2 * (c % 2), 0:HT], op0=ALU.mult, op1=ALU.add))
                                dve.tensor_tensor(hy[:, c, :], t1, hy[:, HYC * (o + 1) + c, :], ALU.mult).then_inc(s_z, 1)


            with ExitStack() as scope:
                al = scope_alloc(scope)
                wo = al("wo_c", [P, KC, D])
                s_wo = sem("c5_w_loaded")
                with ExitStack() as s2:
                    al2 = scope_alloc(s2)
                    lg = al2("ln_gb", [P, 2, HYC])
                    mu, sq, rt = al2("ln_mu", [P, T]), al2("ln_sq", [P, HYC, T]), al2("ln_rt", [P, T])
                    s_ld, s_s1, s_sq, s_s2, s_ms, s_rt, s_xc, s_out = (sem(f"c4_{n}") for n in (
                        "loaded", "sums", "squares", "square_sums", "variance", "root", "scaled", "silu"))
                    with nc.Block() as block:
                        @block.sync
                        def _(sp):
                            sp.dma_start(lg[:, :, :], A["ln_gb"]).then_inc(s_ld, 16)
                            load_out_weights(sp, wo, A["c_w_out"], s_wo)

                        @block.tensor
                        def _(pe):
                            for n in range(2):
                                for c in range(HYC):
                                    last = pe.matmul(ps[:, n, 0:HT], ones[:, :], cc[:, c, n * HT:(n + 1) * HT], start=c == 0, stop=c == HYC - 1)
                            last.then_inc(s_s1, 1)
                            pe.wait_ge(s_sq, 1)
                            for n in range(2):
                                for c in range(HYC):
                                    last = pe.matmul(ps[:, 2 + n, 0:HT], ones[:, :], sq[:, c, n * HT:(n + 1) * HT], start=c == 0, stop=c == HYC - 1)
                            last.then_inc(s_s2, 1)

                        @block.vector
                        def _(dve):
                            dve.wait_ge(s_s1, 1)
                            dve_chain.link(dve, dve.tensor_scalar(halves(mu[:, :]), pair(0), 1.0 / HYW, None, ALU.mult))
                            bc = mu[:, :].unsqueeze(1).to_broadcast([P, HYC, T])
                            dve_chain.link(dve, dve.tensor_tensor(cc[:, :, :], cc[:, :, :], bc, ALU.subtract))
                            dve.tensor_tensor(sq[:, :, :], cc[:, :, :], cc[:, :, :], ALU.mult).then_inc(s_sq, 1)
                            dve.wait_ge(s_s2, 1)
                            dve.tensor_scalar(halves(mu[:, :]), pair(1), 1.0 / HYW, EPS, ALU.mult, ALU.add).then_inc(s_ms, 1)
                            dve.wait_ge(s_rt, 1)
                            dve_chain.link(dve, dve.reciprocal(mu[:, :], rt[:, :]))
                            dve.tensor_tensor(cc[:, :, :], cc[:, :, :], bc, ALU.mult).then_inc(s_xc, 1)

                        @block.scalar
                        def _(act):
                            act.wait_ge(s_ms, 1)
                            act.activation(rt[:, :], mu[:, :], ACT.Sqrt).then_inc(s_rt, 1)
                            act.wait_ge(s_ld, 16)
                            act.wait_ge(s_xc, 1)
                            for c in range(HYC):
                                act.activation(cc[:, c, :], cc[:, c, :], ACT.Silu, bias=lg[:, 1, c:c + 1],
                                               scale=lg[:, 0, c:c + 1]).then_inc(s_out, 1)
                            act.wait_ge(s_out, HYC)

                ring = ExitStack()
                weights = expert_weights(1, ring)
                out_phase("c5", lambda k: hy[:, k, :] if k < HYC else cc[:, k - HYC, :], wo, s_wo, time_cols, NT - 1, weights[-1])

        moe_phase(1, weights, ring, NT - 1)
        with ExitStack() as scope:
            xn = scope_alloc(scope)("xn_out", [P, NT, D])
            norm_phase("nrm4", A["norm_final"], xn, None)
            s_out = sem("output_stored")
            with nc.Block() as block:
                @block.sync
                def _(sp):
                    for t in range(4):
                        sp.dma_start(A["out"][0, P * t:P * t + P, :], xn[:, t, :]).then_inc(s_out, 16)
                    sp.wait_ge(s_out, 64)



def tables():
    t = {}
    t["ident"] = np.eye(P, dtype=np.float32)
    t["zeros"] = np.zeros((P, D))
    pos = np.arange(T, dtype=np.float32)
    inv = (np.float32(10000.0) ** (-np.arange(0, ROPE, 2, dtype=np.float32) / ROPE)).astype(np.float32)
    ang = (inv[:, None] * pos[None, :]).astype(np.float32)
    c, s = np.cos(ang), np.sin(ang)
    t["rope_cos"] = np.tile(np.concatenate([c, c]), (4, 1))
    t["rope_sin"] = np.tile(np.concatenate([-s, s]), (4, 1))
    qc, kc = np.arange(GRID_W)[:, None], np.arange(GRID_W)[None, :]
    start = np.clip(qc - WIN_COLS // 2, 0, GRID_W - WIN_COLS)
    inside = (kc >= start) & (kc < start + WIN_COLS)
    t["nat_mask"] = np.tile(np.where(inside, 0.0, NEG), (2, 1))
    n, k = np.arange(T)[:, None], np.arange(FC * P)[None, :]
    w = 2 * np.pi * ((n * k) % NFFT) / NFFT
    real = k < NF
    both = np.concatenate([np.cos(w) * real, np.sin(w) * real], axis=1)
    dft = np.zeros((P, NT, 2 * FC * P))
    neg_time = np.zeros((P, NT))
    tt = np.linspace(0.0, 1.0, T, dtype=np.float32)
    for i in range(NT):
        r = rows_of(i)
        dft[:r, i] = both[time_cols(i)]
        neg_time[:r, i] = -tt[time_cols(i)]
    t["dft"], t["neg_time"] = dft, neg_time
    t["idft"] = both.T.reshape(2 * FC, P, T).transpose(1, 0, 2)
    weight = np.where((np.arange(FC * P) % T) == 0, 1.0, 2.0) / NFFT
    t["ck"] = weight.reshape(FC, P).T
    bands = np.linspace(1e-4, 15, 16, dtype=np.float32)
    a = (np.float32(2.0 * math.pi) * tt[:, None] * bands[None, :]).astype(np.float32)
    t["feat"] = np.concatenate([tt[:, None], np.cos(a), np.sin(a)], axis=1).T
    e = np.arange(NE)
    t["later"] = (np.arange(P)[:, None] < np.arange(P)[None, :])
    t["later_e"] = (e[:, None] < e[None, :])
    valid = np.zeros((P, NT))
    for i in range(NT):
        valid[:rows_of(i), i] = 1.0
    t["valid"] = valid
    t["first4"] = np.tile(np.arange(GROUPS, 0, -1), (P, 1))
    t["first8"] = np.tile(np.arange(EXPERTS, 0, -1), (P, 1))
    t["expert_row"] = np.tile(e, (P, 1))
    t["expert_col"] = e[:, None]
    t["extra_row"] = np.tile(np.arange(NX), (NE, 1))
    return {k: np.ascontiguousarray(v, dtype=np.float32) for k, v in t.items()}


def lay_out(x):
    a = dict(tables())
    by_chunk = lambda w: w.reshape(P, KC, -1, P).transpose(2, 0, 1, 3)
    cols = lambda v: v.reshape(-1, P).T
    rep = lambda v: np.broadcast_to(v.reshape(1, -1), (P, v.size))
    a["x"], a["meta_tokens"] = x["x"], x["meta_tokens"]
    for i in range(2):
        a[f"norm_mix{i}"], a[f"norm_ffn{i}"] = rep(x["norm_mix"][i]), rep(x["norm_ffn"][i])
        a[f"router_w{i}"] = np.concatenate([x["moe_w_group"][i], x["moe_w_router"][i].transpose(1, 0, 2).reshape(D, NE)],
                                           axis=1).reshape(P, KC, GROUPS + NE)
        a[f"router_b{i}"] = rep(np.concatenate([x["moe_b_group"][i], x["moe_b_router"][i].reshape(-1)]))
    a["norm_final"] = rep(x["norm_final"])
    w = x["a_w_in"][0]
    kpe = w[:, 384:416]
    swap = np.concatenate([kpe[:, 16:], kpe[:, :16]], axis=1)
    a["wa"] = by_chunk(np.concatenate([w[:, 0:384], np.tile(kpe, (1, 4)), np.tile(swap, (1, 4)), w[:, 416:1440]], axis=1))
    a["wnv"] = w[:, 1440:1952].reshape(P, KC, 512)
    uq = x["mla_w_uq"][0].reshape(2, P, HEADS, QK).transpose(1, 0, 2, 3)
    a["wuq"] = uq.reshape(P, 2, HEADS * QK)
    a["wsw"] = np.concatenate([uq[..., NOPE + 16:], uq[..., NOPE:NOPE + 16]], axis=-1).reshape(P, 2, HEADS * ROPE)
    ukv = x["mla_w_ukv"][0].reshape(P, HEADS, NOPE + VD)
    a["wkn"], a["wv"] = ukv[:, :, :NOPE].reshape(P, -1), ukv[:, :, NOPE:].reshape(P, -1)
    a["gl"] = np.concatenate([cols(x["mla_q_norm"][0]), cols(x["mla_kv_norm"][0])], axis=1)
    rpb = x["nat_rpb"][0]
    half, qc = np.divmod(np.arange(P), GRID_W)
    row = np.arange(14)[None, :] + 1 - half[:, None]
    col = np.clip(np.arange(GRID_W)[None, :] - qc[:, None] + WIN_COLS - 1, 0, 2 * WIN_COLS - 2)
    a["nat_table"] = rpb[:, row[:, :, None], col[:, None, :]].transpose(1, 0, 2, 3)
    a["a_w_out"] = x["a_w_out"][0]
    w = x["c_w_in"][0]
    parts = [w[:, 0:1536]]
    for i in range(HYC):
        parts += [w[:, 2048 + P * i:2048 + P * (i + 1)], w[:, 1536 + P * i:1536 + P * (i + 1)]]
    a["wc"] = by_chunk(np.concatenate(parts, axis=1))
    a["short_w"] = x["hy_short_w"][0].reshape(3, 12, P).transpose(2, 1, 0)
    a["short_b"] = cols(x["hy_short_b"][0])
    a["hy_ffn_w1"], a["hy_ffn_w2"] = x["hy_ffn_w1"][0], x["hy_ffn_w2"][0]
    a["hy_ffn_w3"] = x["hy_ffn_w3"][0].reshape(HY_FFN, 4, HYW)
    a["hy_vec"] = np.stack([x["hy_ffn_b1"][0], x["hy_ffn_b2"][0], x["hy_sin_freq"][0]], axis=1)
    a["log_decay"] = np.broadcast_to(x["hy_log_decay"][0].reshape(1, 4, HYW), (P, 4, HYW))
    a["hy_bias"] = x["hy_bias"][0].reshape(2, HYC, P).transpose(2, 0, 1)
    a["cf_w"] = x["cf_dw_w"][0].reshape(CFK, HYC, P).transpose(2, 1, 0)
    a["cf_b"] = cols(x["cf_dw_b"][0])
    a["ln_gb"] = np.stack([cols(x["cf_ln_g"][0]), cols(x["cf_ln_b"][0])], axis=1)
    a["c_w_out"] = x["c_w_out"][0]
    for name in ("moe_w1", "moe_w3", "moe_w2"):
        a[name] = x[name]
    return {k: np.ascontiguousarray(v) for k, v in a.items()}


def kernel(**inputs):
    import concourse.bacc as bacc
    from concourse.bass_utils import run_bass_kernel_spmd

    laid = lay_out({k: np.asarray(v) for k, v in inputs.items()})
    nc = bacc.Bacc("TRN2", target_bir_lowering=False, num_devices=1)
    arrays, aps = {}, {}
    for name, a in laid.items():
        arrays[f"in_{name}"] = a
        aps[name] = nc.dram_tensor(f"in_{name}", a.shape, mybir.dt.from_np(a.dtype), kind="ExternalInput").ap()
    aps["out"] = nc.dram_tensor("out_0_dram", (1, SEQ, D), F32, kind="ExternalOutput").ap()
    build(nc, aps)
    r = run_bass_kernel_spmd(nc, [arrays], core_ids=[0])
    return r.results[0]["out_0_dram"]
```

```python
import math
from contextlib import ExitStack

import numpy as np

import concourse.bass as bass
from concourse import mybir

F32 = mybir.dt.float32
I32 = mybir.dt.int32
ALU = mybir.AluOpType
ACT = mybir.ActivationFunctionType
AX = mybir.AxisListType

P = 128
D = 1024
KC = D // P
META = 16
SEQ = 512
T = META + SEQ
HT = T // 2
NT = 5
EPS = 1e-6
HEADS = 8
NOPE, ROPE, VD = 64, 32, 64
QK = NOPE + ROPE
QR, KVR = 256, 128
WIN_ROWS, WIN_COLS, GRID_W = 8, 16, 64
GROUPS, EXPERTS, HID = 4, 8, 256
NE = GROUPS * EXPERTS
NL = GROUPS + NE
CAP = 64
RING = 4
AROUND = 4
NX = (2 * T - 1) // CAP
SLOTS = (NE + NX) * CAP
HYW = 512
HYC = HYW // P
CFK = 31
PAD31 = CFK // 2
HY_EMB, HY_FFN = 33, 64
NFFT = 2 * T
NF = T + 1
FC = 5
FL = T // 2 + 1
FT = 3
NEG = -1e30
MAGIC = 1.5 * 2.0 ** 23
TURN = (6.28125, 0.0019350051879882812, 2 * math.pi - 6.28125 - 0.0019350051879882812)
PI_IN = 3.1415925


def rows_of(t):
    return P if t < 4 else META


def fold_rows(t):
    return min(P, FL - P * t)


def spectrum_rows(m):
    return P if m < 4 else 64


def time_cols(t):
    return slice(META + P * t, META + P * t + P) if t < 4 else slice(0, META)


def tile_cols(t):
    return slice(P * t, P * t + rows_of(t))


class Chain:

    def __init__(self, sem):
        self.sem, self.n = sem, 0

    def link(self, eng, ins):
        self.n += 1
        ins.then_inc(self.sem, 1)
        eng.wait_ge(self.sem, self.n)


def build(nc, A):
    top = ExitStack()

    def sem(name):
        return top.enter_context(nc.semaphore(name))

    reused = {}

    def sem_again(name):
        if name not in reused:
            reused[name] = sem(name)
        return reused[name]

    def clear(*sems):
        for s in sems:
            nc.gpsimd.sem_clear(s)

    def scope_alloc(scope):
        def alloc(name, shape, dt=F32):
            return scope.enter_context(nc.sbuf_tensor(name, shape, dt))
        return alloc

    with top:
        sb = scope_alloc(top)
        ps = top.enter_context(nc.psum_tensor("ps", [P, 8, 512], F32))
        flat = ps[:, :, :].rearrange("p a b -> p (a b)")

        def pair(s, rows=slice(0, P)):
            return ps[rows, 2 * s:2 * s + 2, 0:HT]

        def halves(ap):
            return ap.rearrange("p (a b) -> p a b", a=2)

        h = sb("h", [P, NT, D])
        ident = sb("ident", [P, P])
        ones = sb("ones", [P, P])
        router_b = sb("router_b", [P, 2, NL])
        later, valid = sb("later", [P, P]), sb("valid", [P, 2, NT])
        first = sb("first", [P, GROUPS + EXPERTS + NE])
        expert_tab = sb("expert_tab", [NE, NE + 1 + NX])
        s_router = sem("router_loaded")
        router_loads = ((router_b, "router_b"), (later, "later"), (valid, "valid"), (first, "first"),
                        (expert_tab, "expert_tab"))
        dve_chain = Chain(sem("dve_chain"))

        xs = nc.dram_tensor("xs_rows", [SLOTS, D], F32).ap()
        ys = nc.dram_tensor("ys_rows", [SLOTS, D], F32).ap()

        s_in, s_one, s_clear = [sem(f"input{t}_loaded") for t in range(NT)], sem("ones_set"), sem("slots_cleared")
        s_ident = sem("ident_loaded")
        s_gain, s_squares = sem_again("norm_gain_loaded"), sem_again("norm_squares_summed")
        ssq = sb("square_sums", [P, NT])

        def on_right(scope, name, shape):
            return scope.enter_context(nc.sbuf_tensor(name, shape, F32, side="right"))

        def load_gain(sp, gbc, gain):
            sp.dma_start(gbc[:, :], gain).then_inc(s_gain, 16)

        def square(act, t, scratch):
            r = rows_of(t)
            act.activation(scratch[0:r, :], h[0:r, t, :], ACT.Square, accum_out=ssq[0:r, t:t + 1]).then_inc(s_squares, 1)

        first_norm = ExitStack()
        gain0 = on_right(first_norm, "gain_mix0", [P, D])
        scratch0 = on_right(first_norm, "squares_mix0", [P, NT, D])
        with nc.Block() as block:
            @block.sync
            def _(sp):
                for t in range(NT):
                    sp.dma_start(h[0:rows_of(t), t, :], A["x"][0, P * t:P * t + P, :] if t < 4 else A["meta_tokens"]).then_inc(s_in[t], 16)
                load_gain(sp, gain0, A["norm_mix0"])
                sp.dma_start(ident[:, :], A["ident"]).then_inc(s_ident, 16)
                for dst, name in router_loads:
                    src = A[name]
                    sp.dma_start(dst[:, :] if len(src.shape) == 2 else dst[:, :, :], src).then_inc(s_router, 16)
                sp.wait_ge(s_ident, 16)

            @block.scalar
            def _(act):
                act.wait_ge(s_one, 2)
                for t in range(NT):
                    act.wait_ge(s_in[t], 16)
                    square(act, t, scratch0[:, t, :])

            @block.vector
            def _(dve):
                dve.memset(ones[:, :], 1.0).then_inc(s_one, 1)
                dve.memset(ssq[:, :], 1.0).then_inc(s_one, 1)
                dve.wait_ge(s_one, 2)

        def clear_slots(eng):
            rows = [xs[n:n + P, :] for n in range(0, SLOTS, P)] + [ys[n:n + P, :] for n in range(NE * CAP, SLOTS, P)]
            for r in rows:
                eng.dma_start(r, A["zeros"]).then_inc(s_clear, 16)
            eng.wait_ge(s_clear, 16 * len(rows))

        LOGIT_BANK = 2

        def norm_phase(tag, gbc, xn, yT, tiles=NT, also=(), store=None, router=None):
            s_ms, s_rt, s_xn = (sem_again(f"norm_{n}") for n in ("mean_ready", "root_ready", "xn_ready"))
            s_tp, s_ea, s_ed = sem_again("norm_turned"), sem_again("norm_act_copied"), sem_again("norm_dve_copied")
            with ExitStack() as scope:
                al = scope_alloc(scope)
                ms, rt, rs = (al(f"{tag}_{n}", [P, NT]) for n in ("ms", "rt", "rs"))
                with nc.Block() as block:
                    @block.sync
                    def _(sp):
                        for dst, src, done in also:
                            sp.dma_start(dst, src).then_inc(done, 16)
                        if store is not None:
                            s_out = sem("output_stored")
                            for t in range(tiles):
                                sp.wait_ge(s_xn, t + 1)
                                sp.dma_start(store[0, P * t:P * t + P, :], xn[:, t, :]).then_inc(s_out, 16)
                            sp.wait_ge(s_out, 16 * tiles)

                    @block.scalar
                    def _(act):
                        act.wait_ge(s_ms, 1)
                        act.activation(rt[:, :], ms[:, :], ACT.Sqrt).then_inc(s_rt, 1)
                        if yT is not None:
                            for t in range(NT):
                                act.wait_ge(s_tp, 2 * t + 1)
                                act.copy(yT[:, 0:4, time_cols(t)],
                                         ps[:, (2 * t) % 8, :].rearrange("p (c n) -> p c n", c=4)[:, :, 0:rows_of(t)]
                                         ).then_inc(s_ea, 1)

                    @block.vector
                    def _(dve):
                        dve.wait_ge(s_squares, tiles)
                        dve.tensor_scalar(ms[:, :], ssq[:, :], 1.0 / D, EPS, ALU.mult, ALU.add).then_inc(s_ms, 1)
                        dve.wait_ge(s_rt, 1)
                        dve_chain.link(dve, dve.reciprocal(rs[:, :], rt[:, :]))
                        dve.wait_ge(s_gain, 16)
                        count = NT if yT is not None else tiles
                        lag = 1 if router is not None else count
                        for i in range(count + lag):
                            if i < count:
                                r = rows_of(i)
                                dve.scalar_tensor_tensor(out=xn[0:r, i, :], in0=h[0:r, i, :], scalar=rs[0:r, i:i + 1],
                                                         in1=gbc[0:r, :], op0=ALU.mult, op1=ALU.mult).then_inc(s_xn, 1)
                            if i >= lag and yT is not None:
                                t = i - lag
                                dve.wait_ge(s_tp, 2 * t + 2)
                                dve.tensor_copy(yT[:, 4:8, time_cols(t)],
                                                ps[:, (2 * t + 1) % 8, :].rearrange("p (c n) -> p c n", c=4)[:, :, 0:rows_of(t)]
                                                ).then_inc(s_ed, 1)
                        if yT is None:
                            dve.wait_ge(s_xn, tiles)

                    @block.tensor
                    def _(pe):
                        if yT is None:
                            return

                        def logits(t):
                            wr, s_loaded, count, s_lg = router
                            if t == 0:
                                pe.wait_ge(s_loaded, count)
                            pe.wait_ge(s_ea, max(t, 1) + 1)
                            pe.wait_ge(s_ed, t + 1)
                            for c in range(KC):
                                last = pe.matmul(ps[0:rows_of(t), LOGIT_BANK, t * NL:(t + 1) * NL], yT[:, c, time_cols(t)],
                                                 wr[:, c, :], start=c == 0, stop=c == KC - 1)
                            if t == NT - 1:
                                last.then_inc(s_lg, 1)

                        for t in range(NT):
                            r = rows_of(t)
                            pe.wait_ge(s_xn, t + 1)
                            xc = xn[0:r, t, :].rearrange("p (q c) -> p c q", c=KC)
                            for half in range(2):
                                if t == 4:
                                    pe.wait_ge(s_ed if half else s_ea, 1)
                                bank = (2 * t + half) % 8
                                for c in range(4):
                                    last = pe.transpose(ps[:, bank, c * P:c * P + r], xc[:, 4 * half + c, :], ident[0:r, 0:r])
                                last.then_inc(s_tp, 1)
                            if router is not None and t >= 2:
                                logits(t - 2)
                        if router is not None:
                            for t in range(NT - 2, NT):
                                logits(t)
            clear(s_gain, s_squares, s_ms, s_rt, s_xn, s_tp, s_ea, s_ed)

        def load_out_weights(sp, wo, w, s_wo):
            for k in range(KC):
                sp.dma_start(wo[:, k, :], w[k * P:(k + 1) * P, :]).then_inc(s_wo, 16)

        def out_phase(tag, chunk, wo, s_wo, cols, tiles, prefetch, scratch):
            s_job, s_add = sem_again("out_product"), sem_again("out_added")
            with nc.Block() as block:
                @block.sync
                def _(sp):
                    prefetch(sp)

                @block.tensor
                def _(pe):
                    pe.wait_ge(s_wo, 16 * KC)
                    for j in range(2 * tiles):
                        t, n = divmod(j, 2)
                        if j >= 8:
                            pe.wait_ge(s_add, j - 7)
                        for k in range(KC):
                            last = pe.matmul(ps[0:rows_of(t), j % 8, :], chunk(k)[:, cols(t)], wo[:, k, n * 512:(n + 1) * 512],
                                             start=k == 0, stop=k == KC - 1)
                        last.then_inc(s_job, 1)

                @block.vector
                def _(dve):
                    for j in range(2 * tiles):
                        t, n = divmod(j, 2)
                        r = rows_of(t)
                        hh = h[0:r, t, n * 512:(n + 1) * 512]
                        dve.wait_ge(s_job, j + 1)
                        dve.tensor_tensor(hh, hh, ps[0:r, j % 8, :], ALU.add).then_inc(s_add, 1)
                    dve.wait_ge(s_add, 2 * tiles)

                squares_behind(block, s_add, tiles, lambda t: scratch)
            clear(s_job, s_add)

        def squares_behind(block, s_add, tiles, scratch):
            @block.scalar
            def _(act):
                for t in range(tiles):
                    act.wait_ge(s_add, 2 * t + 2)
                    if t:
                        act.wait_ge(s_squares, t)
                    square(act, t, scratch(t))

        def expert_weights(L, ring_scope):
            W = [A[n][L].rearrange("g e a b -> (g e) a b") for n in ("moe_w1", "moe_w3", "moe_w2")]
            W1, W3 = (w.rearrange("e (p c) f -> e p c f", c=KC) for w in W[0:2])
            W2 = W[2].rearrange("e (p c) n -> e p c n", c=2)

            def ral(name, shape):
                return ring_scope.enter_context(nc.sbuf_tensor(f"m{L}_{name}", shape, F32, side="right"))

            w1, w3, w2 = ral("w1", [P, RING, KC, HID]), ral("w3", [P, RING, KC, HID]), ral("w2", [P, RING, 2, D])
            s_w13 = [sem_again(f"moe_w13_{r}") for r in range(RING)]
            s_w2 = [sem_again(f"moe_w2_{r}") for r in range(RING)]

            def load_w13(sp, e, r, sm=None):
                sp.dma_start(w1[:, r, :, :], W1[e]).then_inc(sm or s_w13[r], 16)
                sp.dma_start(w3[:, r, :, :], W3[e]).then_inc(sm or s_w13[r], 16)

            def load_w2(sp, e, r, sm=None):
                sp.dma_start(w2[:, r, :, :], W2[e]).then_inc(sm or s_w2[r], 16)

            gbc, scratch = ral("gain", [P, D]), ral("squares", [P, D])

            def prefetch(sp):
                load_gain(sp, gbc, A[f"norm_ffn{L}"])
                for r in range(RING):
                    load_w13(sp, r, r)
                    load_w2(sp, r, r)

            return w1, w3, w2, s_w13, s_w2, load_w13, load_w2, gbc, scratch, prefetch

        def moe_phase(L, weights, ring_scope, tiles, ahead, gain):
            tag = f"m{L}_"

            def sems(*names):
                return [sem_again("moe_" + n) for n in names]

            with ExitStack() as moe:
                al = scope_alloc(moe)
                gate = al(tag + "gate", [P, 2, NT])
                posi = al(tag + "posi", [P, 2, NT], I32)
                xe = al(tag + "extra", [1, NX + 1], I32)
                with ExitStack() as scope:
                    al = scope_alloc(scope)
                    xn = al(tag + "xn", [P, NT, D])
                    yT = al(tag + "yT", [P, KC, T])
                    wr = al(tag + "router_w", [P, KC, NL])
                    s_lg, = sems("logits")
                    norm_phase(f"nrm{2 * L + 1}", weights[-3], xn, yT, tiles, ((wr[:, :, :], A[f"router_w{L}"], s_router),),
                               router=(wr, s_router, 16 * (len(router_loads) + L + 1), s_lg))
                    route_phase(L, tag, sems, al, gate, posi, xe)
                    scatter_phase(tag, xn, posi, tiles)
                expert_phase(tag, sems, weights, xe)
                ring_scope.close()
                gbc = on_right(ahead, tag + "next_gain", [P, D])
                combine_phase(tag, sems, gate, posi, tiles, gbc, gain)
                return gbc

        def route_phase(L, tag, sems, al, gate, posi, xe):
            br, val = router_b[:, L, :], valid[:, L, :]
            xrow = expert_tab[:, NE + 1:NE + 1 + NX]
            Lg = al(tag + "logits", [P, NT, NL])
            m4, oh4, g4, ohv = (al(tag + n, [P, NT, 4]) for n in ("m4", "oh4", "g4", "oh4_valid"))
            el, e2, eq = al(tag + "el", [P, NT, 8]), al(tag + "e2", [P, NT, 8]), al(tag + "eq", [P, NT, 8])
            oh = al(tag + "oh", [P, 2, NT, 8])
            OH = al(tag + "OH", [P, 2, NT, NE])
            M = al(tag + "M", [P, NT, NE])
            pr, pe_ = al(tag + "pr", [P, 2, NT, NE]), al(tag + "pr_expert", [P, 2, NT, NE])
            st = al(tag + "st", [P, 6, NT])
            pair_ = al(tag + "pair_numbers", [P, 7, 2, NT])
            nt, ntb, cnt = al(tag + "nt", [NE, 1]), al(tag + "ntb", [NE, P]), al(tag + "count", [NE, 1])
            bcol, bend, ind, ind2 = al(tag + "bcol", [NE, 1]), al(tag + "bend", [NE, 1]), al(tag + "ind", [NE, NX]), al(tag + "ind2", [NE, NX])
            s_lg, s_ga, s_ex, s_M, s_cum, s_nt, s_base, s_ind, s_xe = sems(
                "logits", "differences", "exps", "choices", "ranks", "tiles", "bases", "extras", "extra_experts")
            col = lambda k: st[:, k, :]
            GM, MM, PG, EE, DN, TMP = range(6)
            num = lambda k: pair_[:, k, :, :]
            TOP, RK, EX, BASE, LT, X, Z = range(7)
            wide = lambda ap, n: ap.unsqueeze(2).to_broadcast([P, NT, n])
            row = lambda ap, n: ap.unsqueeze(1).to_broadcast([P, NT, n])
            NB = (T - 1) // CAP

            with nc.Block() as block:
                @block.tensor
                def _(pe):
                    pe.wait_ge(s_M, 1)
                    for t in range(NT):
                        for k in range(t):
                            pe.matmul(ps[:, 5, t * NE:(t + 1) * NE], ones[:, :], M[:, k, :], start=k == 0, stop=False)
                        pe.matmul(ps[:, 5, t * NE:(t + 1) * NE], later[:, :], M[:, t, :], start=t == 0, stop=True)
                    for k in range(NT):
                        last = pe.matmul(ps[0:NE, 6, 0:1], M[:, k, :], ones[:, 0:1], start=k == 0, stop=k == NT - 1)
                    last.then_inc(s_cum, 1)
                    pe.wait_ge(s_nt, 1)
                    pe.matmul(ps[:, 7, 0:NE], ntb[:, :], expert_tab[:, 0:NE], start=True, stop=True)
                    pe.matmul(ps[0:NE, 7, 64:65], expert_tab[:, 0:NE], nt[:, :], start=True, stop=True).then_inc(s_base, 1)
                    pe.wait_ge(s_ind, 1)
                    pe.matmul(ps[0:1, 6, 0:1], ones[0:NE, 0:1], nt[:, :], start=True, stop=True)
                    pe.matmul(ps[0:1, 6, 1:NX + 1], expert_tab[:, NE:NE + 1], ind2[:, :], start=True, stop=True).then_inc(s_xe, 1)

                @block.scalar
                def _(act):
                    act.wait_ge(s_ga, 1)
                    act.activation(g4[:, :, :], m4[:, :, :], ACT.Exp).then_inc(s_ex, 1)
                    act.wait_ge(s_ga, 2)
                    act.activation(col(EE), col(TMP), ACT.Exp).then_inc(s_ex, 1)

                @block.vector
                def _(dve):
                    def do(ins):
                        dve_chain.link(dve, ins)

                    def tt(out, a, b, op):
                        do(dve.tensor_tensor(out, a, b, op))

                    def reduce(out, a, op):
                        do(dve.tensor_reduce(out, a, AX.X, op))

                    def both(*ins):
                        for i in ins:
                            i.then_inc(dve_chain.sem, 1)
                        dve_chain.n += len(ins)
                        dve.wait_ge(dve_chain.sem, dve_chain.n)

                    do(dve.memset(Lg[:, NT - 1, :], 0.0))
                    dve.wait_ge(s_router, 16 * (len(router_loads) + L + 1))
                    dve.wait_ge(s_lg, 1)
                    logits = ps[:, LOGIT_BANK, 0:NT * NL].rearrange("p (t n) -> p t n", t=NT)
                    both(dve.tensor_tensor(Lg[:, 0:NT - 1, :], logits[:, 0:NT - 1, :],
                                           br.unsqueeze(1).to_broadcast([P, NT - 1, NL]), ALU.add),
                         dve.tensor_tensor(Lg[0:META, NT - 1, :], logits[0:META, NT - 1, :], br[0:META, :], ALU.add))
                    G = Lg[:, :, 0:4]
                    reduce(col(GM), G, ALU.max)
                    dve.tensor_tensor(m4[:, :, :], G, wide(col(GM), 4), ALU.subtract).then_inc(s_ga, 1)
                    tt(oh4[:, :, :], G, wide(col(GM), 4), ALU.is_equal)
                    tt(oh4[:, :, :], oh4[:, :, :], row(first[:, 0:4], 4), ALU.mult)
                    reduce(col(MM), oh4[:, :, :], ALU.max)
                    tt(oh4[:, :, :], oh4[:, :, :], wide(col(MM), 4), ALU.is_equal)
                    by_group = lambda ap: ap.rearrange("p t (g e) -> p t g e", g=GROUPS)
                    each = lambda ap: ap.unsqueeze(3).to_broadcast([P, NT, GROUPS, EXPERTS])
                    both(dve.tensor_tensor(by_group(M[:, :, :]), by_group(Lg[:, :, GROUPS:NL]), each(oh4[:, :, :]), ALU.mult),
                         dve.tensor_tensor(ohv[:, :, :], oh4[:, :, :], wide(val, 4), ALU.mult))
                    reduce(el[:, :, :], M[:, :, :].rearrange("p t (g e) -> p t e g", g=GROUPS), ALU.add)
                    src = el
                    for k in range(2):
                        top_k = pair_[:, TOP, k, :]
                        reduce(top_k, src[:, :, :], ALU.max)
                        tt(eq[:, :, :], src[:, :, :], wide(top_k, 8), ALU.is_equal)
                        tt(eq[:, :, :], eq[:, :, :], row(first[:, 4:12], 8), ALU.mult)
                        reduce(col(MM), eq[:, :, :], ALU.max)
                        tt(oh[:, k, :, :], eq[:, :, :], wide(col(MM), 8), ALU.is_equal)
                        if k == 0:
                            do(dve.scalar_tensor_tensor(out=e2[:, :, :], in0=oh[:, 0, :, :], scalar=NEG, in1=el[:, :, :],
                                                        op0=ALU.mult, op1=ALU.add))
                            src = e2
                    dve.tensor_tensor(col(TMP), pair_[:, TOP, 1, :], pair_[:, TOP, 0, :], ALU.subtract).then_inc(s_ga, 1)
                    both(*(dve.tensor_tensor(by_group(OH[:, k, :, :]), oh[:, k, :, :].unsqueeze(2).to_broadcast([P, NT, GROUPS, EXPERTS]),
                                             each(ohv[:, :, :]), ALU.mult) for k in range(2)))
                    dve.tensor_tensor(M[:, :, :], OH[:, 0, :, :], OH[:, 1, :, :], ALU.add).then_inc(s_M, 1)
                    two = lambda ap: ap.unsqueeze(1).to_broadcast([P, 2, NT, NE])
                    do(dve.tensor_tensor(pe_[:, :, :, :].rearrange("p k t e -> p (k t) e"), OH[:, :, :, :].rearrange("p k t e -> p (k t) e"),
                                         first[:, 12:12 + NE].unsqueeze(1).to_broadcast([P, 2 * NT, NE]), ALU.mult))
                    reduce(num(EX), pe_[:, :, :, :], ALU.add)
                    dve.wait_ge(s_ex, 2)
                    both(dve.tensor_reduce(col(PG), g4[:, :, :], AX.X, ALU.add),
                         dve.tensor_scalar(num(EX), num(EX), float(CAP), float(-(NE - 1) * CAP), ALU.mult, ALU.add))
                    do(dve.scalar_tensor_tensor(out=col(DN), in0=col(EE), scalar=1.0, in1=col(PG), op0=ALU.add, op1=ALU.mult))
                    dve.wait_ge(s_cum, 1)
                    both(dve.tensor_scalar(cnt[:, :], ps[0:NE, 6, 0:1], 1.0 / CAP, -1.0, ALU.mult, ALU.add),
                         dve.tensor_tensor(pr[:, :, :, :], OH[:, :, :, :], two(ps[:, 5, 0:NT * NE].rearrange("p (a b) -> p a b", a=NT)),
                                           ALU.mult))
                    do(dve.tensor_scalar(ind[:, 0:NB], xrow[:, 0:NB], cnt[:, 0:1], None, ALU.is_lt))
                    reduce(nt[:, :], ind[:, 0:NB], ALU.add)
                    dve.tensor_scalar(ntb[:, :], ones[0:NE, :], nt[:, 0:1], None, ALU.mult).then_inc(s_nt, 1)
                    both(dve.tensor_reduce(num(RK), pr[:, :, :, :], AX.X, ALU.add),
                         dve.reciprocal(gate[:, 0, :], col(DN)))
                    both(dve.tensor_scalar(num(LT), num(RK), float(CAP), None, ALU.is_lt),
                         dve.tensor_scalar(num(RK), num(RK), float((NE - 1) * CAP), None, ALU.add),
                         dve.tensor_tensor(gate[:, 1, :], gate[:, 0, :], col(EE), ALU.mult))
                    dve.wait_ge(s_base, 1)
                    both(dve.tensor_scalar(bcol[:, :], ps[0:NE, 7, 64:65], 0.0, None, ALU.add),
                         dve.tensor_tensor(pr[:, :, :, :].rearrange("p k t e -> p (k t) e"), OH[:, :, :, :].rearrange("p k t e -> p (k t) e"),
                                           ps[:, 7, 0:NE].unsqueeze(1).to_broadcast([P, 2 * NT, NE]), ALU.mult))
                    both(dve.tensor_tensor(bend[:, :], bcol[:, :], nt[:, :], ALU.add),
                         dve.tensor_scalar(ind[:, :], xrow[:, :], bcol[:, 0:1], None, ALU.is_ge),
                         dve.tensor_reduce(num(BASE), pr[:, :, :, :], AX.X, ALU.add))
                    dve.scalar_tensor_tensor(out=ind2[:, :], in0=xrow[:, :], scalar=bend[:, 0:1], in1=ind[:, :],
                                             op0=ALU.is_lt, op1=ALU.mult).then_inc(s_ind, 1)
                    both(dve.scalar_tensor_tensor(out=num(X), in0=num(BASE), scalar=float(-CAP), in1=num(EX), op0=ALU.mult, op1=ALU.add),
                         dve.scalar_tensor_tensor(out=num(Z), in0=num(BASE), scalar=float(CAP), in1=num(RK), op0=ALU.mult, op1=ALU.add))
                    tt(num(X), num(X), num(LT), ALU.mult)
                    tt(num(X), num(X), num(Z), ALU.add)
                    do(dve.tensor_copy(posi[:, :, :], num(X)))
                    dve.wait_ge(s_xe, 1)
                    do(dve.tensor_copy(xe[:, :], ps[0:1, 6, 0:NX + 1]))
            clear(s_lg, s_ga, s_ex, s_M, s_cum, s_nt, s_base, s_ind, s_xe)

        def scatter_phase(tag, xn, posi, tiles):
            s_sc = sem(tag + "rows_scattered")
            with nc.Block() as block:
                @block.gpsimd
                def _(pool):
                    for t in range(tiles):
                        for k in range(2):
                            r = rows_of(t)
                            pool.indirect_dma_start(xs[:, :], bass.IndirectOffsetOnAxis(posi[0:r, k, t:t + 1], 0),
                                                    xn[0:r, t, :], None).then_inc(s_sc, 16)
                    pool.wait_ge(s_sc, 2 * tiles * 16)

        def expert_phase(tag, sems, weights, xe):
            w1, w3, w2, s_w13, s_w2, load_w13, load_w2 = weights[0:7]
            with ExitStack() as scope:
                al = scope_alloc(scope)
                xg = al(tag + "xg", [CAP, RING, D])
                xgT = al(tag + "xgT", [P, KC, CAP])
                sg, hd = al(tag + "sg", [P, HID]), al(tag + "hd", [CAP, HID])
                hT = al(tag + "hT", [P, 2, CAP])
                yb = al(tag + "yb", [P, 2, D // 2])
                s_x = sems(*(f"x_{r}" for r in range(RING)))
                s_yo = sems("y_out_0", "y_out_1")
                s_tx, s_txc, s_ab, s_sg, s_hd, s_th, s_thc, s_y, s_yd = sems(
                    "x_turned", "xT_copied", "hidden_products", "silu_done", "hidden_ready", "hidden_turned", "hT_copied",
                    "y_product", "y_copied")
                s_ew, s_ex, s_eo = sems("extra_weights", "extra_x", "extra_y_out")
                s_turning, = sems("turning")
                C, UP = slice(0, CAP), slice(CAP, 2 * CAP)
                Q = NE // RING

                def turn_x(pe, r, value, sm=None):
                    pe.wait_ge(sm or s_x[r], value)
                    pe.sem_inc(s_turning, 1)
                    xc = xg[:, r, :].rearrange("p (q c) -> p c q", c=KC)
                    for c in range(KC):
                        last = pe.transpose(ps[:, 0, c * CAP:(c + 1) * CAP], xc[:, c, :], ident[C, C])
                    last.then_inc(s_tx, 1)

                def hidden(pe, r, bank):
                    for c in range(KC):
                        pe.matmul(ps[C, bank, 0:HID], xgT[:, c, :], w1[:, r, c, :], start=c == 0, stop=c == KC - 1)
                        last = pe.matmul(ps[UP, bank, 0:HID], xgT[:, c, :], w3[:, r, c, :], start=c == 0, stop=c == KC - 1)
                    last.then_inc(s_ab, 1)

                def turn_hidden(pe, value):
                    pe.wait_ge(s_hd, value)
                    pe.sem_inc(s_turning, 1)
                    hc = hd[:, :].rearrange("p (q c) -> p c q", c=2)
                    for c in range(2):
                        last = pe.transpose(ps[:, 1, c * CAP:(c + 1) * CAP], hc[:, c, :], ident[C, C])
                    last.then_inc(s_th, 1)

                def output(pe, r):
                    for c in range(2):
                        pe.matmul(ps[C, 5, :], hT[:, c, :], w2[:, r, c, 0:512], start=c == 0, stop=c == 1)
                        last = pe.matmul(ps[UP, 5, :], hT[:, c, :], w2[:, r, c, 512:D], start=c == 0, stop=c == 1)
                    last.then_inc(s_y, 1)

                def pe_step(pe, e, q, r, last=False):
                    pe.wait_ge(s_txc, e + 1)
                    pe.wait_ge(s_w13[r], 32 * (q + 1))
                    hidden(pe, r, 2 + r % 2)
                    turn_hidden(pe, e)
                    if not last:
                        n = (r + 1) % RING
                        turn_x(pe, n, 16 * (q + (2 if n == 0 else 1)))
                    pe_output(pe, e, q if r else q - 1, (r - 1) % RING)

                def pe_output(pe, e, q, r):
                    pe.wait_ge(s_thc, e)
                    pe.wait_ge(s_w2[r], 16 * (q + 1))
                    pe.wait_ge(s_yd, e)
                    output(pe, r)

                def copy_xT(act, e):
                    act.wait_ge(s_tx, e + 1)
                    act.copy(xgT[:, :, :].rearrange("p c n -> p (c n)"), ps[:, 0, :]).then_inc(s_txc, 1)

                def silu(act, e, bank):
                    act.wait_ge(s_ab, e + 1)
                    act.activation(sg[UP, :], ps[C, bank, 0:HID], ACT.Silu).then_inc(s_sg, 1)

                def store_y(act, e, u, sm):
                    act.wait_ge(s_yd, e + 2)
                    for n, part in enumerate((C, UP)):
                        act.dma_start(slot_rows(ys, e)[:, n * 512:(n + 1) * 512], yb[part, u, :]).then_inc(sm, 16)

                def hide(dve, e, bank):
                    dve.wait_ge(s_sg, e + 1)
                    dve.tensor_tensor(hd[:, :], sg[UP, :], ps[UP, bank, 0:HID], ALU.mult).then_inc(s_hd, 1)

                def copy_hT(dve, e):
                    dve.wait_ge(s_th, e + 1)
                    dve.tensor_copy(hT[:, :, :].rearrange("p a b -> p (a b)"), ps[:, 1, 0:2 * CAP]).then_inc(s_thc, 1)

                def copy_y(dve, e, u):
                    dve.wait_ge(s_y, e + 1)
                    dve.tensor_copy(yb[:, u, :], ps[:, 5, :]).then_inc(s_yd, 1)

                def slot_rows(buf, e):
                    return buf[bass.ds(e * CAP, CAP), :]

                with nc.Block() as block:
                    @block.sync
                    def _(sp):
                        def load_x(e, r, sm):
                            sp.dma_start(xg[:, r, :], slot_rows(xs, e)).then_inc(sm, 16)

                        def load_tile(tile, e, r, sm, before):
                            sp.wait_ge(s_tx, before + 1)
                            load_x(tile, r, sm)
                            sp.wait_ge(s_ab, before + 1)
                            load_w13(sp, e, r)
                            sp.wait_ge(s_y, before + 1)
                            load_w2(sp, e, r)

                        for r in range(RING):
                            load_x(r, r, s_x[r])
                        with sp.Fori(0, Q - 1) as i:
                            for r in range(RING):
                                e = RING * i + RING + r
                                load_tile(e, e, r, s_x[r], RING * i + r)
                        for e in range(RING * Q, NE):
                            load_tile(e, e, e % RING, s_x[e % RING], e - RING)
                        n_extra = sp.value_load(xe[0:1, 0:1], min_val=0, max_val=NX)
                        for j in range(AROUND):
                            with sp.If(n_extra > j):
                                e = sp.value_load(xe[0:1, j + 1:j + 2], min_val=0, max_val=NE - 1)
                                r = (NE + j) % RING
                                load_tile(NE + j, e, r, s_x[r], NE + j - RING)
                        with sp.If(n_extra > AROUND):
                            with sp.Fori(AROUND, n_extra) as j:
                                sp.wait_ge(s_y, NE + j)
                                e = sp.value_load(xe[0:1, bass.ds(j + 1, 1)], min_val=0, max_val=NE - 1)
                                load_x(NE + j, 0, s_ex)
                                load_w13(sp, e, 0, s_ew)
                                load_w2(sp, e, 0, s_ew)

                    @block.tensor
                    def _(pe):
                        turn_x(pe, 0, 16)
                        pe.wait_ge(s_txc, 1)
                        pe.wait_ge(s_w13[0], 32)
                        hidden(pe, 0, 2)
                        turn_x(pe, 1, 16)
                        with pe.Fori(0, Q - 1) as i:
                            for k in range(RING):
                                r = (k + 1) % RING
                                pe_step(pe, RING * i + k + 1, i + (k + 1) // RING, r)
                        for e in range(RING * (Q - 1) + 1, NE):
                            pe_step(pe, e, e // RING, e % RING, last=e == NE - 1)
                        turn_hidden(pe, NE)
                        pe_output(pe, NE, (NE - 1) // RING, (NE - 1) % RING)
                        n_extra = pe.value_load(xe[0:1, 0:1], min_val=0, max_val=NX)
                        for j in range(AROUND):
                            with pe.If(n_extra > j):
                                q, r = divmod(NE + j, RING)
                                turn_x(pe, r, 16 * (q + 1))
                                pe.wait_ge(s_txc, NE + j + 1)
                                pe.wait_ge(s_w13[r], 32 * (q + 1))
                                hidden(pe, r, 2)
                                turn_hidden(pe, NE + j + 1)
                                pe_output(pe, NE + j + 1, q, r)
                        with pe.If(n_extra > AROUND):
                            with pe.Fori(AROUND, n_extra) as j:
                                turn_x(pe, 0, 16 * (j - (AROUND - 1)), s_ex)
                                pe.wait_ge(s_txc, NE + j + 1)
                                pe.wait_ge(s_ew, 48 * (j - (AROUND - 1)))
                                hidden(pe, 0, 2)
                                turn_hidden(pe, NE + j + 1)
                                pe.wait_ge(s_thc, NE + j + 1)
                                pe.wait_ge(s_yd, NE + j + 1)
                                output(pe, 0)

                    @block.scalar
                    def _(act):
                        def act_step(e, r, last=False):
                            act.wait_ge(s_hd, e)
                            silu(act, e, 2 + r % 2)
                            if not last:
                                copy_xT(act, e + 1)
                            store_y(act, e - 1, (r - 1) % 2, s_yo[(r - 1) % 2])

                        copy_xT(act, 0)
                        silu(act, 0, 2)
                        copy_xT(act, 1)
                        with act.Fori(0, Q - 1) as i:
                            for k in range(RING):
                                act_step(RING * i + k + 1, (k + 1) % RING)
                        for e in range(RING * (Q - 1) + 1, NE):
                            act_step(e, e % RING, last=e == NE - 1)
                        store_y(act, NE - 1, 1, s_yo[1])
                        n_extra = act.value_load(xe[0:1, 0:1], min_val=0, max_val=NX)
                        for j in range(AROUND):
                            with act.If(n_extra > j):
                                copy_xT(act, NE + j)
                                act.wait_ge(s_hd, NE + j)
                                silu(act, NE + j, 2)
                                store_y(act, NE + j, j % 2, s_yo[j % 2])
                        for u in range(2):
                            act.wait_ge(s_yo[u], 16 + 32 * (NE // 2))
                        for j in range(AROUND):
                            with act.If(n_extra > j):
                                act.wait_ge(s_yo[j % 2], 16 + 32 * ((NE + j) // 2 + 1))
                        with act.If(n_extra > AROUND):
                            with act.Fori(AROUND, n_extra) as j:
                                copy_xT(act, NE + j)
                                act.wait_ge(s_hd, NE + j)
                                silu(act, NE + j, 2)
                                store_y(act, NE + j, 0, s_eo)
                                act.wait_ge(s_eo, 32 * (j - (AROUND - 1)))

                    @block.vector
                    def _(dve):
                        dve.sem_inc(s_yd, 1)
                        for u in range(2):
                            dve.sem_inc(s_yo[u], 16)

                        hide(dve, 0, 2)
                        with dve.Fori(0, Q - 1) as i:
                            for k in range(RING):
                                e = RING * i + k + 1
                                copy_hT(dve, e - 1)
                                hide(dve, e, 2 + (k + 1) % 2)
                                dve.wait_ge(s_yo[k % 2], 16 + 32 * (RING // 2 * i + k // 2))
                                copy_y(dve, e - 1, k % 2)
                        for e in range(RING * (Q - 1) + 1, NE + 1):
                            copy_hT(dve, e - 1)
                            if e < NE:
                                hide(dve, e, 2 + e % 2)
                            dve.wait_ge(s_yo[(e - 1) % 2], 16 + 32 * ((e - 1) // 2))
                            copy_y(dve, e - 1, (e - 1) % 2)
                        n_extra = dve.value_load(xe[0:1, 0:1], min_val=0, max_val=NX)
                        for j in range(AROUND):
                            with dve.If(n_extra > j):
                                hide(dve, NE + j, 2)
                                copy_hT(dve, NE + j)
                                dve.wait_ge(s_yo[j % 2], 16 + 32 * ((NE + j) // 2))
                                copy_y(dve, NE + j, j % 2)
                        with dve.If(n_extra > AROUND):
                            with dve.Fori(AROUND, n_extra) as j:
                                hide(dve, NE + j, 2)
                                copy_hT(dve, NE + j)
                                copy_y(dve, NE + j, 0)
            clear(*s_w13, *s_w2, *s_x, *s_yo, s_tx, s_txc, s_ab, s_sg, s_hd, s_th, s_thc, s_y, s_yd, s_ew, s_ex, s_eo,
                  s_turning)

        def combine_phase(tag, sems, gate, posi, tiles, gbc, gain):
            with ExitStack() as scope:
                yg = scope_alloc(scope)(tag + "yg", [P, 2 * tiles, D])
                s_add, = sems("rows_added")
                s_g = [sem(f"{tag}gather{n}") for n in range(2 * tiles)]
                with nc.Block() as block:
                    @block.sync
                    def _(sp):
                        load_gain(sp, gbc, gain)

                    @block.gpsimd
                    def _(pool):
                        for n in range(2 * tiles):
                            t, k = divmod(n, 2)
                            r = rows_of(t)
                            pool.indirect_dma_start(yg[0:r, n, :], None, ys[:, :],
                                                    bass.IndirectOffsetOnAxis(posi[0:r, k, t:t + 1], 0)).then_inc(s_g[n], 16)

                    @block.vector
                    def _(dve):
                        for n in range(2 * tiles):
                            t, k = divmod(n, 2)
                            r = rows_of(t)
                            dve.wait_ge(s_g[n], 16)
                            dve.scalar_tensor_tensor(out=h[0:r, t, :], in0=yg[0:r, n, :], scalar=gate[0:r, k, t:t + 1],
                                                     in1=h[0:r, t, :], op0=ALU.mult, op1=ALU.add).then_inc(s_add, 1)
                            dve.wait_ge(s_add, n + 1)

                    squares_behind(block, s_add, tiles, lambda t: yg[:, 2 * t, :])
            clear(s_add)

        with ExitStack() as last:
          al = scope_alloc(last)
          mT = al("mT", [P, KC, T])
          with ExitStack() as attn:
            qkT = al("qkT", [P, 2 * HEADS, T])
            qT, kT = qkT[:, 0:HEADS, :], qkT[:, HEADS:2 * HEADS, :]
            al = scope_alloc(attn)
            Vm = al("Vm", [P, NT, HEADS * VD])
            nqT = al("nqT", [P, HEADS, T])
            nkT = al("nkT", [P, 4, T])
            Vn = al("Vn", [P, NT, HEADS * VD])

            with ExitStack() as scope:
                al = scope_alloc(scope)
                yT = al("yT_a", [P, KC, T])
                R = 4
                s_w = [sem_again(f"projection_w{j}_loaded") for j in range(R)]
                wr = al("a1_w", [P, R, KC, P])
                with ExitStack() as s2:
                    xn = scope_alloc(s2)("xn_a", [P, NT, D])
                    norm_phase("nrm0", gain0, xn, yT, also=[(wr[:, j, :, :], A["wa"][j], s_w[j]) for j in range(R)])
                first_norm.close()

                cT = al("cT", [P, 3, T])
                kpe = al("kpe", [P, 2, T])
                NJ = 13
                dests = [cT[:, j, :] for j in range(3)] + [kpe[:, j, :] for j in range(2)] \
                    + [None] * 4 + [nkT[:, j, :] for j in range(4)]
                s_zero = sem("a1_padding_zero")
                s_wnv, s_job, s_ea, s_ed = sem("a1_wnv_loaded"), sem("a1_product"), sem("a1_act_copied"), sem("a1_dve_copied")
                wuq = al("wuq", [P, 2, HEADS * QK])
                wsw = al("wsw", [P, 2, HEADS * ROPE])
                wkn = al("wkn", [P, HEADS * NOPE])
                wv = al("wv", [P, HEADS * VD])
                gl = al("gl", [P, 3])
                rc = al("rope_cos", [P, T])
                rsn = al("rope_sin", [P, T])
                a2_loads = ((wuq[:, :, :], "wuq"), (wsw[:, :, :], "wsw"), (wkn[:, :], "wkn"), (wv[:, :], "wv"),
                            (gl[:, :], "gl"), (rc[:, :], "rope_cos"), (rsn[:, :], "rope_sin"))
                s_ld, s_sq, s_sum, s_ms, s_rt, s_cn, s_kr, s_kc = (sem(f"a2_{n}") for n in (
                    "weights_loaded", "squares", "sums", "means", "roots", "latents_normed", "key_rotated", "key_copied"))
                with ExitStack() as s2:
                    al2 = scope_alloc(s2)
                    sq = al2("lat_sq", [P, 3, T])
                    mr = al2("lat_ms", [P, 2, T])
                    kr = al2("kr", [P, T])
                    wnv = al2("a1_wnv", [P, KC, 512])
                    with nc.Block() as block:
                        @block.sync
                        def _(sp):
                            for j in range(NJ):
                                if j >= R:
                                    sp.wait_ge(s_job, j - R + 1)
                                    sp.dma_start(wr[:, j % R, :, :], A["wa"][j]).then_inc(s_w[j % R], 16)
                                if j == R - 1:
                                    for dst, name in a2_loads:
                                        sp.dma_start(dst, A[name]).then_inc(s_ld, 16)
                                    sp.dma_start(wnv[:, :, :], A["wnv"]).then_inc(s_wnv, 16)

                        @block.tensor
                        def _(pe):
                            for j in range(NJ + NT):
                                s = j % 4
                                if j >= 4:
                                    pe.wait_ge(s_ed if j % 2 else s_ea, (j - 4) // 2 + 1)
                                if j == 5:
                                    pe.wait_ge(s_ea, 2)
                                    pe.wait_ge(s_ed, 2)
                                    pe.wait_ge(s_sq, 1)
                                    for a, chunks in enumerate(((0, 1), (2,))):
                                        for n in range(2):
                                            for c in chunks:
                                                last = pe.matmul(ps[:, 4 + 2 * a + n, 0:HT], ones[:, :], sq[:, c, n * HT:(n + 1) * HT],
                                                                 start=c == chunks[0], stop=c == chunks[-1])
                                        last.then_inc(s_sum, 1)
                                elif j in (6, 7):
                                    pe.wait_ge(s_ms, j - 5)
                                if j < NJ:
                                    pe.wait_ge(s_w[j % R], 16 * (j // R + 1))
                                    for n in range(2):
                                        for c in range(KC):
                                            last = pe.matmul(ps[:, 2 * s + n, 0:HT], wr[:, j % R, c, :],
                                                             yT[:, c, n * HT:(n + 1) * HT], start=c == 0, stop=c == KC - 1)
                                else:
                                    t = j - NJ
                                    pe.wait_ge(s_wnv, 16)
                                    for c in range(KC):
                                        last = pe.matmul(ps[0:rows_of(t), 2 * s, :], yT[:, c, time_cols(t)],
                                                         wnv[:, c, :], start=c == 0, stop=c == KC - 1)
                                last.then_inc(s_job, 1)

                        def copy_out(j, eng, copy, done):
                            eng.wait_ge(s_job, j + 1)
                            if j < NJ and dests[j] is None:
                                for i in range(2):
                                    rr, g = slice(64 * i, 64 * i + 64), 2 * (j - 5) + i
                                    last = copy(halves(nqT[rr, g, :]), pair(j % 4, rr))
                                last.then_inc(done, 1)
                            elif j < NJ:
                                copy(halves(dests[j]), pair(j % 4)).then_inc(done, 1)
                            else:
                                r = rows_of(j - NJ)
                                copy(Vn[0:r, j - NJ, :], ps[0:r, 2 * (j % 4), :]).then_inc(done, 1)

                        @block.gpsimd
                        def _(pool):
                            for part in (nqT[:, :, :], Vn[:, NT - 1, :], Vm[:, NT - 1, :]):
                                pool.memset(part, 0.0).then_inc(s_zero, 1)
                            pool.wait_ge(s_zero, 3)
                            pool.wait_ge(s_kr, 1)
                            for g in range(HEADS):
                                pool.tensor_copy(kT[NOPE:QK, g, :], kr[NOPE:QK, :]).then_inc(s_kc, 1)
                            pool.wait_ge(s_kc, HEADS)

                        @block.scalar
                        def _(act):
                            act.wait_ge(s_zero, 3)
                            for j in range(0, NJ + NT, 2):
                                copy_out(j, act, act.copy, s_ea)
                                if j == 4:
                                    act.wait_ge(s_ms, 2)
                                    act.activation(sq[:, 0:2, :], mr[:, :, :], ACT.Sqrt).then_inc(s_rt, 1)

                        @block.vector
                        def _(dve):
                            dve.wait_ge(s_zero, 3)
                            for j in range(1, NJ + NT, 2):
                                copy_out(j, dve, dve.tensor_copy, s_ed)
                                if j == 1:
                                    dve.wait_ge(s_ea, 2)
                                    dve.wait_ge(s_ed, 1)
                                    dve.tensor_tensor(sq[:, :, :], cT[:, :, :], cT[:, :, :], ALU.mult).then_inc(s_sq, 1)
                                elif j == 3:
                                    dve.wait_ge(s_sum, 1)
                                    dve.tensor_scalar(halves(mr[:, 0, :]), pair(2), 1.0 / QR, EPS, ALU.mult, ALU.add).then_inc(s_ms, 1)
                                    dve.wait_ge(s_sum, 2)
                                    dve.tensor_scalar(halves(mr[:, 1, :]), pair(3), 1.0 / KVR, EPS, ALU.mult, ALU.add).then_inc(s_ms, 1)
                                    dve.wait_ge(s_rt, 1)
                                    dve_chain.link(dve, dve.reciprocal(mr[:, :, :], sq[:, 0:2, :]))
                                    dve.wait_ge(s_ld, 16 * len(a2_loads))
                                    for i in range(3):
                                        dve.scalar_tensor_tensor(out=cT[:, i, :], in0=cT[:, i, :], scalar=gl[:, i:i + 1],
                                                                 in1=mr[:, i // 2, :], op0=ALU.mult, op1=ALU.mult).then_inc(s_cn, 1)
                                elif j == 5:
                                    dve.wait_ge(s_ed, 2)
                                    dve_chain.link(dve, dve.tensor_tensor(kpe[:, 0, :], kpe[:, 0, :], rc[:, :], ALU.mult))
                                    dve_chain.link(dve, dve.tensor_tensor(kpe[:, 1, :], kpe[:, 1, :], rsn[:, :], ALU.mult))
                                    dve.tensor_tensor(kr[:, :], kpe[:, 0, :], kpe[:, 1, :], ALU.add).then_inc(s_kr, 1)
                            dve.wait_ge(s_cn, 3)

                clear(*s_w)

                with ExitStack() as s2:
                    al2 = scope_alloc(s2)
                    ra = al2("rope_a", [P, 2, T])
                    rb = al2("rope_b", [P, 2, T])
                    s_q, s_qa, s_qd, s_k, s_ka = (sem(f"a2_{n}") for n in (
                        "q_product", "q_act_copied", "q_rotated", "kv_product", "kv_copied"))
                    with nc.Block() as block:
                        @block.vector
                        def _(dve):
                            R6 = slice(NOPE, QK)
                            for g in range(HEADS):
                                s = 2 * (g % 2)
                                dve.wait_ge(s_q, g + 1)
                                a, b = ra[R6, g % 2, :], rb[R6, g % 2, :]
                                dve.tensor_tensor(halves(a), pair(s, R6), halves(rc[R6, :]), ALU.mult).then_inc(dve_chain.sem, 1)
                                dve_chain.n += 1
                                dve_chain.link(dve, dve.tensor_tensor(halves(b), pair(s + 1, R6), halves(rsn[R6, :]), ALU.mult))
                                dve.tensor_tensor(qT[R6, g, :], a, b, ALU.add).then_inc(s_qd, 1)
                            dve.wait_ge(s_qd, HEADS)

                        @block.tensor
                        def _(pe):
                            for g in range(HEADS):
                                s = 2 * (g % 2)
                                if g >= 2:
                                    pe.wait_ge(s_qa, g - 1)
                                    pe.wait_ge(s_qd, g - 1)
                                for n in range(2):
                                    for j in range(2):
                                        pe.matmul(ps[0:QK, 2 * s + n, 0:HT], wuq[:, j, g * QK:(g + 1) * QK],
                                                  cT[:, j, n * HT:(n + 1) * HT], start=j == 0, stop=j == 1)
                                    for j in range(2):
                                        last = pe.matmul(ps[NOPE:QK, 2 * s + 2 + n, 0:HT], wsw[:, j, g * ROPE:(g + 1) * ROPE],
                                                         cT[:, j, n * HT:(n + 1) * HT], start=j == 0, stop=j == 1)
                                last.then_inc(s_q, 1)
                            pe.wait_ge(s_qa, HEADS)
                            pe.wait_ge(s_qd, HEADS)
                            for g in range(HEADS + NT):
                                s = g % 4
                                if g >= 4:
                                    pe.wait_ge(s_ka, g - 3)
                                if g < HEADS:
                                    for n in range(2):
                                        last = pe.matmul(ps[0:NOPE, 2 * s + n, 0:HT], wkn[:, g * NOPE:(g + 1) * NOPE],
                                                         cT[:, 2, n * HT:(n + 1) * HT], start=True, stop=True)
                                else:
                                    t = g - HEADS
                                    last = pe.matmul(ps[0:rows_of(t), 2 * s, :], cT[:, 2, time_cols(t)], wv[:, :],
                                                     start=True, stop=True)
                                last.then_inc(s_k, 1)

                        @block.scalar
                        def _(act):
                            for g in range(HEADS):
                                act.wait_ge(s_q, g + 1)
                                act.copy(halves(qT[0:NOPE, g, :]), pair(2 * (g % 2), slice(0, NOPE))).then_inc(s_qa, 1)
                            for g in range(HEADS + NT):
                                act.wait_ge(s_k, g + 1)
                                if g < HEADS:
                                    act.copy(halves(kT[0:NOPE, g, :]), pair(g % 4, slice(0, NOPE))).then_inc(s_ka, 1)
                                else:
                                    t = g - HEADS
                                    act.copy(Vm[0:rows_of(t), t, :], ps[0:rows_of(t), 2 * (g % 4), :]).then_inc(s_ka, 1)

            wo = qkT[:, :, :].rearrange("p a b -> p (a b)")[:, 0:KC * D].rearrange("p (k n) -> p k n", k=KC)
            s_wo = sem("a4_w_loaded")
            with ExitStack() as scope:
                al = scope_alloc(scope)
                Pb = al("Pb", [P, 2, NT, T])
                PT = al("PT", [P, 3, NT, T])
                dg = al("diagonals", [P, 10, P])
                tb = al("tb", [P, HEADS, 14, GRID_W])
                mk = al("mk", [P, GRID_W])
                mx, ng, sm, rc = (al(f"at_{n}", [P, 10]) for n in ("mx", "ng", "sm", "rc"))
                s_tb, s_bias, s_sc, s_ng, s_ex, s_rc, s_dg, s_tr, s_te, s_pv, s_me = (sem(f"at_{n}") for n in (
                    "table_loaded", "bias_ready", "scores", "max_ready", "exps", "reciprocal", "diagonal",
                    "turned", "turned_copied", "pv", "merged"))
                s_cl, s_pad = sem("at_meta_cleared"), sem("at_padding_zero")
                NH = 2 * HEADS
                STEPS = NT * NH
                LAG, PVLAG = 6, 7
                MLA_SCALE, NAT_SCALE = QK ** -0.5, NOPE ** -0.5

                def prob(n):
                    g, t = divmod(n, NT)
                    return Pb[0:rows_of(t), g % 2, t, :]

                def copy_turned(eng, copy, m):
                    g, kc = divmod(m, NT)
                    if m % (NT * HEADS) == 0:
                        eng.wait_ge(s_pad, 3)
                    if kc == 0 and g >= 3:
                        eng.wait_ge(s_pv, (g - 3) // 2 + 1)
                    eng.wait_ge(s_tr, m + 1)
                    k = rows_of(kc)
                    copy(PT[0:k, g % 3, kc, :], flat[0:k, 4 * 512:4 * 512 + T]).then_inc(s_te, 1)

                with nc.Block() as block:
                    @block.sync
                    def _(sp):
                        sp.dma_start(tb[:, :, :, :], A["nat_table"]).then_inc(s_tb, 16)
                        sp.dma_start(mk[:, :], A["nat_mask"]).then_inc(s_tb, 16)
                        sp.wait_ge(s_sc, HEADS * NT)
                        load_out_weights(sp, wo, A["a_w_out"], s_wo)
                        clear_slots(sp)

                    @block.tensor
                    def _(pe):
                        for n in range(STEPS + PVLAG + NT):
                            if n < STEPS:
                                g, t = divmod(n, NT)
                                s, r = n % 2, rows_of(t)
                                if n >= 2:
                                    pe.wait_ge(s_ex, n - 1)
                                if g < HEADS:
                                    for k in range(2):
                                        last = pe.matmul(ps[0:r, 2 * s + k, 0:HT], qT[0:QK, g, time_cols(t)],
                                                         kT[0:QK, g, k * HT:(k + 1) * HT], start=True, stop=True)
                                else:
                                    q = nqT[:, g - HEADS, time_cols(t)]
                                    c = (g - HEADS) // 2
                                    if t < 4:
                                        pe.matmul(ps[0:r, 2 * s, :], q, nkT[:, c, META:T], start=True, stop=True)
                                    last = pe.matmul(ps[0:r, 2 * s + 1, 0:META], q, nkT[:, c, 0:META], start=True, stop=True)
                                last.then_inc(s_sc, 1)
                            m = n - LAG - NT
                            if m >= 0 and m % (2 * NT) == NT and m // NT < NH:
                                g = m // NT - 1
                                pe.wait_ge(s_te, NT * (g + 2))
                                pe.wait_ge(s_pad, 3)
                                if g:
                                    pe.wait_ge(s_me, g // 2)
                                V = Vm if g < HEADS else Vn
                                for k in range(2):
                                    for kc in range(NT):
                                        for i in range(2):
                                            at = (g + i) % HEADS * VD
                                            last = pe.matmul(ps[64 * i:64 * i + 64, 6 + k, 0:HT], V[:, kc, at:at + VD],
                                                             PT[:, (g + i) % 3, kc, k * HT:(k + 1) * HT],
                                                             start=kc == 0, stop=kc == NT - 1)
                                last.then_inc(s_pv, 1)
                            m = n - LAG
                            if 0 <= m < STEPS:
                                g, kc = divmod(m, NT)
                                pe.wait_ge(s_dg, NT * (g + 1))
                                if m >= 1:
                                    pe.wait_ge(s_te, m)
                                for t in range(NT):
                                    r, k = rows_of(t), rows_of(kc)
                                    last = pe.matmul(flat[0:k, 4 * 512 + P * t:4 * 512 + P * t + r],
                                                     Pb[0:r, g % 2, t, time_cols(kc)], dg[0:r, NT * (g % 2) + t, 0:r],
                                                     start=True, stop=True)
                                last.then_inc(s_tr, 1)

                    @block.vector
                    def _(dve):
                        for n in range(STEPS + LAG):
                            if n < STEPS:
                                g, t = divmod(n, NT)
                                s, r, b = n % 2, rows_of(t), n % 10
                                if 2 <= g < HEADS and t < 2 and 2 * (g - 2) + t < HEADS:
                                    i = 2 * (g - 2) + t
                                    dve.wait_ge(s_tb, 32)
                                    dve.tensor_tensor(tb[:, i, :, :], tb[:, i, :, :],
                                                      mk[:, :].unsqueeze(1).to_broadcast([P, 14, GRID_W]), ALU.add).then_inc(s_bias, 1)
                                if g >= HEADS and t == 0:
                                    dve.wait_ge(s_bias, HEADS)
                                    dve.wait_ge(s_tr, NT * (g - 1))
                                    if g < HEADS + 2:
                                        dve.memset(Pb[0:META, g % 2, 4, META:T], 0.0).then_inc(s_cl, 1)
                                dve.wait_ge(s_sc, n + 1)
                                if n >= 10:
                                    dve.wait_ge(s_ex, n - 9)
                                if g < HEADS:
                                    dve_chain.link(dve, dve.tensor_reduce(mx[0:r, b:b + 1], pair(s, slice(0, r)), AX.XY, ALU.max))
                                else:
                                    row = prob(n)
                                    if t < 4:
                                        bias = tb[:, g - HEADS, :, :].rearrange("p a b -> p (a b)")
                                        at = (6 - 2 * t) * GRID_W
                                        dve.scalar_tensor_tensor(
                                            out=row[:, META:T], in0=ps[0:r, 2 * s, :], scalar=NAT_SCALE,
                                            in1=bias[:, at:at + SEQ], op0=ALU.mult, op1=ALU.add).then_inc(dve_chain.sem, 1)
                                        dve_chain.n += 1
                                    dve_chain.link(dve, dve.tensor_scalar(row[:, 0:META], ps[0:r, 2 * s + 1, 0:META],
                                                                          NAT_SCALE, None, ALU.mult))
                                    cols = T if t < 4 else META
                                    dve_chain.link(dve, dve.tensor_reduce(mx[0:r, b:b + 1], row[:, 0:cols], AX.X, ALU.max))
                                dve.tensor_scalar(ng[0:r, b:b + 1], mx[0:r, b:b + 1],
                                                  -MLA_SCALE if g < HEADS else -1.0, None, ALU.mult).then_inc(s_ng, 1)
                            m = n - 1
                            if 0 <= m < STEPS:
                                r, b = rows_of(m % NT), m % 10
                                dve.wait_ge(s_ex, m + 1)
                                if m >= 10:
                                    dve.wait_ge(s_dg, m - 9)
                                dve.reciprocal(rc[0:r, b:b + 1], sm[0:r, b:b + 1]).then_inc(s_rc, 1)
                            if 0 <= n - LAG < NT * HEADS:
                                copy_turned(dve, dve.tensor_copy, n - LAG)

                    @block.scalar
                    def _(act):
                        for n in range(STEPS + PVLAG + NT):
                            if NT * HEADS <= n - LAG < STEPS:
                                copy_turned(act, act.copy, n - LAG)
                            if n < STEPS:
                                g, t = divmod(n, NT)
                                r, b = rows_of(t), n % 10
                                act.wait_ge(s_ng, n + 1)
                                if n >= 10:
                                    act.wait_ge(s_rc, n - 9)
                                if g < HEADS:
                                    if t == 0 and g >= 2:
                                        act.wait_ge(s_tr, NT * (g - 1))
                                    act.activation(halves(prob(n)), pair(n % 2, slice(0, r)), ACT.Exp, bias=ng[0:r, b:b + 1],
                                                   scale=MLA_SCALE, accum_out=sm[0:r, b:b + 1]).then_inc(s_ex, 1)
                                else:
                                    row = prob(n)[:, 0:T if t < 4 else META]
                                    act.activation(row, row, ACT.Exp, bias=ng[0:r, b:b + 1],
                                                   accum_out=sm[0:r, b:b + 1]).then_inc(s_ex, 1)
                            m = n - LAG - NT
                            if m >= 0 and m % (2 * NT) == NT and m // NT < NH:
                                c = m // (2 * NT)
                                act.wait_ge(s_pv, c + 1)
                                act.copy(halves(mT[:, c, :]), pair(3)).then_inc(s_me, 1)

                    @block.gpsimd
                    def _(pool):
                        for g in range(3):
                            pool.memset(PT[:, g, NT - 1, :], 0.0).then_inc(s_pad, 1)
                        for n in range(STEPS):
                            g, t = divmod(n, NT)
                            b, r = n % 10, rows_of(t)
                            if t == 0 and g >= 2:
                                pool.wait_ge(s_tr, NT * (g - 1))
                            pool.wait_ge(s_rc, n + 1)
                            pool.tensor_scalar(dg[0:r, b, 0:r], ident[0:r, 0:r], rc[0:r, b:b + 1], None, ALU.mult).then_inc(s_dg, 1)

          ring = ExitStack()
          weights = expert_weights(0, ring)
          out_phase("a4", lambda k: mT[:, k, :], wo, s_wo, tile_cols, NT, weights[-1], weights[-2])

        ahead = ExitStack()
        gain = moe_phase(0, weights, ring, NT, ahead, A["norm_mix1"])

        with ExitStack() as conv:
            al = scope_alloc(conv)
            hy = al("hy", [P, HYC, T])
            cc = al("cc", [P, HYC, T])

            long = ExitStack()
            al = scope_alloc(long)
            gates = al("gates", [P, 2 * HYC, T])
            dft = al("dft", [P, 2, FT, FC * P])
            idft = al("idft", [P, 2 * FC, FL])
            w3 = al("w3f", [P, 4, HYW])
            hid = al("hidf", [P, 2, FL])
            eld = al("eld", [P, 4, HYW])
            zf = al("z_folded", [P, HYC, 2, FL])
            ntc = al("neg_time", [P, 2, FT])
            ck = al("ck", [P, FC])
            hb = al("hy_bias", [P, 2, HYC])
            HF = slice(0, HY_FFN)
            s_ld, s_tables, s_u, s_arg, s_sin, s_eld, s_zf = (sem(f"c2_{n}") for n in (
                "constants_loaded", "tables_loaded", "affine", "argument", "sine", "rates", "z_folded"))

            with ExitStack() as scope:
                al = scope_alloc(scope)
                yT = al("yT_c", [P, KC, T])
                R = 6
                s_w = [sem_again(f"projection_w{j}_loaded") for j in range(R)]
                wr = al("c1_w", [P, R, KC, P])
                with ExitStack() as s2:
                    xn = scope_alloc(s2)("xn_c", [P, NT, D])
                    norm_phase("nrm2", gain, xn, yT, also=[(wr[:, j, :, :], A["wc"][j], s_w[j]) for j in range(R)])
                ahead.close()
                NJ, NG, NHY = 20, 8, 12
                xp = al("c1_padded", [P, 2, T + 2])
                glu = al("glu", [P, HYC, T + 2 * PAD31])
                tap = al("c1_tap", [P, 2, T])
                sg = al("c1_sigmoid", [P, 2, T])
                sw = al("short_w", [P, NHY, 3])
                sbias = al("short_b", [P, NHY])
                cw = al("cf_w", [P, HYC, CFK])
                cb = al("cf_b", [P, HYC])
                s_dw = sem("c1_depthwise")
                feat = al("feat", [HY_EMB, 2 * FL])
                w1 = al("w1f", [HY_EMB, HY_FFN])
                w2 = al("w2f", [HY_FFN, HY_FFN])
                vec = al("hy_vec", [HY_FFN, 3])
                arg, kk = al("sin_arg", [HY_FFN, 2, FL]), al("sin_turns", [HY_FFN, 2, FL])
                small = [(feat[:, :], "feat"), (w1[:, :], "hy_ffn_w1"), (w2[:, :], "hy_ffn_w2"), (vec[:, :], "hy_vec"),
                         (w3[0:HY_FFN, :, :], "hy_ffn_w3"), (eld[:, :, :], "log_decay"), (ntc[:, :, :], "neg_time"),
                         (ck[:, :], "ck"), (hb[:, :, :], "hy_bias")]
                LD = 16 * len(small)

                def fold(dve, c):
                    x, mirror = hy[:, c, 1:FL], hy[:, c, T - 1:T - FL:-1]
                    dve.tensor_tensor(zf[:, c, 0, 1:FL], x, mirror, ALU.add).then_inc(dve_chain.sem, 1)
                    dve.tensor_tensor(zf[:, c, 1, 1:FL], x, mirror, ALU.subtract).then_inc(dve_chain.sem, 1)
                    dve_chain.n += 2
                    dve.wait_ge(dve_chain.sem, dve_chain.n)
                    dve.tensor_copy(zf[:, c, :, 0:1], hy[:, c, 0:1].unsqueeze(1).to_broadcast([P, 2, 1])).then_inc(s_zf, 1)

                s_taps, s_pad, s_job, s_ea, s_ed, s_cv = (sem(f"c1_{n}") for n in (
                    "taps_loaded", "pads_set", "product", "act_copied", "gated", "short_done"))
                with nc.Block() as block:
                    @block.sync
                    def _(sp):
                        sp.dma_start(sw[:, :, :], A["short_w"]).then_inc(s_taps, 16)
                        sp.dma_start(sbias[:, :], A["short_b"]).then_inc(s_taps, 16)
                        sp.dma_start(cw[:, :, :], A["cf_w"]).then_inc(s_taps, 16)
                        sp.dma_start(cb[:, :], A["cf_b"]).then_inc(s_taps, 16)
                        for j in range(NJ):
                            if j >= R:
                                sp.wait_ge(s_job, j - R + 1)
                                sp.dma_start(wr[:, j % R, :, :], A["wc"][j]).then_inc(s_w[j % R], 16)
                            if j == 0:
                                for dst, name in small:
                                    sp.dma_start(dst, A[name]).then_inc(s_ld, 16)
                        sp.dma_start(dft[:, :, :, :], A["dft"]).then_inc(s_tables, 16)
                        sp.dma_start(idft[:, :, :], A["idft"]).then_inc(s_tables, 16)

                    @block.tensor
                    def _(pe):
                        for j in range(NJ):
                            s = j % 4
                            if j >= 4:
                                if j - 4 >= NG:
                                    pe.wait_ge(s_ea, HYC + 2 * (j - 4 - NG) + 1)
                                else:
                                    pe.wait_ge(s_ed if j % 2 else s_ea, (j - 4) // 2 + 1)
                            if j == 1:
                                pe.wait_ge(s_ld, LD)
                                for n in range(2):
                                    last = pe.matmul(ps[HF, 6 + n, 0:FL], w1[:, :], feat[:, n * FL:(n + 1) * FL],
                                                     start=True, stop=True)
                                last.then_inc(s_u, 1)
                            elif j == 3:
                                pe.wait_ge(s_arg, 1)
                            elif j == 6:
                                pe.wait_ge(s_sin, 1)
                                pe.wait_ge(s_ed, 2)
                                for n in range(2):
                                    last = pe.matmul(ps[HF, 6 + n, 0:FL], w2[:, :], hid[HF, n, :], start=True, stop=True)
                                last.then_inc(s_u, 1)
                            elif j == 7:
                                pe.wait_ge(s_arg, 2)
                            pe.wait_ge(s_w[j % R], 16 * (j // R + 1))
                            for n in range(2):
                                for c in range(KC):
                                    last = pe.matmul(ps[:, 2 * s + n, 0:HT], wr[:, j % R, c, :],
                                                     yT[:, c, n * HT:(n + 1) * HT], start=c == 0, stop=c == KC - 1)
                            last.then_inc(s_job, 1)

                    @block.scalar
                    def _(act):
                        act.wait_ge(s_pad, 1)
                        act.wait_ge(s_taps, 64)
                        for i in range(HYC):
                            if i in (1, 3):
                                act.wait_ge(s_arg, (i + 1) // 2)
                                act.activation(hid[HF, :, :], arg[:, :, :], ACT.Sin).then_inc(s_sin, 1)
                            if i == 3:
                                act.wait_ge(s_ld, LD)
                                act.activation(eld[:, :, :], eld[:, :, :], ACT.Exp).then_inc(s_eld, 1)
                                act.wait_ge(s_eld, 1)
                            act.wait_ge(s_job, 2 * i + 1)
                            if i >= 2:
                                act.wait_ge(s_ed, i - 1)
                            act.activation(halves(sg[:, i % 2, :]), pair((2 * i) % 4), ACT.Sigmoid).then_inc(s_ea, 1)
                        for j in range(NHY):
                            act.wait_ge(s_job, NG + j + 1)
                            if j >= 2:
                                act.wait_ge(s_cv, j - 1)
                            act.copy(halves(xp[:, j % 2, 1:T + 1]), pair((NG + j) % 4)).then_inc(s_ea, 1)
                            act.wait_ge(s_ea, HYC + 2 * j + 1)
                            act.activation(tap[:, j % 2, :], xp[:, j % 2, 0:T], ACT.Identity, bias=sbias[:, j:j + 1],
                                           scale=sw[:, j, 0:1]).then_inc(s_ea, 1)

                    @block.vector
                    def _(dve):
                        taps = 0

                        def depthwise(count):
                            nonlocal taps
                            for n in range(taps, min(taps + count, CFK * HYC)):
                                c = 2 * (n // (2 * CFK)) + n % 2
                                k = n % (2 * CFK) // 2
                                x = glu[:, c, k:k + T]
                                if k == 0:
                                    ins = dve.tensor_scalar(cc[:, c, :], x, cw[:, c, 0:1], cb[:, c:c + 1], ALU.mult, ALU.add)
                                else:
                                    dve.wait_ge(s_dw, n - 1)
                                    ins = dve.scalar_tensor_tensor(out=cc[:, c, :], in0=x, scalar=cw[:, c, k:k + 1],
                                                                   in1=cc[:, c, :], op0=ALU.mult, op1=ALU.add)
                                ins.then_inc(s_dw, 1)
                                taps = n + 1

                        def affine(k):
                            dve.wait_ge(s_u, k + 1)
                            if k:
                                dve.wait_ge(s_sin, 1)
                            dve_chain.link(dve, dve.tensor_scalar(arg[:, :, :], ps[HF, 6:8, 0:FL], vec[:, k:k + 1], vec[:, 2:3],
                                                                  ALU.add, ALU.mult))
                            dve_chain.link(dve, dve.tensor_scalar(kk[:, :, :], arg[:, :, :], 1.0 / (2 * math.pi), MAGIC, ALU.mult, ALU.add))
                            dve_chain.link(dve, dve.tensor_scalar(kk[:, :, :], kk[:, :, :], MAGIC, None, ALU.subtract))
                            for part in TURN:
                                dve_chain.link(dve, dve.scalar_tensor_tensor(out=arg[:, :, :], in0=kk[:, :, :], scalar=-part, in1=arg[:, :, :],
                                                                             op0=ALU.mult, op1=ALU.add))
                            dve.tensor_scalar(arg[:, :, :], arg[:, :, :], PI_IN, -PI_IN, ALU.min, ALU.max).then_inc(s_arg, 1)

                        dve_chain.link(dve, dve.memset(glu[:, :, :], 0.0))
                        dve_chain.link(dve, dve.memset(w3[HY_FFN:P, :, :], 0.0))
                        dve_chain.link(dve, dve.memset(hid[HY_FFN:P, :, :], 0.0))
                        dve.memset(xp[:, :, :], 0.0).then_inc(s_pad, 1)
                        dve.wait_ge(s_taps, 64)
                        dve.wait_ge(s_ld, LD)
                        affine(0)
                        for i in range(HYC):
                            dve.wait_ge(s_ea, i + 1)
                            dve.wait_ge(s_job, 2 * i + 2)
                            dve.tensor_tensor(halves(glu[:, i, PAD31:PAD31 + T]), pair((2 * i + 1) % 4), halves(sg[:, i % 2, :]),
                                              ALU.mult).then_inc(s_ed, 1)
                            dve.wait_ge(s_ed, i + 1)
                            if i == 1:
                                depthwise(20)
                            if i == 2:
                                affine(1)
                                depthwise(20)
                        for j in range(NHY):
                            x, y = xp[:, j % 2, :], tap[:, j % 2, :]
                            dve.wait_ge(s_ea, HYC + 2 * j + 2)
                            dve_chain.link(dve, dve.scalar_tensor_tensor(out=y, in0=x[:, 1:T + 1], scalar=sw[:, j, 1:2],
                                                                         in1=y, op0=ALU.mult, op1=ALU.add))
                            dve.scalar_tensor_tensor(out=hy[:, j, :] if j < HYC else gates[:, j - HYC, :], in0=x[:, 2:T + 2], scalar=sw[:, j, 2:3],
                                                     in1=y, op0=ALU.mult, op1=ALU.add).then_inc(s_cv, 1)
                            if j < HYC:
                                dve.wait_ge(s_cv, j + 1)
                                fold(dve, j)
                            if j < NHY - 1:
                                depthwise(8)
                        depthwise(CFK * HYC)
                        dve.wait_ge(s_dw, CFK * HYC)

            with ExitStack() as scope:
                al = scope_alloc(scope)
                CD = al("CD", [P, 2 * FC, HYW])
                FS = al("FS", [P, 4 * FT, HYW])
                product = al("product", [P, 2 * FC, HYW])
                zt = al("zt", [P, 2, FT, HYW])
                dec = al("dec", [P, 2, 2, HYW])
                uv = al("fil_uv", [P, 2, 2, HYW])
                tm = al("tm", [P, 4, HYW])
                s_f, s_dec, s_fe, s_fs = (sem(f"c2_{n}") for n in ("filter_product", "decay", "filter_decayed", "filter_ready"))
                s_tp, s_zt, s_sp, s_se, s_ab, s_cx, s_iv, s_z = (sem(f"c2_{n}") for n in (
                    "z_turned", "z_copied", "spectrum", "spectrum_copied", "z_spectrum", "product_ready", "inverse", "z_ready"))
                s_zero, s_uv = sem("c2_padding_zero"), sem("c2_filter_sums")

                with nc.Block() as block:
                    def filters(pe, o, t):
                        n, r = FT * o + t, fold_rows(t)
                        if n:
                            pe.wait_ge(s_fe, n)
                        if o:
                            pe.wait_ge(s_cx, FC)
                        for v in range(2):
                            for d in range(2):
                                last = pe.matmul(ps[0:r, 2 * v + d, :], hid[:, v, P * t:P * t + r], w3[:, 2 * d + o, :],
                                                 start=True, stop=True)
                        last.then_inc(s_f, 1)

                    def turn_z(pe, o):
                        pe.wait_ge(s_zf, HYC * (o + 1))
                        for i in range(2 * FT):
                            t, g = divmod(i, 2)
                            r = fold_rows(t)
                            if i >= 2:
                                pe.wait_ge(s_zt, 2 * FT * o + i - 1)
                            if o:
                                pe.wait_ge(s_z, HYC)
                            for c in range(HYC):
                                last = pe.transpose(ps[0:r, 4 + g, c * P:(c + 1) * P], zf[:, c, g, P * t:P * t + r], ident[:, :])
                            last.then_inc(s_tp, 1)

                    def spectrum_bank(o):
                        return 0 if o else 6

                    def filter_spectrum(pe, o):
                        pe.wait_ge(s_fs, 2 * FT * (o + 1))
                        if o:
                            pe.wait_ge(s_fe, 2 * FT)
                        for i in range(2 * FC):
                            m, g = divmod(i, 2)
                            if i >= 2:
                                pe.wait_ge(s_se, 2 * FC * o + i - 1)
                            sources = ((0, 1), (3, 2))[g]
                            if m < 4:
                                for t in range(FT):
                                    last = pe.matmul(ps[:, spectrum_bank(o) + g, :], dft[:, g, t, m * P:(m + 1) * P],
                                                     FS[:, 4 * t + sources[m // 2], :], start=t == 0, stop=t == FT - 1)
                            else:
                                for odd in range(2):
                                    at = 32 * odd
                                    for t in range(FT):
                                        last = pe.matmul(ps[at:at + 32, spectrum_bank(o) + g, :], dft[:, g, t, 4 * P + at:4 * P + at + 32],
                                                         FS[:, 4 * t + sources[odd], :], start=t == 0, stop=t == FT - 1)
                            last.then_inc(s_sp, 1)

                    def z_spectrum(pe, o):
                        pe.wait_ge(s_zt, 2 * FT * (o + 1))
                        pe.wait_ge(s_fe, FT * (o + 1))
                        pe.wait_ge(s_se, 2 * FC * (o + 1))
                        for m in range(FC):
                            r = spectrum_rows(m)
                            if m >= 2:
                                pe.wait_ge(s_cx, FC * o + m - 1)
                            for g in range(2):
                                for t in range(FT):
                                    last = pe.matmul(ps[0:r, 2 * (m % 2) + g, :], dft[:, g, t, m * P:m * P + r], zt[:, g, t, :],
                                                     start=t == 0, stop=t == FT - 1)
                            last.then_inc(s_ab, 1)

                    def inverse(pe, o, c):
                        pe.wait_ge(s_se, 2 * FC * (o + 1))
                        if c >= 2:
                            pe.wait_ge(s_z, HYC * o + c - 1)
                        for m in range(FC):
                            pe.wait_ge(s_cx, FC * o + m + 1)
                            for g in range(2):
                                last = pe.matmul(ps[:, 4 + 2 * (c % 2) + g, 0:FL], product[:, 2 * m + g, c * P:(c + 1) * P],
                                                 idft[:, 2 * m + g, :], start=m == 0, stop=m == FC - 1)
                        last.then_inc(s_iv, 1)

                    @block.tensor
                    def _(pe):
                        filters(pe, 0, 0)
                        turn_z(pe, 0)
                        for t in range(1, FT):
                            filters(pe, 0, t)
                        pe.wait_ge(s_zero, 2)
                        pe.wait_ge(s_tables, 32)
                        filter_spectrum(pe, 0)
                        z_spectrum(pe, 0)
                        for c in range(HYC):
                            if c < FT:
                                filters(pe, 1, c)
                            inverse(pe, 0, c)
                        filter_spectrum(pe, 1)
                        turn_z(pe, 1)
                        z_spectrum(pe, 1)
                        for c in range(HYC):
                            inverse(pe, 1, c)

                    def decays(act, o):
                        for t in range(FT):
                            r = fold_rows(t)
                            if FT * o + t >= 1:
                                act.wait_ge(s_fe, FT * o + t)
                            for v in range(2):
                                act.activation(dec[0:r, v, :, :], eld[0:r, o::2, :], ACT.Exp,
                                               scale=ntc[0:r, v, t:t + 1]).then_inc(s_dec, 1)

                    def copy_zt(act, o):
                        for i in range(2 * FT):
                            t, g = divmod(i, 2)
                            r = fold_rows(t)
                            act.wait_ge(s_tp, 2 * FT * o + i + 1)
                            if t == FT - 1:
                                act.wait_ge(s_zero, 1)
                            act.copy(zt[0:r, g, t, :], ps[0:r, 4 + g, :]).then_inc(s_zt, 1)

                    def scale_spectrum(act, o):
                        for i in range(2 * FC):
                            r = spectrum_rows(i // 2)
                            act.wait_ge(s_sp, 2 * FC * o + i + 1)
                            act.mul(CD[0:r, i, :], ps[0:r, spectrum_bank(o) + i % 2, :], ck[0:r, i // 2:i // 2 + 1]).then_inc(s_se, 1)

                    @block.scalar
                    def _(act):
                        r = fold_rows(0)
                        for v in range(2):
                            act.activation(dec[0:r, v, :, :], eld[0:r, 0::2, :], ACT.Exp,
                                           scale=ntc[0:r, v, 0:1]).then_inc(s_dec, 1)
                        copy_zt(act, 0)
                        for t in range(1, FT):
                            r = fold_rows(t)
                            act.wait_ge(s_fe, t)
                            for v in range(2):
                                act.activation(dec[0:r, v, :, :], eld[0:r, 0::2, :], ACT.Exp,
                                               scale=ntc[0:r, v, t:t + 1]).then_inc(s_dec, 1)
                        scale_spectrum(act, 0)
                        decays(act, 1)
                        act.wait_ge(s_cx, FC)
                        scale_spectrum(act, 1)
                        copy_zt(act, 1)

                    @block.gpsimd
                    def _(pool):
                        pool.memset(zt[:, :, FT - 1, :], 0.0).then_inc(s_zero, 1)
                        pool.memset(product[:, 2 * (FC - 1):2 * FC, :], 0.0).then_inc(s_zero, 1)
                        for n in range(2 * FT):
                            r, t = fold_rows(n % FT), n % FT
                            if n == FT:
                                pool.wait_ge(s_sp, 2 * FC)
                            pool.wait_ge(s_uv, 2 * n + 2)
                            pool.tensor_tensor(FS[0:r, 4 * t:4 * t + 2, :], uv[0:r, 0, :, :], uv[0:r, 1, :, :], ALU.add).then_inc(s_fs, 1)

                    def fold_filters(dve, o, t):
                        n = FT * o + t
                        r = fold_rows(t)
                        dve.wait_ge(s_f, n + 1)
                        dve.wait_ge(s_dec, 2 * n + 2)
                        if n:
                            dve.wait_ge(s_uv, 2 * n)
                            dve.wait_ge(s_fs, 2 * n)
                        if o:
                            dve.wait_ge(s_cx, FC)
                            if t:
                                dve.wait_ge(s_z, t)
                        fil = tm[:, :, :].rearrange("p (v d) c -> p v d c", v=2)
                        dve.tensor_tensor(tm[0:r, :, :], ps[0:r, 0:4, :], dec[0:r, :, :, :].rearrange("p v d c -> p (v d) c"),
                                          ALU.mult).then_inc(s_fe, 1)
                        dve.wait_ge(s_fe, n + 1)
                        if t == 0:
                            dve_chain.link(dve, dve.memset(fil[0:1, 0, 1, :], 0.0))
                            dve_chain.link(dve, dve.memset(fil[0:1, 1, :, :], 0.0))
                        for k, op in enumerate((ALU.add, ALU.subtract)):
                            dve.tensor_tensor(uv[0:r, :, k, :], fil[0:r, :, 0, :], fil[0:r, :, 1, :], op).then_inc(s_uv, 1)
                        dve.wait_ge(s_uv, 2 * n + 2)
                        dve.tensor_tensor(FS[0:r, 4 * t + 2:4 * t + 4, :], uv[0:r, 0, :, :], uv[0:r, 1, :, :],
                                          ALU.subtract).then_inc(s_fs, 1)

                    def multiply_spectra(dve, o):
                        dve.wait_ge(s_uv, 2 * FT * (o + 1))
                        dve.wait_ge(s_zero, 2)
                        if o:
                            dve.wait_ge(s_z, HYC)
                        for m in range(FC):
                            bank = 2 * (m % 2)
                            r = spectrum_rows(m)
                            dve.wait_ge(s_ab, FC * o + m + 1)
                            dve.wait_ge(s_se, 2 * FC * o + 2 * m + 2)
                            if FC * o + m:
                                dve.wait_ge(s_cx, FC * o + m)
                            for k, (x, y) in enumerate(((0, 0), (1, 1), (0, 1), (1, 0))):
                                op = dve.tensor_tensor(tm[0:r, k, :], ps[0:r, bank + x, :], CD[0:r, 2 * m + y, :], ALU.mult)
                                if k == 3:
                                    dve_chain.link(dve, op)
                            rows = [(slice(0, r), m // 2)] if m < 4 else [(slice(0, 32), 0), (slice(32, 64), 1)]
                            for k, (at, odd) in enumerate(rows):
                                dve_chain.link(dve, dve.tensor_tensor(product[at, 2 * m + odd, :], tm[at, 0, :], tm[at, 1, :], ALU.subtract))
                                op = dve.tensor_tensor(product[at, 2 * m + 1 - odd, :], tm[at, 2, :], tm[at, 3, :], ALU.add)
                                if k == len(rows) - 1:
                                    op.then_inc(s_cx, 1)
                                else:
                                    dve_chain.link(dve, op)

                    def unfold(dve, o, c):
                        dve.wait_ge(s_iv, HYC * o + c + 1)
                        dve.wait_ge(s_cx, FC * (o + 1))
                        if not o:
                            dve.wait_ge(s_uv, 2 * (FT + min(c + 1, FT)))
                        if HYC * o + c:
                            dve.wait_ge(s_z, HYC * o + c)
                        bank = 4 + 2 * (c % 2)
                        t1 = tm[:, 2 * (c % 2):2 * (c % 2) + 2, :].rearrange("p a b -> p (a b)")[:, 0:T]
                        parts = ((slice(0, FL), slice(0, FL), ALU.add), (slice(FL, T), slice(FL - 2, 0, -1), ALU.subtract))
                        for at, mirror, op in parts:
                            ins = dve.scalar_tensor_tensor(out=t1[:, at], in0=hy[:, c, at], scalar=hb[:, o, c:c + 1],
                                                           in1=ps[:, bank, mirror], op0=ALU.mult, op1=ALU.add)
                        dve_chain.link(dve, ins)
                        for at, mirror, op in parts:
                            ins = dve.tensor_tensor(t1[:, at], t1[:, at], ps[:, bank + 1, mirror], op)
                        dve_chain.link(dve, ins)
                        dve.tensor_tensor(hy[:, c, :], t1, gates[:, HYC * o + c, :], ALU.mult).then_inc(s_z, 1)

                    @block.vector
                    def _(dve):
                        dve_chain.link(dve, dve.memset(FS[:, 4 * (FT - 1):4 * FT, :], 0.0))
                        for t in range(FT):
                            fold_filters(dve, 0, t)
                        multiply_spectra(dve, 0)
                        for c in range(HYC):
                            if c < FT:
                                fold_filters(dve, 1, c)
                            unfold(dve, 0, c)
                            dve.wait_ge(s_z, c + 1)
                            fold(dve, c)
                        multiply_spectra(dve, 1)
                        for c in range(HYC):
                            unfold(dve, 1, c)

            long.close()
            with ExitStack() as scope:
                al = scope_alloc(scope)
                wo = al("wo_c", [P, KC, D])
                lg = al("ln_gb", [P, 2, HYC])
                mu, sq = al("ln_mu", [P, T]), al("ln_sq", [P, HYC, T])
                s_wz, s_wc = sem("c5_z_w_loaded"), sem("c5_conformer_w_loaded")
                s_ld, s_s1, s_sq, s_s2, s_ms, s_rt, s_xc, s_out = (sem(f"c4_{n}") for n in (
                    "loaded", "sums", "squares", "square_sums", "variance", "root", "scaled", "silu"))
                s_job, s_add = sem_again("out_product"), sem_again("out_added")
                ring = ExitStack()
                weights = expert_weights(1, ring)
                JOBS = 2 * (NT - 1)
                with nc.Block() as block:
                    @block.sync
                    def _(sp):
                        for k in range(KC):
                            sp.dma_start(wo[:, k, :], A["c_w_out"][k * P:(k + 1) * P, :]).then_inc(s_wz if k < HYC else s_wc, 16)
                        sp.dma_start(lg[:, :, :], A["ln_gb"]).then_inc(s_ld, 16)
                        weights[-1](sp)

                    def channel_sums(pe, x, done):
                        for n in range(2):
                            for c in range(HYC):
                                last = pe.matmul(ps[:, 6 + n, 0:HT], ones[:, :], x[:, c, n * HT:(n + 1) * HT], start=c == 0, stop=c == HYC - 1)
                        last.then_inc(done, 1)

                    def product(pe, j, chunks):
                        t, n = divmod(j, 2)
                        for k in chunks:
                            x = hy[:, k, time_cols(t)] if k < HYC else cc[:, k - HYC, time_cols(t)]
                            last = pe.matmul(ps[:, j, :], x, wo[:, k, n * 512:(n + 1) * 512], start=k == 0, stop=k == KC - 1)
                        return last

                    @block.tensor
                    def _(pe):
                        channel_sums(pe, cc, s_s1)
                        pe.wait_ge(s_wz, 16 * HYC)
                        for j in range(3):
                            product(pe, j, range(HYC))
                        pe.wait_ge(s_sq, 1)
                        channel_sums(pe, sq, s_s2)
                        for j in range(3, 6):
                            product(pe, j, range(HYC))
                        pe.wait_ge(s_ms, 1)
                        for j in range(6, JOBS):
                            product(pe, j, range(HYC))
                        pe.wait_ge(s_wc, 16 * HYC)
                        pe.wait_ge(s_out, HYC)
                        for j in range(JOBS):
                            product(pe, j, range(HYC, KC)).then_inc(s_job, 1)

                    @block.vector
                    def _(dve):
                        dve.wait_ge(s_s1, 1)
                        dve_chain.link(dve, dve.tensor_scalar(halves(mu[:, :]), pair(3), 1.0 / HYW, None, ALU.mult))
                        bc = mu[:, :].unsqueeze(1).to_broadcast([P, HYC, T])
                        dve_chain.link(dve, dve.tensor_tensor(cc[:, :, :], cc[:, :, :], bc, ALU.subtract))
                        dve.tensor_tensor(sq[:, :, :], cc[:, :, :], cc[:, :, :], ALU.mult).then_inc(s_sq, 1)
                        dve.wait_ge(s_s2, 1)
                        dve.tensor_scalar(halves(mu[:, :]), pair(3), 1.0 / HYW, EPS, ALU.mult, ALU.add).then_inc(s_ms, 1)
                        dve.wait_ge(s_rt, 1)
                        dve_chain.link(dve, dve.reciprocal(mu[:, :], sq[:, 0, :]))
                        for c in range(HYC):
                            dve.tensor_tensor(cc[:, c, :], cc[:, c, :], mu[:, :], ALU.mult).then_inc(s_xc, 1)
                        for j in range(JOBS):
                            t, n = divmod(j, 2)
                            hh = h[:, t, n * 512:(n + 1) * 512]
                            dve.wait_ge(s_job, j + 1)
                            dve.tensor_tensor(hh, hh, ps[:, j, :], ALU.add).then_inc(s_add, 1)
                        dve.wait_ge(s_add, JOBS)

                    @block.scalar
                    def _(act):
                        act.wait_ge(s_ms, 1)
                        act.activation(sq[:, 0, :], mu[:, :], ACT.Sqrt).then_inc(s_rt, 1)
                        act.wait_ge(s_ld, 16)
                        for c in range(HYC):
                            act.wait_ge(s_xc, c + 1)
                            act.activation(cc[:, c, :], cc[:, c, :], ACT.Silu, bias=lg[:, 1, c:c + 1],
                                           scale=lg[:, 0, c:c + 1]).then_inc(s_out, 1)
                        for t in range(NT - 1):
                            act.wait_ge(s_add, 2 * t + 2)
                            if t:
                                act.wait_ge(s_squares, t)
                            square(act, t, weights[-2])

        ahead = ExitStack()
        gain = moe_phase(1, weights, ring, NT - 1, ahead, A["norm_final"])
        with ahead:
            xn = scope_alloc(ahead)("xn_out", [P, NT, D])
            norm_phase("nrm4", gain, xn, None, NT - 1, store=A["out"])



def tables():
    t = {}
    t["ident"] = np.eye(P, dtype=np.float32)
    t["zeros"] = np.zeros((P, D))
    pos = np.arange(T, dtype=np.float32)
    inv = (np.float32(10000.0) ** (-np.arange(0, ROPE, 2, dtype=np.float32) / ROPE)).astype(np.float32)
    ang = (inv[:, None] * pos[None, :]).astype(np.float32)
    c, s = np.cos(ang), np.sin(ang)
    t["rope_cos"] = np.tile(np.concatenate([c, c]), (4, 1))
    t["rope_sin"] = np.tile(np.concatenate([-s, s]), (4, 1))
    qc, kc = np.arange(GRID_W)[:, None], np.arange(GRID_W)[None, :]
    start = np.clip(qc - WIN_COLS // 2, 0, GRID_W - WIN_COLS)
    inside = (kc >= start) & (kc < start + WIN_COLS)
    t["nat_mask"] = np.tile(np.where(inside, 0.0, NEG), (2, 1))
    k = np.full(FC * P, -1)
    k[0:2 * P], k[2 * P:4 * P] = 2 * np.arange(2 * P), 2 * np.arange(2 * P) + 1
    rest = np.arange(4 * P, NF)
    k[4 * P:4 * P + len(rest[rest % 2 == 0])] = rest[rest % 2 == 0]
    k[4 * P + 32:4 * P + 32 + len(rest[rest % 2 == 1])] = rest[rest % 2 == 1]
    n, real = np.arange(FL)[:, None], k >= 0
    w = 2 * np.pi * ((n * k[None, :]) % NFFT) / NFFT
    odd = (k % 2 == 1) & real
    groups = np.stack([np.where(odd, np.sin(w), np.cos(w)), np.where(odd, np.cos(w), np.sin(w))]) * real
    count = np.where(n == T // 2, 0.5, 1.0)
    dft = np.zeros((FT * P, 2, FC * P))
    dft[:FL] = (groups * count).transpose(1, 0, 2)
    t["dft"] = dft.reshape(FT, P, 2, FC * P).transpose(1, 2, 0, 3)
    inverse = groups * np.stack([np.ones(FC * P), np.where(odd, -1.0, 1.0)])[:, None, :]
    t["idft"] = inverse.reshape(2, FL, FC, P).transpose(3, 2, 0, 1).reshape(P, 2 * FC, FL)
    weight = np.where(k % T == 0, 1.0, 2.0) * real / NFFT
    t["ck"] = weight.reshape(FC, P).T
    tt = np.linspace(0.0, 1.0, T, dtype=np.float32)
    times = np.stack([np.arange(FL), (T - np.arange(FL)) % T])
    neg_time = np.zeros((2, FT * P))
    neg_time[:, :FL] = -tt[times]
    t["neg_time"] = neg_time.reshape(2, FT, P).transpose(2, 0, 1)
    bands = np.linspace(1e-4, 15, 16, dtype=np.float32)
    a = (np.float32(2.0 * math.pi) * tt[:, None] * bands[None, :]).astype(np.float32)
    t["feat"] = np.concatenate([tt[:, None], np.cos(a), np.sin(a)], axis=1).T[:, times.reshape(-1)]
    e = np.arange(NE)
    t["later"] = (np.arange(P)[:, None] < np.arange(P)[None, :])
    valid = np.zeros((P, NT))
    for i in range(NT):
        valid[:rows_of(i), i] = 1.0
    t["valid"] = np.stack([valid, valid * (np.arange(NT) < NT - 1)], axis=1)
    t["first"] = np.tile(np.concatenate([np.arange(GROUPS, 0, -1), np.arange(EXPERTS, 0, -1), e]), (P, 1))
    t["expert_tab"] = np.concatenate([e[:, None] < e[None, :], e[:, None], np.tile(np.arange(NX), (NE, 1))], axis=1)
    return {k: np.ascontiguousarray(v, dtype=np.float32) for k, v in t.items()}


def lay_out(x):
    a = dict(tables())
    by_chunk = lambda w: w.reshape(P, KC, -1, P).transpose(2, 0, 1, 3)
    cols = lambda v: v.reshape(-1, P).T
    rep = lambda v: np.broadcast_to(v.reshape(1, -1), (P, v.size))
    a["x"], a["meta_tokens"] = x["x"], x["meta_tokens"]
    for i in range(2):
        a[f"norm_mix{i}"], a[f"norm_ffn{i}"] = rep(x["norm_mix"][i]), rep(x["norm_ffn"][i])
    for i in range(2):
        a[f"router_w{i}"] = np.concatenate([x["moe_w_group"][i], x["moe_w_router"][i].transpose(1, 0, 2).reshape(D, NE)],
                                           axis=1).reshape(P, KC, NL)
    a["router_b"] = np.stack([rep(np.concatenate([x["moe_b_group"][i], x["moe_b_router"][i].reshape(-1)])) for i in range(2)], axis=1)
    a["norm_final"] = rep(x["norm_final"])
    w = x["a_w_in"][0]
    kpe = w[:, 384:416]
    swap = np.concatenate([kpe[:, 16:], kpe[:, :16]], axis=1)
    a["wa"] = by_chunk(np.concatenate([w[:, 0:384], np.tile(kpe, (1, 4)), np.tile(swap, (1, 4)), w[:, 416:1440]], axis=1))
    a["wnv"] = w[:, 1440:1952].reshape(P, KC, 512)
    uq = x["mla_w_uq"][0].reshape(2, P, HEADS, QK).transpose(1, 0, 2, 3)
    a["wuq"] = uq.reshape(P, 2, HEADS * QK)
    a["wsw"] = np.concatenate([uq[..., NOPE + 16:], uq[..., NOPE:NOPE + 16]], axis=-1).reshape(P, 2, HEADS * ROPE)
    ukv = x["mla_w_ukv"][0].reshape(P, HEADS, NOPE + VD)
    a["wkn"], a["wv"] = ukv[:, :, :NOPE].reshape(P, -1), ukv[:, :, NOPE:].reshape(P, -1)
    a["gl"] = np.concatenate([cols(x["mla_q_norm"][0]), cols(x["mla_kv_norm"][0])], axis=1)
    rpb = x["nat_rpb"][0]
    half, qc = np.divmod(np.arange(P), GRID_W)
    row = np.arange(14)[None, :] + 1 - half[:, None]
    col = np.clip(np.arange(GRID_W)[None, :] - qc[:, None] + WIN_COLS - 1, 0, 2 * WIN_COLS - 2)
    a["nat_table"] = rpb[:, row[:, :, None], col[:, None, :]].transpose(1, 0, 2, 3)
    a["a_w_out"] = x["a_w_out"][0]
    w = x["c_w_in"][0]
    parts = []
    for i in range(HYC):
        parts += [w[:, 2048 + P * i:2048 + P * (i + 1)], w[:, 1536 + P * i:1536 + P * (i + 1)]]
    parts.append(w[:, 0:1536])
    a["wc"] = by_chunk(np.concatenate(parts, axis=1))
    a["short_w"] = x["hy_short_w"][0].reshape(3, 12, P).transpose(2, 1, 0)
    a["short_b"] = cols(x["hy_short_b"][0])
    a["hy_ffn_w1"], a["hy_ffn_w2"] = x["hy_ffn_w1"][0], x["hy_ffn_w2"][0]
    a["hy_ffn_w3"] = x["hy_ffn_w3"][0].reshape(HY_FFN, 4, HYW)
    a["hy_vec"] = np.stack([x["hy_ffn_b1"][0], x["hy_ffn_b2"][0], x["hy_sin_freq"][0]], axis=1)
    a["log_decay"] = np.broadcast_to(x["hy_log_decay"][0].reshape(1, 4, HYW), (P, 4, HYW))
    a["hy_bias"] = x["hy_bias"][0].reshape(2, HYC, P).transpose(2, 0, 1)
    a["cf_w"] = x["cf_dw_w"][0].reshape(CFK, HYC, P).transpose(2, 1, 0)
    a["cf_b"] = cols(x["cf_dw_b"][0])
    a["ln_gb"] = np.stack([cols(x["cf_ln_g"][0]), cols(x["cf_ln_b"][0])], axis=1)
    a["c_w_out"] = x["c_w_out"][0]
    for name in ("moe_w1", "moe_w3", "moe_w2"):
        a[name] = x[name]
    return {k: np.ascontiguousarray(v) for k, v in a.items()}


def kernel(**inputs):
    import concourse.bacc as bacc
    from concourse.bass_utils import run_bass_kernel_spmd

    laid = lay_out({k: np.asarray(v) for k, v in inputs.items()})
    nc = bacc.Bacc("TRN2", target_bir_lowering=False, num_devices=1)
    arrays, aps = {}, {}
    for name, a in laid.items():
        arrays[f"in_{name}"] = a
        aps[name] = nc.dram_tensor(f"in_{name}", a.shape, mybir.dt.from_np(a.dtype), kind="ExternalInput").ap()
    aps["out"] = nc.dram_tensor("out_0_dram", (1, SEQ, D), F32, kind="ExternalOutput").ap()
    build(nc, aps)
    r = run_bass_kernel_spmd(nc, [arrays], core_ids=[0])
    return r.results[0]["out_0_dram"]
```
